# Optimizing a Trainium2 kernel written in Bass

```python
import math
import jax, jax.numpy as jnp
from jax import lax
import numpy as np

D_MODEL = 2048
BATCH = 1
SEQ = 256
DEPTH = 1
DEC_BATCH = 8
DEC_SEQ = 8
PAST_LEN = 2048
PAGE_SIZE = 128

N_HEADS_ATTN = 8
HEAD_DIM_QK = 64
HEAD_DIM_V = 2 * HEAD_DIM_QK
ATTN_WIDTH = N_HEADS_ATTN * HEAD_DIM_V
CONV_WIDTH = D_MODEL - ATTN_WIDTH
CONV_GROUPS = 8
CONV_KERNEL = 31
D_FF = 5632
D_PLE = 256
Q_BLOCK = 128
RMS_EPS = 1e-6
LN_EPS = 1e-5
NEG_INF = -1e30
QK_COLS = N_HEADS_ATTN * 2 * HEAD_DIM_QK
IN_COLS = 2 * QK_COLS + ATTN_WIDTH + 2 * CONV_WIDTH
POOL_NUM, POOL_DEN = 5, 4

kernel_name = "hymba_diffattn_conformer_step"

def rms_norm(x, g):
    xf = x.astype(jnp.float32)
    y = xf * lax.rsqrt(jnp.mean(xf * xf, axis=-1, keepdims=True) + RMS_EPS)
    return (y * g).astype(x.dtype)

def group_layer_norm(x, g, b):
    xf = x.astype(jnp.float32).reshape(*x.shape[:-1], CONV_GROUPS, -1)
    mu = jnp.mean(xf, axis=-1, keepdims=True)
    var = jnp.mean(jnp.square(xf - mu), axis=-1, keepdims=True)
    y = ((xf - mu) * lax.rsqrt(var + LN_EPS)).reshape(x.shape)
    return (y * g + b).astype(x.dtype)

def swiglu(x, w_gate, w_up, w_down):
    return (jax.nn.silu(x @ w_gate) * (x @ w_up)) @ w_down

def alibi_slopes():
    return jnp.asarray(np.array([2.0 ** (-8.0 * (h + 1) / N_HEADS_ATTN) for h in range(N_HEADS_ATTN)], dtype=np.float32))

def alibi_bias(qpos, kpos):
    dist = (qpos[:, None] - kpos[None, :]).astype(jnp.float32)
    return jnp.where(dist[None] >= 0, -alibi_slopes()[:, None, None] * dist[None], NEG_INF)

def lambda_init(layer_idx):
    return 0.8 - 0.6 * math.exp(-0.3 * layer_idx)

def diff_weights(s, lam):
    p = jax.nn.softmax(s, axis=-1)
    return p[:, :, 0] - lam * p[:, :, 1]

def diff_attn_prompt(q, k, v, lam):
    b, s = q.shape[:2]
    nblk = s // Q_BLOCK
    scale = HEAD_DIM_QK ** -0.5
    kpos = jnp.arange(s)
    qb = q.reshape(b, nblk, Q_BLOCK, *q.shape[2:]).swapaxes(0, 1)

    def one_block(args):
        q_blk, i = args
        qpos = i * Q_BLOCK + jnp.arange(Q_BLOCK)
        sc = jnp.einsum('bqhmd,bkhmd->bhmqk', q_blk, k, preferred_element_type=jnp.float32) * scale
        w = diff_weights(sc + alibi_bias(qpos, kpos)[None, :, None], lam)
        return jnp.einsum('bhqk,bkhd->bqhd', w.astype(v.dtype), v, preferred_element_type=jnp.float32).astype(v.dtype)

    out = lax.map(one_block, (qb, jnp.arange(nblk)))
    return out.swapaxes(0, 1).reshape(b, s, N_HEADS_ATTN, HEAD_DIM_V)

def diff_attn_sample(q, k_new, v_new, k_past, v_past, lam):
    t = q.shape[1]
    p = k_past.shape[1]
    scale = HEAD_DIM_QK ** -0.5
    s_past = jnp.einsum('bqhmd,bkhmd->bhmqk', q, k_past, preferred_element_type=jnp.float32)
    s_new = jnp.einsum('bqhmd,bkhmd->bhmqk', q, k_new, preferred_element_type=jnp.float32)
    sc = jnp.concatenate([s_past, s_new], axis=-1) * scale
    qpos = p + jnp.arange(t)
    kpos = jnp.arange(p + t)
    w = diff_weights(sc + alibi_bias(qpos, kpos)[None, :, None], lam).astype(v_new.dtype)
    out = (jnp.einsum('bhqk,bkhd->bqhd', w[..., :p], v_past, preferred_element_type=jnp.float32)
           + jnp.einsum('bhqk,bkhd->bqhd', w[..., p:], v_new, preferred_element_type=jnp.float32))
    return out.astype(v_new.dtype)

def conformer_conv(c_in, conv_prev, w_dw, b_dw, g_cn, b_cn):
    a, g = jnp.split(c_in, 2, axis=-1)
    u = a * jax.nn.sigmoid(g)
    u_ext = jnp.concatenate([conv_prev.astype(u.dtype), u], axis=1)
    y = lax.conv_general_dilated(u_ext, w_dw[:, None, :].astype(u.dtype), window_strides=(1,), padding='VALID',
                                 dimension_numbers=('NWC', 'WIO', 'NWC'), feature_group_count=CONV_WIDTH) + b_dw
    y = jax.nn.silu(group_layer_norm(y, g_cn, b_cn))
    return y, u_ext[:, -(CONV_KERNEL - 1):]

def layer_forward(h, p_l, conv_prev, attend, layer_idx, W):
    b, s, _ = h.shape
    h = h + 0.5 * swiglu(rms_norm(h, W['g_ffn1']), W['w_ffn1_gate'], W['w_ffn1_up'], W['w_ffn1_down'])
    u = rms_norm(h, W['g_mix']) @ W['w_in']
    q = u[..., :QK_COLS].reshape(b, s, N_HEADS_ATTN, 2, HEAD_DIM_QK)
    k = u[..., QK_COLS:2 * QK_COLS].reshape(b, s, N_HEADS_ATTN, 2, HEAD_DIM_QK)
    v = u[..., 2 * QK_COLS:2 * QK_COLS + ATTN_WIDTH].reshape(b, s, N_HEADS_ATTN, HEAD_DIM_V)
    c_in = u[..., 2 * QK_COLS + ATTN_WIDTH:]
    lam_init = lambda_init(layer_idx)
    lam = (jnp.exp(jnp.sum(W['lambda_q1'].astype(jnp.float32) * W['lambda_k1'].astype(jnp.float32)))
           - jnp.exp(jnp.sum(W['lambda_q2'].astype(jnp.float32) * W['lambda_k2'].astype(jnp.float32))) + lam_init)
    o_attn = attend(q, k, v, lam)
    o_attn = (rms_norm(o_attn, W['g_subln']) * (1.0 - lam_init)).reshape(b, s, ATTN_WIDTH)
    o_conv, conv_new = conformer_conv(c_in, conv_prev, W['w_dw'], W['b_dw'], W['g_conv_norm'], W['b_conv_norm'])
    h = h + jnp.concatenate([o_attn, o_conv.astype(o_attn.dtype)], axis=-1) @ W['w_out']
    h = h + 0.5 * swiglu(rms_norm(h, W['g_ffn2']), W['w_ffn2_gate'], W['w_ffn2_up'], W['w_ffn2_down'])
    gate = jax.nn.sigmoid(rms_norm(h, W['g_ple']) @ W['w_ple_gate'])
    h = h + (p_l @ W['w_ple_proj']) * gate
    k_rows = k.reshape(b, s, N_HEADS_ATTN, 2 * HEAD_DIM_QK)
    return h, k_rows, v, conv_new

def setup_inputs(seed: int = 0) -> dict:
    key = jax.random.key(seed)
    ks = iter(jax.random.split(key, 40))
    f32 = jnp.float32
    n_pages = PAST_LEN // PAGE_SIZE
    n_pool = (DEC_BATCH * n_pages * POOL_NUM) // POOL_DEN

    def nrm(shape, scale=1.0):
        return jax.random.normal(next(ks), shape, f32) * scale

    def gain(shape):
        return 1.0 + nrm(shape, 0.05)

    page_table = jax.random.permutation(next(ks), n_pool)[:DEC_BATCH * n_pages].reshape(DEC_BATCH, n_pages).astype(jnp.int32)
    return {
        'x_prompt': nrm((BATCH, SEQ, D_MODEL)),
        'x_sample': nrm((DEC_BATCH, DEC_SEQ, D_MODEL)),
        'cache_k': nrm((DEPTH, n_pool, PAGE_SIZE, N_HEADS_ATTN, 2 * HEAD_DIM_QK)),
        'cache_v': nrm((DEPTH, n_pool, PAGE_SIZE, N_HEADS_ATTN, HEAD_DIM_V)),
        'state_conv': nrm((DEPTH, DEC_BATCH, CONV_KERNEL - 1, CONV_WIDTH)),
        'page_table': page_table,
        'p_prompt': nrm((DEPTH, BATCH, SEQ, D_PLE)),
        'p_sample': nrm((DEPTH, DEC_BATCH, DEC_SEQ, D_PLE)),
        'g_ffn1': gain((DEPTH, D_MODEL)),
        'w_ffn1_gate': nrm((DEPTH, D_MODEL, D_FF), D_MODEL ** -0.5),
        'w_ffn1_up': nrm((DEPTH, D_MODEL, D_FF), D_MODEL ** -0.5),
        'w_ffn1_down': nrm((DEPTH, D_FF, D_MODEL), D_FF ** -0.5),
        'g_mix': gain((DEPTH, D_MODEL)),
        'w_in': nrm((DEPTH, D_MODEL, IN_COLS), D_MODEL ** -0.5),
        'lambda_q1': nrm((DEPTH, HEAD_DIM_QK), 0.1),
        'lambda_k1': nrm((DEPTH, HEAD_DIM_QK), 0.1),
        'lambda_q2': nrm((DEPTH, HEAD_DIM_QK), 0.1),
        'lambda_k2': nrm((DEPTH, HEAD_DIM_QK), 0.1),
        'g_subln': gain((DEPTH, HEAD_DIM_V)),
        'w_dw': nrm((DEPTH, CONV_KERNEL, CONV_WIDTH), CONV_KERNEL ** -0.5),
        'b_dw': nrm((DEPTH, CONV_WIDTH), 0.01),
        'g_conv_norm': gain((DEPTH, CONV_WIDTH)),
        'b_conv_norm': nrm((DEPTH, CONV_WIDTH), 0.01),
        'w_out': nrm((DEPTH, D_MODEL, D_MODEL), D_MODEL ** -0.5),
        'g_ffn2': gain((DEPTH, D_MODEL)),
        'w_ffn2_gate': nrm((DEPTH, D_MODEL, D_FF), D_MODEL ** -0.5),
        'w_ffn2_up': nrm((DEPTH, D_MODEL, D_FF), D_MODEL ** -0.5),
        'w_ffn2_down': nrm((DEPTH, D_FF, D_MODEL), D_FF ** -0.5),
        'g_ple': gain((DEPTH, D_MODEL)),
        'w_ple_gate': nrm((DEPTH, D_MODEL, D_MODEL), D_MODEL ** -0.5),
        'w_ple_proj': nrm((DEPTH, D_PLE, D_MODEL), D_PLE ** -0.5),
        'g_final': gain((D_MODEL,)),
    }

def reference(x_prompt, x_sample, cache_k, cache_v, state_conv, page_table, p_prompt, p_sample,
              g_ffn1, w_ffn1_gate, w_ffn1_up, w_ffn1_down, g_mix, w_in,
              lambda_q1, lambda_k1, lambda_q2, lambda_k2, g_subln,
              w_dw, b_dw, g_conv_norm, b_conv_norm, w_out,
              g_ffn2, w_ffn2_gate, w_ffn2_up, w_ffn2_down,
              g_ple, w_ple_gate, w_ple_proj, g_final):
    n_pages = page_table.shape[1]
    past = n_pages * PAGE_SIZE
    h_p = x_prompt
    h_s = x_sample
    kp_l, vp_l, cp_l, ks_l, vs_l, cs_l = [], [], [], [], [], []
    for l in range(DEPTH):
        W = dict(g_ffn1=g_ffn1[l], w_ffn1_gate=w_ffn1_gate[l], w_ffn1_up=w_ffn1_up[l], w_ffn1_down=w_ffn1_down[l],
                 g_mix=g_mix[l], w_in=w_in[l],
                 lambda_q1=lambda_q1[l], lambda_k1=lambda_k1[l], lambda_q2=lambda_q2[l], lambda_k2=lambda_k2[l],
                 g_subln=g_subln[l], w_dw=w_dw[l], b_dw=b_dw[l], g_conv_norm=g_conv_norm[l], b_conv_norm=b_conv_norm[l],
                 w_out=w_out[l], g_ffn2=g_ffn2[l], w_ffn2_gate=w_ffn2_gate[l], w_ffn2_up=w_ffn2_up[l],
                 w_ffn2_down=w_ffn2_down[l], g_ple=g_ple[l], w_ple_gate=w_ple_gate[l], w_ple_proj=w_ple_proj[l])
        zero_conv = jnp.zeros((h_p.shape[0], CONV_KERNEL - 1, CONV_WIDTH), h_p.dtype)
        h_p, kp, vp, cp = layer_forward(h_p, p_prompt[l], zero_conv, diff_attn_prompt, l, W)
        k_past = cache_k[l][page_table].reshape(page_table.shape[0], past, N_HEADS_ATTN, 2, HEAD_DIM_QK)
        v_past = cache_v[l][page_table].reshape(page_table.shape[0], past, N_HEADS_ATTN, HEAD_DIM_V)
        attend_s = lambda q, k, v, lam, kpst=k_past, vpst=v_past: diff_attn_sample(q, k, v, kpst, vpst, lam)
        h_s, ksn, vsn, csn = layer_forward(h_s, p_sample[l], state_conv[l], attend_s, l, W)
        kp_l.append(kp); vp_l.append(vp); cp_l.append(cp)
        ks_l.append(ksn); vs_l.append(vsn); cs_l.append(csn)
    y_prompt = rms_norm(h_p, g_final)
    y_sample = rms_norm(h_s, g_final)
    k_prompt = jnp.stack(kp_l)
    v_prompt = jnp.stack(vp_l)
    conv_prompt = jnp.stack(cp_l)
    k_sample = jnp.stack(ks_l)
    v_sample = jnp.stack(vs_l)
    conv_sample = jnp.stack(cs_l)
    return (y_prompt, y_sample, k_prompt, v_prompt, conv_prompt, k_sample, v_sample, conv_sample)


_drawn_inputs = setup_inputs


def setup_inputs(seed=0):
    import zlib

    import numpy as np

    out = dict(_drawn_inputs(seed))
    spreads = {}
    factors = {'lambda_q1': 8.0,
     'g_subln': 2.792,
     'b_dw': 8.0,
     'g_conv_norm': 2.822,
     'b_conv_norm': 8.0,
     'g_ffn2': 3.656,
     'g_ple': 7.245}
    for name, (base, spread) in spreads.items():
        noise = np.random.default_rng([zlib.crc32(name.encode()), seed]).standard_normal(out[name].shape)
        drawn = base * np.exp(spread * noise) if base else spread * noise
        out[name] = __import__('jax').numpy.asarray(drawn.astype(out[name].dtype))
    for name, factor in factors.items():
        out[name] = (out[name] * factor).astype(out[name].dtype)
    return out
```

```python
from contextlib import ExitStack

import numpy as np

import concourse.bass as bass
from concourse import mybir

F32 = mybir.dt.float32
F32R = mybir.dt.float32r
I32 = mybir.dt.int32
ALU = mybir.AluOpType
ACT = mybir.ActivationFunctionType
AX = mybir.AxisListType

P = 128
D = 2048
SEQ = 256
NB = 8
TS = 8
NTOK = SEQ + NB * TS
KD = D // P
DFF = 5632
FPC = 4
CHUNKS = DFF // P // FPC
HEADS = 8
QD = 64
PAGE = 128
PAST = 2048
PAGES = PAST // PAGE
NPOOL = 160
TAPS = 31
HIST = TAPS - 1
PLE_K = 2
RMS_EPS = 1e-6
LN_EPS = 1e-5
LAM_INIT = 0.2
MASKED = -1e32

SLAB = 16
RAW = 4
FFN_SLABS = 12
N_FFN = CHUNKS * FFN_SLABS
N_IN = 40
S_FFN1 = 0
S_IN = S_FFN1 + N_FFN
S_OUT = S_IN + N_IN
S_FFN2 = S_OUT + KD
S_PLE = S_FFN2 + N_FFN
N_PLE = 2 + KD
SLABS_ALL = S_PLE + N_PLE

KV_SLOTS = PAGES // 2
KCOLS = PAST + NB * TS
EV0 = 4

G_FFN1, G_MIX, G_FFN2, G_PLE, G_FINAL = (KD * i for i in range(5))
G_CN = KD * 5
B_CN = G_CN + 8
G_SUB = B_CN + 8
N_VEC = G_SUB + 1


def hymba_step(nc, x_t, slabs_ffn1, slabs_in, slabs_out, slabs_ffn2, slabs_ple, k_pool, v_pool, pages,
               state_ext, p_t, vecs, dw, lams, y_t, k_t, v_tok, conv_p, conv_s):
    ctx = ExitStack()
    with ctx:
        arena_bytes = nc.sbuf_bytes_remaining - 64
        start = nc.sbuf_base
        arena_bytes -= arena_bytes % 64
        ctx.enter_context(nc.sbuf_tensor("arena", [P, arena_bytes // 4], F32))
        start = (start + 31) // 32 * 32
        at = [start]

        def place(name, shape, dt=F32, offset=None):
            size = int(np.prod(shape[1:])) * 4
            size = (size + 31) // 32 * 32
            if offset is None:
                offset = at[0]
                at[0] += size
            assert offset + size <= start + arena_bytes, (name, offset + size - start, arena_bytes)
            return nc.alloc_sbuf_tensor_at(name, shape, dt, offset=offset)

        h = place("h", [P, KD, NTOK])
        x_at = at[0]
        x_hi = place("x_hi", [P, KD, NTOK], F32R)
        x_lo = place("x_lo", [P, KD, NTOK], F32R)
        raw = [place(f"raw{i}", [P, SLAB * P]) for i in range(RAW)]
        w_at = at[0]
        w_hi = [place(f"w_hi{i}", [P, SLAB, P], F32R) for i in range(2)]
        w_lo = [place(f"w_lo{i}", [P, SLAB, P], F32R) for i in range(2)]
        mid_at = at[0]
        mid_hi = place("mid_hi", [P, FPC, NTOK], F32R)
        mid_lo = place("mid_lo", [P, FPC, NTOK], F32R)
        qk_at = at[0]
        qT = place("qT", [P, HEADS, NTOK])
        kT = place("kT", [P, HEADS, NTOK])
        v_at = at[0]
        vtok = place("vtok", [P, 3, HEADS * P])
        u_p = place("u_p", [P, 8, HIST + SEQ])
        u_s = place("u_s", [P, 8, NB, HIST + TS])
        oT = place("oT", [P, HEADS, NTOK])
        sig = [place(f"sig{i}", [P, NTOK]) for i in range(2)]
        tmp = [place(f"tmp{i}", [P, NTOK]) for i in range(2)]
        gated = place("gated", [P, NTOK])
        ssq = place("ssq", [P, NTOK])
        rms = ssq
        rinv = place("rinv", [P, NTOK])
        ident = place("ident", [P, P])
        ones = place("ones", [P, P])
        vec = place("vec", [P, N_VEC])
        wdw = place("wdw", [P, 8, TAPS + 1])
        eps = place("eps", [P, 2])
        slope_s = place("slope_s", [P, 2])
        slope_p = place("slope_p", [P, HEADS])
        lam_row = place("lam_row", [1, 4, QD], offset=mid_at)
        lam_s = place("lam_s", [1, 8])
        neglam = place("neglam", [P, 1])
        g_sub8 = place("g_sub8", [P, 1])
        page_row = place("page_row", [1, NB * PAGES], I32)
        l_sum = place("l_sum", [P, 2 * NB])
        l_inv = place("l_inv", [P, 2 * NB])
        neg_max = place("neg_max", [P, 2])
        head_max = place("head_max", [P, 2, 2])
        head_sum = place("head_sum", [P, 2, 2])
        head_inv = place("head_inv", [P, 2, 2])
        head_c1 = place("head_c1", [P, 2])
        conv_y = place("conv_y", [P, 8, NTOK], offset=mid_at)
        v_tmp = [place(f"v_tmp{i}", [P, NTOK], offset=mid_at + 4 * NTOK * i) for i in range(4)]
        S = place("S", [P, 2, KCOLS], offset=x_at)
        ET = place("ET", [P, 2, PAGES + 1, P], offset=x_at + 2 * KCOLS * 4)
        w_cur = [w_at]

        def in_w(name, shape, dt=F32):
            t = place(name, shape, dt, offset=w_cur[0])
            w_cur[0] += (int(np.prod(shape[1:])) * 4 + 31) // 32 * 32
            assert w_cur[0] <= mid_at
            return t

        kpos = in_w("kpos", [P, PAST])
        kpos_p = in_w("kpos_p", [P, 3 * P])
        kpos_n = in_w("kpos_n", [P, 120])
        n_mask = in_w("n_mask", [P, 120])
        n_keep = in_w("n_keep", [P, 120])
        trow_i = in_w("trow_i", [P, 1], I32)
        trow = in_w("trow", [P, 1])
        comb = in_w("comb", [P, 4, TS])
        comb1 = in_w("comb1", [P, 4, TS])
        Qb = in_w("Qb", [P, HEADS, 32])
        q_st = in_w("q_st", [P, SEQ])
        k_st = in_w("k_st", [P, SEQ])
        v_st = in_w("v_st", [P, 2, P])
        S_p = in_w("S_p", [P, 2, 3 * P])
        w_p = in_w("w_p", [P, 3 * P])
        wT_p = in_w("wT_p", [P, 3 * P])
        O_n = in_w("O_n", [P, 2, P])
        y_c = in_w("y_c", [P, NTOK])
        u_st = in_w("u_st", [P, NB, HIST + TS])
        wdw_st = in_w("wdw_st", [P, TAPS + 1])
        tap_s = [in_w(f"tap_s{i}", [P, NB, TS]) for i in range(2)]
        sub_sq = [place(f"sub_sq{i}", [P, NTOK], offset=w_at + 4 * NTOK * i) for i in range(HEADS)]
        proj = place("proj", [P, KD, NTOK], offset=qk_at)
        p_raw = place("p_raw", [P, PLE_K, NTOK], offset=v_at)
        p_hi = place("p_hi", [P, PLE_K, NTOK], F32R, offset=v_at + 4 * PLE_K * NTOK)
        p_lo = place("p_lo", [P, PLE_K, NTOK], F32R, offset=v_at + 8 * PLE_K * NTOK)

        bank = [ctx.enter_context(nc.psum_tensor(f"bank{i}", [P, 512], F32)) for i in range(8)]
        NORM = bank[7]
        K_BANK, T_BANK, O_BANK = bank[0:2], bank[2:4], bank[4:6]
        G_BANK, H_BANK = bank[6], bank[7]

        def sem(name):
            return ctx.enter_context(nc.semaphore(name))

        x_in = sem("x_in")
        small_in = sem("small_in")
        p_in = sem("p_in")
        raw_in = [sem(f"raw_in{i}") for i in range(RAW)]
        kv_in = [sem(f"kv_in{i}") for i in range(RAW)]
        stored = sem("stored")
        y_stored = sem("y_stored")
        w_hi_done = sem("w_hi_done")
        w_lo_done = sem("w_lo_done")
        slab_done = sem("slab_done")
        evacuated = sem("evacuated")
        sig_done = sem("sig_done")
        gated_done = sem("gated_done")
        mid_hi_done = sem("mid_hi_done")
        mid_done = sem("mid_done")
        h_done = sem("h_done")
        sq_done = sem("sq_done")
        ssq_done = sem("ssq_done")
        norm_mm = sem("norm_mm")
        rms_done = sem("rms_done")
        r_done = sem("r_done")
        xt_done = sem("xt_done")
        x_hi_done = sem("x_hi_done")
        x_done = sem("x_done")
        consts = sem("consts")
        attc = sem("attc")
        cchain = sem("cchain")
        lam_exp = sem("lam_exp")
        lam_mm = sem("lam_mm")
        v_turned = sem("v_turned")
        vtok_done = sem("vtok_done")
        v_used = sem("v_used")
        qb_ready = sem("qb_ready")
        scored = sem("scored")
        s_read = sem("s_read")
        maxed = sem("maxed")
        exped = sem("exped")
        l_done = sem("l_done")
        turned = sem("turned")
        et_done = sem("et_done")
        pv_done = sem("pv_done")
        o_read = sem("o_read")
        comb_mm = sem("comb_mm")
        o_done = sem("o_done")
        staged = sem("staged")
        h_scored = sem("h_scored")
        hs_done = sem("hs_done")
        h_maxed = sem("h_maxed")
        h_exped = sem("h_exped")
        h_chain = sem("h_chain")
        h_w = sem("h_w")
        h_turned = sem("h_turned")
        h_wT = sem("h_wT")
        h_pv = sem("h_pv")
        h_o = sem("h_o")
        tapped = sem("tapped")
        s_mult = sem("s_mult")
        s_tapped = sem("s_tapped")
        ln_mm = sem("ln_mm")
        ln_d = sem("ln_d")
        ln_sq = sem("ln_sq")
        ln_rms = sem("ln_rms")
        ln_chain = sem("ln_chain")
        ln_sig = sem("ln_sig")
        ln_done = sem("ln_done")
        sub_sqd = sem("sub_sqd")
        sub_mm = sem("sub_mm")
        sub_rms = sem("sub_rms")
        sub_r = sem("sub_r")
        p_hi_done = sem("p_hi_done")
        p_done = sem("p_done")
        y_done = sem("y_done")

        N_SMALL = 5

        def E(s):
            return s + 1 + EV0

        X_FFN1, X_IN, X_OUT, X_FFN2, X_PLE = (KD * i for i in range(5))
        XT = {X_FFN1: 0, X_IN: KD, X_FFN2: 2 * KD + HEADS, X_PLE: 3 * KD + HEADS}

        block = ctx.enter_context(nc.Block())

        @block.sync
        def _(sp):
            def slab(src, idx, s, slot, wait):
                if wait == "split":
                    sp.wait_ge(w_lo_done, s - RAW + 1)
                sp.dma_start(raw[slot][:, :], src[idx, :, :]).then_inc(raw_in[slot], 16)

            for t in range(2):
                sp.dma_start(h[:, 8 * t:8 * t + 8, :], x_t[:, 8 * t:8 * t + 8, :]).then_inc(x_in, 16)
            for j in range(RAW):
                slab(slabs_ffn1, j, j, j, None)
            with sp.Fori(1, N_FFN // RAW) as i:
                for j in range(RAW):
                    slab(slabs_ffn1, 4 * i + j, S_FFN1 + 4 * i + j, j, "split")
            with sp.Fori(0, N_IN // RAW) as i:
                for j in range(RAW):
                    slab(slabs_in, 4 * i + j, S_IN + 4 * i + j, j, "split")

            sp.wait_ge(small_in, 16 * N_SMALL)

            def two_pages(pool, b, g, slot):
                for e in range(2):
                    page = sp.value_load(page_row[0:1, bass.ds(PAGES * b + 2 * g + e, 1)],
                                         min_val=0, max_val=NPOOL - 1)
                    sp.dma_start(raw[slot][:, 1024 * e:1024 * e + 1024],
                                 pool[bass.ds(page, 1), :, :].rearrange("o p n -> (o p) n")
                                 ).then_inc(kv_in[slot], 16)

            def keys_used(b, g):
                sp.wait_ge(scored, 10 * b + 2 * (g // 2) + 2)

            def values_used(b, g):
                sp.wait_ge(v_used, KV_SLOTS * b + g + 1)

            def load_keys(b, before):
                for g in range(KV_SLOTS):
                    if g < RAW:
                        before(g + RAW)
                    else:
                        keys_used(b, g - RAW)
                    two_pages(k_pool, b, g, g % RAW)

            def load_values(b, before):
                for g in range(KV_SLOTS):
                    if g < RAW:
                        before(g + RAW)
                    else:
                        values_used(b, g - RAW)
                    two_pages(v_pool, b, g, g % RAW)

            load_keys(0, lambda g: sp.wait_ge(w_lo_done, S_OUT - KV_SLOTS + 1 + g))
            load_keys(1, lambda g: keys_used(0, g))
            load_values(0, lambda g: keys_used(1, g))
            with sp.Fori(2, NB) as b:
                load_keys(b, lambda g: values_used(b - 2, g))
                load_values(b - 1, lambda g: keys_used(b, g))
            load_values(NB - 1, lambda g: values_used(NB - 2, g))

            for j in range(RAW):
                values_used(NB - 1, j + RAW)
                slab(slabs_out, j, S_OUT + j, j, None)
            with sp.Fori(1, KD // RAW) as i:
                for j in range(RAW):
                    slab(slabs_out, 4 * i + j, S_OUT + 4 * i + j, j, "split")
            with sp.Fori(0, N_FFN // RAW) as i:
                for j in range(RAW):
                    slab(slabs_ffn2, 4 * i + j, S_FFN2 + 4 * i + j, j, "split")
            with sp.Fori(0, N_PLE // RAW) as i:
                for j in range(RAW):
                    slab(slabs_ple, 4 * i + j, S_PLE + 4 * i + j, j, "split")
            for j in range(N_PLE % RAW):
                s = N_PLE // RAW * RAW + j
                slab(slabs_ple, s, S_PLE + s, j, "split")
            for c in range(4):
                sp.wait_ge(y_done, 4 * c + 4)
                sp.dma_start(y_t[:, 4 * c:4 * c + 4, :], proj[:, 4 * c:4 * c + 4, :]).then_inc(y_stored, 16)
            sp.wait_ge(stored, 16 * 5)
            sp.wait_ge(y_stored, 16 * 4)

        @block.gpsimd
        def _(pool):
            for dst, src in ((vec[:, :], vecs), (wdw[:, :, :], dw), (u_s[:, :, :, :], state_ext),
                             (page_row[:, :], pages), (lam_row[0:1, :, :], lams)):
                pool.dma_start(dst, src).then_inc(small_in, 16)
            nc.gpsimd.memset(ones[:, :], 1.0)
            nc.gpsimd.memset(ident[:, :], 0.0)
            nc.gpsimd.memset(eps[:, 0:1], RMS_EPS)
            nc.gpsimd.memset(eps[:, 1:2], LN_EPS)
            nc.gpsimd.memset(u_p[:, :, 0:HIST], 0.0)
            for hd in range(HEADS):
                last = nc.gpsimd.memset(slope_p[:, hd:hd + 1], 2.0 ** -(hd + 1))
            last.then_inc(consts, 1)
            pool.wait_ge(consts, 1)
            nc.gpsimd.affine_select(out=ident[:, :], in_=ident[:, :], compare_op=ALU.not_equal, fill=1.0,
                                    base=0, pattern=[[-1, P]], channel_multiplier=1).then_inc(consts, 1)

            def queries(b):
                if not isinstance(b, int):
                    pool.wait_ge(scored, 10 * b)
                col = SEQ + TS * b
                nc.gpsimd.tensor_copy(Qb[0:QD, :, 0:TS], qT[0:QD, :, bass.ds(col, TS)]).then_inc(qb_ready, 1)
                pool.wait_ge(qb_ready, 2 * b + 1)
                nc.gpsimd.tensor_copy(Qb[QD:P, :, TS:2 * TS], qT[QD:P, :, bass.ds(col, TS)]).then_inc(qb_ready, 1)
                pool.wait_ge(qb_ready, 2 * b + 2)

            pool.wait_ge(slab_done, S_OUT)
            nc.gpsimd.memset(Qb[:, :, :], 0.0).then_inc(attc, 1)
            pool.wait_ge(attc, 1)
            queries(0)
            nc.gpsimd.iota(kpos[:, :], [[1, PAST]], base=-PAST, channel_multiplier=0,
                           allow_small_or_imprecise_dtypes=True).then_inc(attc, 1)
            nc.gpsimd.memset(comb[:, :, :], 0.0)
            nc.gpsimd.memset(comb1[:, :, :], 0.0)
            nc.gpsimd.iota(kpos_p[:, 0:P], [[1, P]], base=0, channel_multiplier=-1,
                           allow_small_or_imprecise_dtypes=True)
            nc.gpsimd.iota(kpos_p[:, P:3 * P], [[1, 2 * P]], base=-P, channel_multiplier=-1,
                           allow_small_or_imprecise_dtypes=True)
            nc.gpsimd.iota(kpos_n[:, :], [[1, 120]], base=-56, channel_multiplier=0,
                           allow_small_or_imprecise_dtypes=True)
            nc.gpsimd.iota(trow_i[:, :], [[0, 1]], base=0, channel_multiplier=1).then_inc(attc, 1)
            pool.wait_ge(attc, 3)
            nc.gpsimd.affine_select(out=kpos_p[:, 0:P], in_=kpos_p[:, 0:P], compare_op=ALU.is_ge,
                                    fill=MASKED, base=0, pattern=[[-1, P]], channel_multiplier=1)
            nc.gpsimd.affine_select(out=kpos_p[:, P:3 * P], in_=kpos_p[:, P:3 * P], compare_op=ALU.is_ge,
                                    fill=MASKED, base=P, pattern=[[-1, 2 * P]], channel_multiplier=1)
            nc.gpsimd.affine_select(out=kpos_n[:, :], in_=kpos_n[:, :], compare_op=ALU.is_ge,
                                    fill=1000.0, base=-56, pattern=[[1, 120]], channel_multiplier=0)
            nc.gpsimd.affine_select(out=comb[:, :, :], in_=comb[:, :, :], compare_op=ALU.not_equal,
                                    fill=1.0, base=0, pattern=[[-32, 4], [-1, TS]], channel_multiplier=1)
            nc.gpsimd.affine_select(out=comb1[:, :, :], in_=comb1[:, :, :], compare_op=ALU.not_equal,
                                    fill=1.0, base=-TS, pattern=[[-32, 4], [-1, TS]],
                                    channel_multiplier=1).then_inc(attc, 1)
            pool.wait_ge(evacuated, E(S_OUT - 1))
            pool.wait_ge(vtok_done, HEADS)
            pool.dma_start(k_t, kT[:, :, :]).then_inc(stored, 16)
            pool.dma_start(v_tok[0:SEQ, :].rearrange("(a p) n -> p a n", p=P), vtok[:, 0:2, :]).then_inc(stored, 16)
            pool.dma_start(v_tok[SEQ:NTOK, :], vtok[P - NB * TS:P, 2, :]).then_inc(stored, 16)
            pool.dma_start(conv_p, u_p[:, :, SEQ:SEQ + HIST]).then_inc(stored, 16)
            pool.dma_start(conv_s, u_s[:, :, :, :]).then_inc(stored, 16)

            def iteration(b):
                first = isinstance(b, int)
                if not first:
                    queries(b)
                if not first:
                    pool.wait_ge(h_pv, b)
                nc.gpsimd.tensor_copy(q_st[:, :], qT[:, bass.ds(b, 1), 0:SEQ].rearrange("p o n -> p (o n)"))
                nc.gpsimd.tensor_copy(k_st[:, :], kT[:, bass.ds(b, 1), 0:SEQ].rearrange("p o n -> p (o n)"))
                nc.gpsimd.tensor_copy(v_st[:, :, :], vtok[:, 0:2, bass.ds(P * b, P)]).then_inc(staged, 1)
                if not first:
                    pool.wait_ge(ln_d, b)
                    pool.wait_ge(s_tapped, TAPS * b)
                nc.gpsimd.tensor_copy(u_st[:, :, :], u_s[:, bass.ds(b, 1), :, :].rearrange("p o s t -> p (o s) t"))
                nc.gpsimd.tensor_copy(wdw_st[:, :], wdw[:, bass.ds(b, 1), :].rearrange("p o n -> p (o n)")
                                      ).then_inc(s_mult, 1)
                ys = y_c[:, SEQ:NTOK].rearrange("p (s t) -> p s t", t=TS)

                def spread(c):
                    return wdw_st[:, c:c + 1].unsqueeze(2).to_broadcast([P, NB, TS])
                pool.wait_ge(s_mult, (TAPS + 1) * b + 1)
                nc.gpsimd.tensor_tensor(tap_s[0][:, :, :], u_st[:, :, 0:TS], spread(0), ALU.mult).then_inc(s_mult, 1)
                pool.wait_ge(s_mult, (TAPS + 1) * b + 2)
                nc.gpsimd.tensor_tensor(ys, tap_s[0][:, :, :], spread(TAPS), ALU.add).then_inc(s_tapped, 1)
                for k in range(1, TAPS):
                    nc.gpsimd.tensor_scalar(tap_s[k % 2][:, :, :], u_st[:, :, k:k + TS], wdw_st[:, k:k + 1], None,
                                            ALU.mult).then_inc(s_mult, 1)
                    pool.wait_ge(s_mult, (TAPS + 1) * b + 2 + k)
                    pool.wait_ge(s_tapped, TAPS * b + k)
                    nc.gpsimd.tensor_tensor(ys, ys, tap_s[k % 2][:, :, :], ALU.add).then_inc(s_tapped, 1)

            iteration(0)
            with pool.Fori(1, NB) as b:
                iteration(b)
            pool.wait_ge(pv_done, NB)
            pool.wait_ge(h_pv, HEADS)
            pool.wait_ge(staged, HEADS)
            pool.wait_ge(stored, 16 * 5)
            pool.dma_start(p_raw[:, :, :], p_t).then_inc(p_in, 16)

        @block.scalar
        def _(act):
            def split_hi(s, slot2, slot4, before=True):
                act.wait_ge(raw_in[slot4], 16 * (s // RAW) + 16)
                if before:
                    act.wait_ge(slab_done, s - 1)
                nc.scalar.copy(w_hi[slot2][:, :, :], raw[slot4][:, :].rearrange("p (k n) -> p k n", n=P)
                               ).then_inc(w_hi_done, 1)

            def split_next(base, i4, j):
                n = j + 1
                act.wait_ge(raw_in[n % 4], 16 * (base // 4 + i4 + n // 4 + 1))
                act.wait_ge(slab_done, base + 4 * i4 + j)
                nc.scalar.copy(w_hi[n % 2][:, :, :], raw[n % 4][:, :].rearrange("p (k n) -> p k n", n=P)
                               ).then_inc(w_hi_done, 1)

            def square(norm, n, buf):
                act.wait_ge(h_done, KD * norm + n + 1)
                act.wait_ge(ssq_done, KD * norm + n - 1)
                nc.scalar.activation(tmp[buf][:, :], h[:, bass.ds(n, 1), :].rearrange("p o n -> p (o n)"),
                                     ACT.Square).then_inc(sq_done, 1)

            def root(norm):
                act.wait_ge(norm_mm, norm + 1)
                nc.scalar.activation(rms[:, :], NORM[:, 0:NTOK], ACT.Sqrt, bias=eps[:, 0:1],
                                     scale=1.0 / D).then_inc(rms_done, 1)

            def upper_x(norm_x):
                xt = XT[norm_x]
                with act.Fori(0, KD // 2) as kk:
                    for u in range(2):
                        act.wait_ge(xt_done, xt + 2 * kk + u + 1)
                        nc.scalar.copy(x_hi[:, bass.ds(2 * kk + u, 1), :].rearrange("p o n -> p (o n)"),
                                       tmp[u][:, :]).then_inc(x_hi_done, 1)

            def ffn_chunk(base, i, f_base, norm=None):
                s0 = base + FFN_SLABS * i
                for j in range(FFN_SLABS):
                    split_next(base, 3 * i, j)
                    if j < 8 and j % 2 == 0:
                        f = j // 2
                        act.wait_ge(slab_done, s0 + j + 1)
                        act.wait_ge(evacuated, E(s0 + j - 3))
                        nc.scalar.activation(sig[f % 2][:, :], bank[j][:, 0:NTOK], ACT.Sigmoid
                                             ).then_inc(sig_done, 1)
                    if j >= 8 and norm is not None:
                        for q in range(4):
                            square(norm, 4 * (j - 8) + q, q % 2)

            def ffn(base, f_base, norm):
                with act.Fori(0, CHUNKS - 1) as i:
                    ffn_chunk(base, i, f_base)
                ffn_chunk(base, CHUNKS - 1, f_base, norm)

            act.wait_ge(consts, 2)
            act.wait_ge(x_in, 32)
            for n in range(KD):
                if n >= 2:
                    act.wait_ge(ssq_done, n - 1)
                nc.scalar.activation(tmp[n % 2][:, :], h[:, n, :], ACT.Square).then_inc(sq_done, 1)
            split_hi(0, 0, 0, False)
            root(0)
            upper_x(X_FFN1)
            act.wait_ge(cchain, 2)
            nc.scalar.activation(lam_s[0:1, 2:4], lam_s[0:1, 0:2], ACT.Exp).then_inc(lam_exp, 1)
            ffn(S_FFN1, 0, 1)
            root(1)
            upper_x(X_IN)

            with act.Fori(0, 4) as i:
                for j in range(4):
                    split_next(S_IN, i, j)
            with act.Fori(0, 2) as i:
                for j in range(4):
                    split_next(S_IN + 16, i, j)
                for j in range(4):
                    act.wait_ge(v_turned, 4 * i + j + 1)
                    nc.scalar.copy(vtok[:, :, bass.ds(P * (4 * i + j), P)],
                                   bank[4 + j][:, 0:3 * P].rearrange("p (a n) -> p a n", n=P)).then_inc(vtok_done, 1)

            def conv_in(i, last):
                s0 = S_IN + 24 + 4 * i
                for j in range(4):
                    if not (last and j == 3):
                        split_next(S_IN + 24, i, j)
                    if j % 2:
                        act.wait_ge(slab_done, s0 + j + 1)
                        act.wait_ge(evacuated, E(s0 + j - 4))
                        nc.scalar.activation(sig[j // 2][:, :], bank[j][:, 0:NTOK], ACT.Sigmoid
                                             ).then_inc(sig_done, 1)
            with act.Fori(0, 3) as i:
                conv_in(i, False)
            conv_in(3, True)

            def exp_scores(b):
                for half in range(2):
                    act.wait_ge(maxed, 2 * b + half + 1)
                    nc.scalar.activation(S[:, half, :], S[:, half, :], ACT.Exp, bias=neg_max[:, half:half + 1],
                                         accum_out=l_sum[:, bass.ds(2 * b + half, 1)]).then_inc(exped, 1)

            def prompt_head(b):
                act.wait_ge(h_maxed, 2 * b + 2)
                for m in range(2):
                    nc.scalar.activation(S_p[:, m, 0:P], S_p[:, m, 0:P], ACT.Exp,
                                         bias=head_max[:, 0, m:m + 1], accum_out=head_sum[:, 0, m:m + 1])
                for m in range(2):
                    e = nc.scalar.activation(S_p[:, m, P:3 * P], S_p[:, m, P:3 * P], ACT.Exp,
                                             bias=head_max[:, 1, m:m + 1], accum_out=head_sum[:, 1, m:m + 1])
                e.then_inc(h_exped, 1)

            def prompt_copy(b):
                act.wait_ge(h_turned, b + 1)
                nc.scalar.copy(wT_p[:, :], G_BANK[:, 0:3 * P]).then_inc(h_wT, 1)

            def out_read(b):
                act.wait_ge(pv_done, b + 1)
                act.wait_ge(l_done, b + 1)
                for half in range(2):
                    nc.scalar.activation(O_n[:, half, :], O_BANK[half][:, 0:P], ACT.Copy,
                                         scale=l_inv[:, bass.ds(2 * b + half, 1)]).then_inc(o_read, 1)

            def copy_ET(b):
                for idx in range(10):
                    half, g = idx % 2, idx // 2
                    act.wait_ge(turned, 10 * b + idx + 1)
                    if g < 4:
                        e = nc.scalar.copy(ET[:, half, 4 * g:4 * g + 4, :],
                                           T_BANK[idx % 2][:, :].rearrange("p (a n) -> p a n", n=P))
                    else:
                        e = nc.scalar.copy(ET[P - NB * TS:P, half, PAGES, :], T_BANK[idx % 2][P - NB * TS:P, 0:P])
                    e.then_inc(et_done, 1)
                    if idx == 5 and not isinstance(b, int):
                        out_read(b - 1)

            def conv_norm(b):
                act.wait_ge(ln_d, b + 1)
                nc.scalar.activation(tmp[0][:, :], gated[:, :], ACT.Square).then_inc(ln_sq, 1)
                act.wait_ge(ln_mm, 2 * b + 2)
                nc.scalar.activation(rms[:, :], H_BANK[:, 0:NTOK], ACT.Sqrt, bias=eps[:, 1:2],
                                     scale=1.0 / P).then_inc(ln_rms, 1)
                act.wait_ge(ln_chain, 3 * b + 3)
                nc.scalar.activation(sig[0][:, :], tmp[1][:, :], ACT.Sigmoid).then_inc(ln_sig, 1)

            def attention(b):
                if not isinstance(b, int):
                    conv_norm(b - 1)
                prompt_head(b)
                exp_scores(b)
                prompt_copy(b)
                copy_ET(b)

            attention(0)
            with act.Fori(1, NB) as b:
                attention(b)
            conv_norm(NB - 1)
            out_read(NB - 1)

            act.wait_ge(pv_done, NB)
            with act.Fori(0, 4) as i:
                for u in range(2):
                    k = HEADS + 2 * i + u
                    act.wait_ge(ln_done, NB)
                    nc.scalar.copy(x_hi[:, bass.ds(k, 1), :].rearrange("p o n -> p (o n)"),
                                   conv_y[:, bass.ds(2 * i + u, 1), :].rearrange("p o n -> p (o n)")
                                   ).then_inc(x_hi_done, 1)
            act.wait_ge(o_done, NB)
            for hd in range(HEADS):
                nc.scalar.activation(sub_sq[hd][:, :], oT[:, hd, :], ACT.Square).then_inc(sub_sqd, 1)

            def head_upper(hd):
                act.wait_ge(xt_done, 2 * KD + hd + 1)
                nc.scalar.copy(x_hi[:, hd, :], tmp[hd % 2][:, :]).then_inc(x_hi_done, 1)
            for hd in range(HEADS):
                act.wait_ge(sub_mm, hd + 1)
                if hd >= 2:
                    act.wait_ge(sub_r, hd - 1)
                nc.scalar.activation(sig[hd % 2][:, :], bank[hd][:, 0:NTOK], ACT.Sqrt, bias=eps[:, 0:1],
                                     scale=1.0 / P).then_inc(sub_rms, 1)
                if hd:
                    head_upper(hd - 1)
            head_upper(HEADS - 1)
            act.wait_ge(sub_mm, HEADS)
            act.wait_ge(raw_in[0], 16 * (S_OUT // 4) + 16)
            nc.scalar.copy(w_hi[0][:, :, :], raw[0][:, :].rearrange("p (k n) -> p k n", n=P)).then_inc(w_hi_done, 1)
            with act.Fori(0, 4) as i:
                for j in range(4):
                    split_next(S_OUT, i, j)
                    if j >= 1:
                        square(2, 4 * i + j - 1, (j - 1) % 2)
                square(2, 4 * i + 3, 1)
            root(2)
            upper_x(X_FFN2)
            ffn(S_FFN2, 44, 3)
            act.wait_ge(p_in, 16)
            nc.scalar.copy(p_hi[:, :, :], p_raw[:, :, :]).then_inc(p_hi_done, 1)
            root(3)
            split_next(S_PLE, 0, 0)
            upper_x(X_PLE)
            split_next(S_PLE, 0, 1)

            def gates(i, last):
                s0 = S_PLE + 2 + 4 * i
                for j in range(4):
                    n = j + 3
                    if not (last and j == 3):
                        act.wait_ge(raw_in[n % 4], 16 * (S_PLE // 4 + i + n // 4 + 1))
                        act.wait_ge(slab_done, s0 + j)
                        nc.scalar.copy(w_hi[n % 2][:, :, :], raw[n % 4][:, :].rearrange("p (k n) -> p k n", n=P)
                                       ).then_inc(w_hi_done, 1)
                    act.wait_ge(slab_done, s0 + j + 1)
                    act.wait_ge(evacuated, E(s0 + j - 2))
                    nc.scalar.activation(sig[j % 2][:, :], bank[j][:, 0:NTOK], ACT.Sigmoid).then_inc(sig_done, 1)
                    square(4, 4 * i + j, j % 2)
            with act.Fori(0, 3) as i:
                gates(i, False)
            gates(3, True)
            root(4)

        @block.vector
        def _(dve):
            vt = nc.vector

            def split_next(base, i4, j):
                n = j + 1
                dve.wait_ge(w_hi_done, base + 4 * i4 + j + 2)
                split(n)

            def split(n):
                vt.tensor_tensor(w_lo[n % 2][:, :, :], raw[n % 4][:, :].rearrange("p (k n) -> p k n", n=P),
                                 w_hi[n % 2][:, :, :].bitcast(F32), ALU.subtract).then_inc(w_lo_done, 1)

            def tile_of(t, n):
                return t[:, bass.ds(n, 1), :].rearrange("p o n -> p (o n)")

            def sum_square(norm, n, buf):
                dve.wait_ge(sq_done, KD * norm + n + 1)
                if isinstance(n, int) and n == 0:
                    vt.tensor_copy(ssq[:, :], tmp[buf][:, :]).then_inc(ssq_done, 1)
                else:
                    dve.wait_ge(ssq_done, KD * norm + n)
                    vt.tensor_tensor(ssq[:, :], ssq[:, :], tmp[buf][:, :], ALU.add).then_inc(ssq_done, 1)

            def normalize(norm, gains, norm_x):
                dve.wait_ge(rms_done, norm + 1)
                r = vt.reciprocal(rinv[:, :], rms[:, :])
                r.then_inc(r_done, 1)
                dve.wait_ge(r_done, norm + 1)
                xt = XT[norm_x]
                with dve.Fori(0, KD // 2) as kk:
                    dve.wait_ge(x_done, norm_x + 2 * kk)
                    for u in range(2):
                        k = 2 * kk + u
                        vt.scalar_tensor_tensor(out=tmp[u][:, :], in0=tile_of(h, k),
                                                scalar=vec[:, bass.ds(gains + k, 1)], in1=rinv[:, :],
                                                op0=ALU.mult, op1=ALU.mult).then_inc(xt_done, 1)
                    for u in range(2):
                        k = 2 * kk + u
                        dve.wait_ge(x_hi_done, norm_x + k + 1)
                        vt.tensor_tensor(tile_of(x_lo, k), tmp[u][:, :], tile_of(x_hi, k).bitcast(F32),
                                         ALU.subtract).then_inc(x_done, 1)

            def ffn_chunk(base, i, f_base, norm=None):
                s0 = base + FFN_SLABS * i
                for j in range(FFN_SLABS):
                    split_next(base, 3 * i, j)
                    if j < 8 and j % 2:
                        f = j // 2
                        n = f_base + FPC * i + f + 1
                        dve.wait_ge(sig_done, n + (8 if base else 0))
                        vt.tensor_tensor(gated[:, :], bank[j - 1][:, 0:NTOK], sig[f % 2][:, :], ALU.mult
                                         ).then_inc(gated_done, 1)
                        dve.wait_ge(slab_done, s0 + j + 1)
                        dve.wait_ge(gated_done, n)
                        vt.tensor_tensor(tmp[f % 2][:, :], bank[j][:, 0:NTOK], gated[:, :], ALU.mult
                                         ).then_inc(evacuated, 2)
                        dve.wait_ge(evacuated, E(s0 + j))
                        vt.tensor_copy(mid_hi[:, f, :], tmp[f % 2][:, :]).then_inc(mid_hi_done, 1)
                        dve.wait_ge(mid_hi_done, n)
                        vt.tensor_tensor(mid_lo[:, f, :], tmp[f % 2][:, :], mid_hi[:, f, :].bitcast(F32),
                                         ALU.subtract).then_inc(mid_done, 1)
                    if j >= 8:
                        dve.wait_ge(slab_done, s0 + j + 1)
                        for q in range(4):
                            n = 4 * (j - 8) + q
                            e = vt.scalar_tensor_tensor(out=h[:, n, :], in0=bank[n % 8][:, 0:NTOK], scalar=0.5,
                                                        in1=h[:, n, :], op0=ALU.mult, op1=ALU.add)
                            if norm is not None:
                                e.then_inc(h_done, 1)
                        if norm is None:
                            e.then_inc(evacuated, 1)
                        else:
                            for q in range(4):
                                sum_square(norm, 4 * (j - 8) + q, q % 2)
                            dve.wait_ge(ssq_done, KD * norm + 4 * (j - 8) + 4)
                            dve.sem_inc(evacuated, 1)

            def ffn(base, f_base, norm):
                with dve.Fori(0, CHUNKS - 1) as i:
                    ffn_chunk(base, i, f_base)
                ffn_chunk(base, CHUNKS - 1, f_base, norm)

            for j in range(4):
                for half in range(2):
                    vt.memset(slope_s[32 * j:32 * j + 32, half:half + 1], 2.0 ** -(4 * half + j + 1))
            for n in range(KD):
                dve.wait_ge(sq_done, n + 1)
                if n == 0:
                    vt.tensor_copy(ssq[:, :], tmp[0][:, :]).then_inc(ssq_done, 1)
                else:
                    dve.wait_ge(ssq_done, n)
                    vt.tensor_tensor(ssq[:, :], ssq[:, :], tmp[n % 2][:, :], ALU.add).then_inc(ssq_done, 1)
            dve.wait_ge(w_hi_done, 1)
            split(0)
            dve.wait_ge(small_in, 16 * N_SMALL)
            dve.sem_inc(h_done, KD)
            dve.sem_inc(evacuated, EV0)
            vt.tensor_tensor(lam_row[0:1, 0:2, :], lam_row[0:1, 0:2, :], lam_row[0:1, 2:4, :], ALU.mult
                             ).then_inc(cchain, 1)
            dve.wait_ge(cchain, 1)
            vt.tensor_reduce(lam_s[0:1, 0:2], lam_row[0:1, 0:2, :], AX.X, ALU.add).then_inc(cchain, 1)
            vt.tensor_scalar(g_sub8[:, :], vec[:, G_SUB:G_SUB + 1], 1.0 - LAM_INIT, None, ALU.mult).then_inc(cchain, 1)
            normalize(0, G_FFN1, X_FFN1)
            dve.wait_ge(lam_exp, 1)
            vt.tensor_tensor(lam_s[0:1, 4:5], lam_s[0:1, 3:4], lam_s[0:1, 2:3], ALU.subtract).then_inc(cchain, 1)
            dve.wait_ge(cchain, 4)
            vt.tensor_scalar(lam_s[0:1, 5:6], lam_s[0:1, 4:5], -LAM_INIT, None, ALU.add).then_inc(cchain, 1)
            ffn(S_FFN1, 0, 1)
            normalize(1, G_MIX, X_IN)

            with dve.Fori(0, 2) as i:
                for j in range(4):
                    split_next(S_IN, i, j)
                    dve.wait_ge(slab_done, S_IN + 4 * i + j + 1)
                    vt.tensor_scalar(tile_of(qT, 4 * i + j), bank[j][:, 0:NTOK], QD ** -0.5, None, ALU.mult
                                     ).then_inc(evacuated, 1)
            with dve.Fori(0, 2) as i:
                for j in range(4):
                    split_next(S_IN + 8, i, j)
                    dve.wait_ge(slab_done, S_IN + 8 + 4 * i + j + 1)
                    vt.tensor_copy(tile_of(kT, 4 * i + j), bank[j][:, 0:NTOK]).then_inc(evacuated, 1)
            with dve.Fori(0, 2) as i:
                for j in range(4):
                    split_next(S_IN + 16, i, j)
                    dve.wait_ge(slab_done, S_IN + 16 + 4 * i + j + 1)
                    vt.tensor_copy(v_tmp[j][:, :], bank[j][:, 0:NTOK]).then_inc(evacuated, 1)

            def conv_in(i, last):
                s0 = S_IN + 24 + 4 * i
                for j in range(4):
                    if not (last and j == 3):
                        split_next(S_IN + 24, i, j)
                    if j % 2:
                        c = 2 * i + j // 2
                        dve.wait_ge(sig_done, 44 + c + 1)
                        vt.tensor_tensor(u_p[:, bass.ds(c, 1), HIST:HIST + SEQ].rearrange("p o n -> p (o n)"),
                                         bank[j - 1][:, 0:SEQ], sig[j // 2][:, 0:SEQ], ALU.mult)
                        vt.tensor_tensor(u_s[:, bass.ds(c, 1), :, HIST:HIST + TS].rearrange("p o s t -> p (o s) t"),
                                         bank[j - 1][:, SEQ:NTOK].rearrange("p (s t) -> p s t", t=TS),
                                         sig[j // 2][:, SEQ:NTOK].rearrange("p (s t) -> p s t", t=TS), ALU.mult
                                         ).then_inc(evacuated, 2)
            with dve.Fori(0, 3) as i:
                conv_in(i, False)
            conv_in(3, True)

            def tables():
                dve.wait_ge(attc, 4)
                dve.wait_ge(lam_mm, 1)
                vt.tensor_copy(neglam[:, :], bank[7][:, 0:1]).then_inc(cchain, 1)
                vt.tensor_scalar(trow_i[:, :], trow_i[:, :], 7, None, ALU.bitwise_and).then_inc(cchain, 1)
                dve.wait_ge(cchain, 7)
                vt.tensor_copy(trow[:, :], trow_i[:, :]).then_inc(cchain, 1)
                vt.scalar_tensor_tensor(out=comb[:, :, :], in0=comb1[:, :, :], scalar=neglam[:, :], in1=comb[:, :, :],
                                        op0=ALU.mult, op1=ALU.add)
                dve.wait_ge(cchain, 8)
                vt.tensor_scalar(n_mask[:, :], kpos_n[:, :], trow[:, :], None, ALU.is_le).then_inc(cchain, 1)
                dve.wait_ge(cchain, 9)
                vt.tensor_scalar(n_keep[:, :], n_mask[:, :], -MASKED, MASKED, ALU.mult, ALU.add).then_inc(cchain, 1)
                vt.tensor_tensor(n_mask[:, :], n_mask[:, :], kpos_n[:, :], ALU.mult).then_inc(cchain, 1)
                dve.wait_ge(cchain, 11)
                vt.tensor_tensor(kpos_n[:, :], n_mask[:, :], n_keep[:, :], ALU.add).then_inc(cchain, 1)
                dve.wait_ge(cchain, 12)

            def read_scores(b, grp):
                for half in range(2):
                    idx = 2 * grp + half
                    dve.wait_ge(scored, 10 * b + idx + 1)
                    if idx == 0 and not isinstance(b, int):
                        dve.wait_ge(turned, 10 * b)
                    if grp < 4:
                        out, pos = S[:, half, 512 * grp:512 * grp + 512], kpos[:, 512 * grp:512 * grp + 512]
                        src = K_BANK[half][:, :]
                    else:
                        out, pos = S[:, half, PAST:KCOLS], kpos_n[:, bass.ds(56 - TS * b, NB * TS)]
                        src = K_BANK[half][:, 0:NB * TS]
                    vt.scalar_tensor_tensor(out=out, in0=pos, scalar=slope_s[:, half:half + 1], in1=src,
                                            op0=ALU.mult, op1=ALU.add).then_inc(s_read, 1)

            def maxima(b):
                dve.wait_ge(s_read, 10 * b + 10)
                for half in range(2):
                    vt.tensor_reduce(neg_max[:, half:half + 1], S[:, half, :], AX.X, ALU.max, negate=True
                                     ).then_inc(maxed, 1)

            def prompt_head(b):
                dve.wait_ge(h_scored, b + 1)
                slope = slope_p[:, bass.ds(b, 1)]
                for m, src in enumerate((G_BANK, H_BANK)):
                    vt.scalar_tensor_tensor(out=S_p[:, m, :], in0=kpos_p[:, :], scalar=slope, in1=src[:, 0:3 * P],
                                            op0=ALU.mult, op1=ALU.add).then_inc(hs_done, 1)
                dve.wait_ge(hs_done, 2 * b + 2)
                vt.tensor_reduce(head_max[:, 0, :], S_p[:, :, 0:P], AX.X, ALU.max, negate=True).then_inc(h_maxed, 1)
                vt.tensor_reduce(head_max[:, 1, :], S_p[:, :, P:3 * P], AX.X, ALU.max, negate=True).then_inc(h_maxed, 1)

            def prompt_weights(b):
                dve.wait_ge(h_exped, b + 1)
                vt.reciprocal(head_inv[:, :, :], head_sum[:, :, :]).then_inc(h_chain, 1)
                dve.wait_ge(h_chain, 3 * b + 1)
                vt.tensor_scalar(head_c1[:, :], head_inv[:, :, 1], neglam[:, :], None, ALU.mult).then_inc(h_chain, 1)
                dve.wait_ge(h_chain, 3 * b + 2)
                for i, cols in enumerate((slice(0, P), slice(P, 3 * P))):
                    e = vt.tensor_scalar(w_p[:, cols], S_p[:, 1, cols], head_c1[:, i:i + 1], None, ALU.mult)
                e.then_inc(h_chain, 1)
                dve.wait_ge(h_chain, 3 * b + 3)
                for i, cols in enumerate((slice(0, P), slice(P, 3 * P))):
                    e = vt.scalar_tensor_tensor(out=w_p[:, cols], in0=S_p[:, 0, cols], scalar=head_inv[:, i, 0:1],
                                                in1=w_p[:, cols], op0=ALU.mult, op1=ALU.add)
                e.then_inc(h_w, 1)

            def prompt_out(b):
                dve.wait_ge(h_pv, b + 1)
                vt.tensor_copy(oT[:, bass.ds(b, 1), 0:SEQ].rearrange("p o n -> p (o n)"), H_BANK[:, 0:SEQ]
                               ).then_inc(h_o, 1)

            def taps(b):
                y = y_c[:, 0:SEQ]
                if not isinstance(b, int):
                    dve.wait_ge(ln_done, b)

                def w(k):
                    return wdw[:, bass.ds(b, 1), k:k + 1].rearrange("p o n -> p (o n)")

                def u(k):
                    return u_p[:, bass.ds(b, 1), k:k + SEQ].rearrange("p o n -> p (o n)")
                vt.tensor_scalar(y, u(0), w(0), w(TAPS), ALU.mult, ALU.add).then_inc(tapped, 1)
                for k in range(1, TAPS):
                    dve.wait_ge(tapped, TAPS * b + k)
                    vt.scalar_tensor_tensor(out=y, in0=u(k), scalar=w(k), in1=y, op0=ALU.mult, op1=ALU.add
                                            ).then_inc(tapped, 1)

            def inverse_sums(b):
                dve.wait_ge(exped, 2 * b + 2)
                vt.reciprocal(l_inv[:, bass.ds(2 * b, 2)], l_sum[:, bass.ds(2 * b, 2)]).then_inc(l_done, 1)

            def out_store(b):
                dve.wait_ge(comb_mm, b + 1)
                vt.tensor_copy(oT[:, :, bass.ds(SEQ + TS * b, TS)],
                               O_BANK[0][:, 256:320].rearrange("p (h q) -> p h q", q=TS)).then_inc(o_done, 1)

            def conv_center(b):
                dve.wait_ge(ln_mm, 2 * b + 1)
                vt.scalar_tensor_tensor(out=gated[:, :], in0=G_BANK[:, 0:NTOK], scalar=-1.0 / P, in1=y_c[:, :],
                                        op0=ALU.mult, op1=ALU.add).then_inc(ln_d, 1)

            def conv_scale(b):
                g = vec[:, bass.ds(G_CN + b, 1)]
                beta = vec[:, bass.ds(B_CN + b, 1)]
                dve.wait_ge(ln_rms, b + 1)
                vt.reciprocal(rinv[:, :], rms[:, :]).then_inc(ln_chain, 1)
                dve.wait_ge(ln_chain, 3 * b + 1)
                vt.scalar_tensor_tensor(out=gated[:, :], in0=gated[:, :], scalar=g, in1=rinv[:, :],
                                        op0=ALU.mult, op1=ALU.mult).then_inc(ln_chain, 1)
                dve.wait_ge(ln_chain, 3 * b + 2)
                vt.tensor_scalar(tmp[1][:, :], gated[:, :], beta, None, ALU.add).then_inc(ln_chain, 1)

            def conv_swish(b):
                dve.wait_ge(ln_sig, b + 1)
                vt.tensor_tensor(tile_of(conv_y, b), tmp[1][:, :], sig[0][:, :], ALU.mult).then_inc(ln_done, 1)

            def attention(b):
                first = isinstance(b, int)
                if first:
                    dve.wait_ge(attc, 2)
                read_scores(b, 0)
                if not first:
                    conv_center(b - 1)
                read_scores(b, 1)
                if first:
                    tables()
                else:
                    conv_scale(b - 1)
                read_scores(b, 2)
                if not first:
                    conv_swish(b - 1)
                prompt_head(b)
                read_scores(b, 3)
                read_scores(b, 4)
                maxima(b)
                prompt_weights(b)
                inverse_sums(b)
                taps(b)
                prompt_out(b)
                if not first:
                    out_store(b - 1)

            attention(0)
            with dve.Fori(1, NB) as b:
                attention(b)
            conv_center(NB - 1)
            conv_scale(NB - 1)
            conv_swish(NB - 1)
            out_store(NB - 1)

            with dve.Fori(0, 4) as i:
                for u in range(2):
                    dve.wait_ge(x_hi_done, X_OUT + 2 * i + u + 1)
                    vt.tensor_tensor(tile_of(x_lo, HEADS + 2 * i + u), tile_of(conv_y, 2 * i + u),
                                     tile_of(x_hi, HEADS + 2 * i + u).bitcast(F32), ALU.subtract).then_inc(x_done, 1)

            def head_lower(hd):
                dve.wait_ge(x_hi_done, X_OUT + HEADS + hd + 1)
                vt.tensor_tensor(x_lo[:, hd, :], tmp[hd % 2][:, :], x_hi[:, hd, :].bitcast(F32), ALU.subtract
                                 ).then_inc(x_done, 1)
            dve.wait_ge(o_done, NB)
            dve.wait_ge(h_o, HEADS)
            for hd in range(HEADS):
                dve.wait_ge(sub_rms, hd + 1)
                r = (rinv, gated)[hd % 2]
                vt.reciprocal(r[:, :], sig[hd % 2][:, :]).then_inc(sub_r, 1)
                dve.wait_ge(sub_r, hd + 1)
                vt.scalar_tensor_tensor(out=tmp[hd % 2][:, :], in0=oT[:, hd, :], scalar=g_sub8[:, :], in1=r[:, :],
                                        op0=ALU.mult, op1=ALU.mult).then_inc(xt_done, 1)
                if hd:
                    head_lower(hd - 1)
            head_lower(HEADS - 1)
            dve.wait_ge(w_hi_done, S_OUT + 1)
            split(0)
            def out_tile(i, j, first):
                n = 4 * i + j
                split_next(S_OUT, i, j)
                dve.wait_ge(slab_done, S_OUT + n + 1)
                vt.scalar_tensor_tensor(out=tile_of(h, n), in0=bank[j][:, 0:NTOK], scalar=1.0, in1=tile_of(h, n),
                                        op0=ALU.mult, op1=ALU.add).then_inc(h_done, 1)
                dve.wait_ge(h_done, KD * 2 + n + 1)
                dve.sem_inc(evacuated, 1)
                if not (first and j == 0):
                    sum_square(2, n - 1, (j - 1) % 4 % 2 if j else 1)
            for j in range(4):
                out_tile(0, j, True)
            with dve.Fori(1, 4) as i:
                for j in range(4):
                    out_tile(i, j, False)
            sum_square(2, KD - 1, 1)
            normalize(2, G_FFN2, X_FFN2)
            ffn(S_FFN2, 44, 3)
            dve.wait_ge(p_hi_done, 1)
            vt.tensor_tensor(p_lo[:, :, :], p_raw[:, :, :], p_hi[:, :, :].bitcast(F32), ALU.subtract).then_inc(p_done, 1)
            split_next(S_PLE, 0, 0)
            normalize(3, G_PLE, X_PLE)
            for t in range(2):
                dve.wait_ge(slab_done, S_PLE + t + 1)
                for q in range(8):
                    e = vt.tensor_copy(proj[:, 8 * t + q, :], bank[q][:, 0:NTOK])
                e.then_inc(evacuated, 1)
            split_next(S_PLE, 0, 1)

            def gates(i, last):
                s0 = S_PLE + 2 + 4 * i
                for j in range(4):
                    n = 4 * i + j
                    if not (last and j == 3):
                        dve.wait_ge(w_hi_done, s0 + j + 2)
                        split(j + 3)
                    dve.wait_ge(sig_done, 44 + 8 + 44 + n + 1)
                    vt.tensor_tensor(gated[:, :], tile_of(proj, n), sig[j % 2][:, :], ALU.mult).then_inc(evacuated, 1)
                    dve.wait_ge(evacuated, E(s0 + j))
                    vt.tensor_tensor(tile_of(h, n), tile_of(h, n), gated[:, :], ALU.add).then_inc(h_done, 1)
                    if isinstance(i, int) and i == 0 and j == 0:
                        sum_square(4, 0, 0)
                    else:
                        dve.wait_ge(sq_done, KD * 4 + n + 1)
                        dve.wait_ge(ssq_done, KD * 4 + n)
                        vt.tensor_tensor(ssq[:, :], ssq[:, :], tmp[j % 2][:, :], ALU.add).then_inc(ssq_done, 1)
            gates(0, False)
            with dve.Fori(1, 3) as i:
                gates(i, False)
            gates(3, True)
            dve.wait_ge(rms_done, 5)
            vt.reciprocal(rinv[:, :], rms[:, :]).then_inc(r_done, 1)
            dve.wait_ge(r_done, 5)
            for k in range(KD):
                vt.scalar_tensor_tensor(out=proj[:, k, :], in0=h[:, k, :], scalar=vec[:, G_FINAL + k:G_FINAL + k + 1],
                                        in1=rinv[:, :], op0=ALU.mult, op1=ALU.mult).then_inc(y_done, 1)

        @block.tensor
        def _(pe):
            mm = nc.tensor.matmul

            def three(out, w2, t, xh, xl, start, stop):
                mm(out, w_hi[w2][:, t, :], xh, start=start, stop=False)
                mm(out, w_hi[w2][:, t, :], xl, start=False, stop=False)
                return mm(out, w_lo[w2][:, t, :], xh, start=False, stop=stop)

            def dense(s, j, b, order=range(KD), x_base=None):
                pe.wait_ge(w_lo_done, s + 1)
                for n, k in enumerate(order):
                    if x_base is not None:
                        pe.wait_ge(x_done, x_base + n + 1)
                    e = three(bank[b][:, 0:NTOK], j % 2, k, x_hi[:, k, :], x_lo[:, k, :],
                              n == 0, n == len(order) - 1)
                e.then_inc(slab_done, 1)

            def sum_features(norm):
                pe.wait_ge(ssq_done, KD * norm + KD)
                mm(NORM[:, 0:NTOK], ones[:, :], ssq[:, :], start=True, stop=True).then_inc(norm_mm, 1)

            def ffn_chunk(base, i, f_base, x_base):
                s0 = base + FFN_SLABS * i
                for j in range(8):
                    pe.wait_ge(evacuated, E(s0 - 2) if j < 4 else E(s0 - 1))
                    dense(s0 + j, j, j, x_base=x_base if j == 0 else None)
                for d in range(4):
                    pe.wait_ge(w_lo_done, s0 + 8 + d + 1)
                    pe.wait_ge(evacuated, E(s0 + (3, 7, 8, 9)[d]))
                    for f in range(FPC):
                        if d == 0:
                            pe.wait_ge(mid_done, f_base + FPC * i + f + 1)
                        for q in range(4):
                            e = three(bank[(4 * d + q) % 8][:, 0:NTOK], d % 2, 4 * f + q,
                                      mid_hi[:, f, :], mid_lo[:, f, :], f == 0, f == FPC - 1)
                    e.then_inc(slab_done, 1)

            def ffn(base, f_base, x_base):
                with pe.Fori(0, CHUNKS) as i:
                    ffn_chunk(base, i, f_base, x_base)

            pe.wait_ge(consts, 1)
            sum_features(0)
            pe.wait_ge(evacuated, EV0)
            ffn(S_FFN1, 0, X_FFN1)
            sum_features(1)

            with pe.Fori(0, 4) as i:
                for j in range(4):
                    pe.wait_ge(evacuated, E(S_IN + 4 * i + j - 4))
                    dense(S_IN + 4 * i + j, j, j, x_base=X_IN if j == 0 else None)
            pe.wait_ge(consts, 2)
            with pe.Fori(0, 2) as i:
                for j in range(4):
                    pe.wait_ge(evacuated, E(S_IN + 16 + 4 * i + j - 4))
                    dense(S_IN + 16 + 4 * i + j, j, j)
                for j in range(4):
                    pe.wait_ge(evacuated, E(S_IN + 16 + 4 * i + j))
                    pe.wait_ge(vtok_done, 4 * i)
                    for a, t0 in enumerate((0, P, NTOK - P)):
                        e = nc.tensor.transpose(bank[4 + j][:, P * a:P * a + P], v_tmp[j][:, t0:t0 + P], ident[:, :])
                    e.then_inc(v_turned, 1)
            with pe.Fori(0, 4) as i:
                for j in range(4):
                    pe.wait_ge(evacuated, E(S_IN + 24 + 4 * i + (j - 4 if j % 2 else j - 3)))
                    dense(S_IN + 24 + 4 * i + j, j, j)
            pe.wait_ge(vtok_done, HEADS)
            pe.wait_ge(cchain, 5)
            mm(bank[7][:, 0:1], ones[0:1, :], lam_s[0:1, 5:6], start=True, stop=True).then_inc(lam_mm, 1)

            def keys(slot):
                return raw[slot][:, :].rearrange("p (g h k) -> p g h k", g=2, h=HEADS)

            def score(b, grp):
                for half in range(2):
                    idx = 2 * grp + half
                    if not (isinstance(b, int) and idx < 2):
                        pe.wait_ge(s_read, 10 * b + idx - 1)
                    for e2 in range(2):
                        slot = (2 * grp + e2) % RAW
                        if half == 0:
                            pe.wait_ge(kv_in[slot], 32 * kv_round(b, 2 * grp + e2))
                        for j in range(4):
                            e = mm(K_BANK[half][32 * j:32 * j + 32, 256 * e2:256 * e2 + 256],
                                   Qb[:, 4 * half + j, :], keys(slot)[:, :, 4 * half + j, :], start=True, stop=True)
                    e.then_inc(scored, 1)

            def kv_round(b, g):
                return g // 4 + 1 if isinstance(b, int) else 4 * b - 2 + g // 4 + 1

            def score_new(b):
                for half in range(2):
                    pe.wait_ge(s_read, 10 * b + 8 + half - 1)
                    for j in range(4):
                        e = mm(K_BANK[half][32 * j:32 * j + 32, 0:NB * TS], Qb[:, 4 * half + j, :],
                               kT[:, 4 * half + j, SEQ:NTOK], start=True, stop=True)
                    e.then_inc(scored, 1)

            def prompt_scores(b):
                pe.wait_ge(staged, b + 1)
                if isinstance(b, int):
                    pe.wait_ge(cchain, 12)
                else:
                    pe.wait_ge(ln_d, b)
                    pe.wait_ge(ln_rms, b)
                for m, out in enumerate((G_BANK, H_BANK)):
                    rows = slice(QD * m, QD * m + QD)
                    for cols, keys_n, qs in ((0, P, 0), (P, 2 * P, P)):
                        e = mm(out[:, cols:cols + keys_n], q_st[rows, qs:qs + P],
                               k_st[rows, 0:keys_n], start=True, stop=True)
                e.then_inc(h_scored, 1)

            def prompt_turn(b):
                pe.wait_ge(h_w, b + 1)
                for c in range(3):
                    e = nc.tensor.transpose(G_BANK[:, P * c:P * c + P], w_p[:, P * c:P * c + P], ident[:, :])
                e.then_inc(h_turned, 1)

            def prompt_pv(b):
                pe.wait_ge(h_wT, b + 1)
                mm(H_BANK[:, 0:P], v_st[:, 0, :], wT_p[:, 0:P], start=True, stop=True)
                mm(H_BANK[:, P:2 * P], v_st[:, 0, :], wT_p[:, P:2 * P], start=True, stop=False)
                mm(H_BANK[:, P:2 * P], v_st[:, 1, :], wT_p[:, 2 * P:3 * P], start=False, stop=True).then_inc(h_pv, 1)

            def turn(b, group):
                if group == 0:
                    pe.wait_ge(exped, 2 * b + 2)
                for idx in (2 * group, 2 * group + 1):
                    half, g = idx % 2, idx // 2
                    if not (isinstance(b, int) and idx < 2):
                        pe.wait_ge(et_done, 10 * b + idx - 1)
                    if g < 4:
                        for c in range(4):
                            e = nc.tensor.transpose(T_BANK[idx % 2][:, P * c:P * c + P],
                                                    S[:, half, 512 * g + P * c:512 * g + P * c + P], ident[:, :])
                    else:
                        e = nc.tensor.transpose(T_BANK[idx % 2][:, 0:P], S[:, half, KCOLS - P:KCOLS], ident[:, :])
                    e.then_inc(turned, 1)

            def weigh(b, pair):
                if pair == 0:
                    pe.wait_ge(et_done, 10 * b + 10)
                for g in (2 * pair, 2 * pair + 1):
                    slot = g % RAW
                    pe.wait_ge(kv_in[slot], 32 * (4 * b + 4 + g // 4 + 1) if not (isinstance(b, int) and b == NB - 1)
                               else 32 * (2 * KV_SLOTS * NB // RAW - 2 + g // 4 + 1))
                    for half in range(2):
                        for e2 in range(2):
                            for j in range(4):
                                e = mm(O_BANK[half][32 * j:32 * j + 32, 0:P],
                                       ET[:, half, 2 * g + e2, 32 * j:32 * j + 32],
                                       keys(slot)[:, e2, 4 * half + j, :], start=(g == 0 and e2 == 0), stop=False)
                    e.then_inc(v_used, 1)

            def weigh_new(b):
                for half in range(2):
                    for j in range(4):
                        e = mm(O_BANK[half][32 * j:32 * j + 32, 0:P],
                               ET[P - NB * TS:P, half, PAGES, 32 * j:32 * j + 32],
                               vtok[P - NB * TS:P, 2, P * (4 * half + j):P * (4 * half + j) + P], start=False, stop=True)
                e.then_inc(pv_done, 1)

            def combine(b):
                pe.wait_ge(o_read, 2 * b + 2)
                for half in range(2):
                    e = mm(O_BANK[0][:, 256 + 32 * half:288 + 32 * half], O_n[:, half, :],
                           comb[:, :, :].rearrange("p j q -> p (j q)"), start=True, stop=True)
                e.then_inc(comb_mm, 1)

            def conv_mean(b):
                pe.wait_ge(tapped, TAPS * b + TAPS)
                pe.wait_ge(s_tapped, TAPS * b + TAPS)
                pe.wait_ge(h_wT, b + 1)
                mm(G_BANK[:, 0:NTOK], ones[:, :], y_c[:, :], start=True, stop=True).then_inc(ln_mm, 1)

            def conv_var(b):
                pe.wait_ge(ln_sq, b + 1)
                pe.wait_ge(h_o, b + 1)
                mm(H_BANK[:, 0:NTOK], ones[:, :], tmp[0][:, :], start=True, stop=True).then_inc(ln_mm, 1)

            def attention(b):
                pe.wait_ge(qb_ready, 2 * b + 2)
                first = isinstance(b, int)
                score(b, 0)
                if not first:
                    conv_mean(b - 1)
                score(b, 1)
                if not first:
                    conv_var(b - 1)
                score(b, 2)
                prompt_scores(b)
                score(b, 3)
                score_new(b)
                if not first:
                    weigh(b - 1, 0)
                    weigh(b - 1, 1)
                prompt_turn(b)
                turn(b, 0)
                turn(b, 1)
                if not first:
                    weigh(b - 1, 2)
                prompt_pv(b)
                turn(b, 2)
                if not first:
                    weigh(b - 1, 3)
                    weigh_new(b - 1)
                turn(b, 3)
                turn(b, 4)
                if not first:
                    combine(b - 1)

            attention(0)
            with pe.Fori(1, NB) as b:
                attention(b)
            conv_mean(NB - 1)
            conv_var(NB - 1)
            for pair in range(4):
                weigh(NB - 1, pair)
            weigh_new(NB - 1)
            combine(NB - 1)

            for hd in range(HEADS):
                pe.wait_ge(sub_sqd, hd + 1)
                if hd == 0:
                    pe.wait_ge(o_done, NB)
                    pe.wait_ge(ln_done, NB)
                mm(bank[hd][:, 0:NTOK], ones[:, :], sub_sq[hd][:, :], start=True, stop=True).then_inc(sub_mm, 1)

            pe.wait_ge(sub_rms, HEADS)
            order = list(range(HEADS, KD)) + list(range(HEADS))
            with pe.Fori(0, 4) as i:
                for j in range(4):
                    pe.wait_ge(evacuated, E(S_OUT + 4 * i + j - 4))
                    dense(S_OUT + 4 * i + j, j, j, order=order, x_base=X_OUT if j == 0 else None)
            sum_features(2)
            ffn(S_FFN2, 44, X_FFN2)
            sum_features(3)
            pe.wait_ge(p_done, 1)
            pe.wait_ge(rms_done, 4)
            for t in range(2):
                pe.wait_ge(w_lo_done, S_PLE + t + 1)
                if t:
                    pe.wait_ge(evacuated, E(S_PLE))
                for q in range(8):
                    for k in range(PLE_K):
                        e = three(bank[q][:, 0:NTOK], t % 2, PLE_K * q + k, p_hi[:, k, :], p_lo[:, k, :],
                                  k == 0, k == PLE_K - 1)
                e.then_inc(slab_done, 1)
            with pe.Fori(0, 4) as i:
                for j in range(4):
                    s = S_PLE + 2 + 4 * i + j
                    pe.wait_ge(evacuated, E(s - 4))
                    if j == 0:
                        pe.wait_ge(evacuated, E(S_PLE + 1))
                    dense(s, j, j, x_base=X_PLE if j == 0 else None)
            sum_features(4)




def blocks(w, rows, cols):
    return w.reshape(rows, P, cols, P).transpose(0, 2, 1, 3)


def as_slab(b):
    return np.ascontiguousarray(np.moveaxis(b, -3, -2)).reshape(*b.shape[:-3], P, SLAB * P)


def ffn_slabs(w_gate, w_up, w_down):
    nf = DFF // P
    out = np.empty((CHUNKS, FFN_SLABS, P, SLAB * P), np.float32)
    for which, w in enumerate((w_gate, w_up)):
        b = as_slab(blocks(w, KD, nf).transpose(1, 0, 2, 3))
        out[:, which:8:2] = b.reshape(CHUNKS, FPC, P, SLAB * P)
    d = blocks(w_down, nf, KD).reshape(CHUNKS, FPC, 4, 4, P, P)
    out[:, 8:] = as_slab(d.transpose(0, 2, 1, 3, 4, 5).reshape(CHUNKS, 4, SLAB, P, P))
    return out.reshape(N_FFN, P, SLAB * P)


def per_tile(v):
    return v.reshape(-1, P).T


def kernel(**inp):
    from concourse import bacc
    from concourse.bass_utils import run_bass_kernel_spmd

    a = {k: np.asarray(v) for k, v in inp.items()}
    ns = NB * TS

    def feature_major(prompt, sample, tiles):
        t = np.concatenate([prompt.reshape(SEQ, -1), sample.reshape(ns, -1)], 0)
        return np.ascontiguousarray(t.T.reshape(tiles, P, NTOK).transpose(1, 0, 2))

    w_in = as_slab(blocks(a["w_in"][0], KD, N_IN).transpose(1, 0, 2, 3))
    conv_order = [24 + 8 * (j % 2) + j // 2 for j in range(16)]
    w_in = np.ascontiguousarray(w_in[list(range(24)) + conv_order])
    w_out = as_slab(blocks(a["w_out"][0], KD, KD).transpose(1, 0, 2, 3))
    gate = as_slab(blocks(a["w_ple_gate"][0], KD, KD).transpose(1, 0, 2, 3))
    proj = as_slab(blocks(a["w_ple_proj"][0], PLE_K, KD).reshape(PLE_K, 2, 8, P, P).transpose(1, 2, 0, 3, 4)
                   .reshape(2, SLAB, P, P))
    k_pool = np.ascontiguousarray(a["cache_k"][0].transpose(0, 3, 2, 1)).reshape(NPOOL, P, HEADS * PAGE)
    v_pool = np.ascontiguousarray(a["cache_v"][0]).reshape(NPOOL, PAGE, HEADS * P)
    state = np.zeros((P, 8, NB, HIST + TS), np.float32)
    state[:, :, :, :HIST] = a["state_conv"][0].reshape(NB, HIST, 8, P).transpose(3, 2, 0, 1)
    vecs = np.concatenate([per_tile(a[n].reshape(-1)) for n in
                           ("g_ffn1", "g_mix", "g_ffn2", "g_ple", "g_final", "g_conv_norm", "b_conv_norm",
                            "g_subln")], 1)
    dw = np.concatenate([a["w_dw"][0].reshape(TAPS, 8, P).transpose(2, 1, 0),
                         a["b_dw"][0].reshape(8, P).T[:, :, None]], 2)
    lams = np.concatenate([a[n].reshape(1, 1, QD) for n in ("lambda_q1", "lambda_q2", "lambda_k1", "lambda_k2")], 1)
    arrays = {
        "x_t": feature_major(a["x_prompt"], a["x_sample"], KD),
        "slabs_ffn1": ffn_slabs(a["w_ffn1_gate"][0], a["w_ffn1_up"][0], a["w_ffn1_down"][0]),
        "slabs_in": w_in, "slabs_out": w_out,
        "slabs_ffn2": ffn_slabs(a["w_ffn2_gate"][0], a["w_ffn2_up"][0], a["w_ffn2_down"][0]),
        "slabs_ple": np.concatenate([proj, gate], 0),
        "k_pool": k_pool, "v_pool": v_pool,
        "pages": a["page_table"].reshape(1, -1),
        "state_ext": state,
        "p_t": feature_major(a["p_prompt"], a["p_sample"], PLE_K),
        "vecs": vecs, "dw": dw, "lams": lams,
    }
    arrays = {k: np.ascontiguousarray(v) for k, v in arrays.items()}
    outs = {"y_t": (P, KD, NTOK), "k_t": (P, HEADS, NTOK), "v_tok": (NTOK, HEADS * P),
            "conv_p": (P, 8, HIST), "conv_s": (P, 8, NB, HIST + TS)}

    nc = bacc.Bacc("TRN2", target_bir_lowering=False, num_devices=1)
    args = {k: nc.dram_tensor(k, v.shape, mybir.dt.from_np(v.dtype), kind="ExternalInput").ap()
            for k, v in arrays.items()}
    args |= {k: nc.dram_tensor(k, s, F32, kind="ExternalOutput").ap() for k, s in outs.items()}
    hymba_step(nc, **args)
    res = run_bass_kernel_spmd(nc, [arrays], core_ids=[0]).results[0]

    y = res["y_t"].transpose(2, 1, 0).reshape(NTOK, D)
    k = res["k_t"].transpose(2, 1, 0).reshape(NTOK, HEADS, P)
    v = res["v_tok"].reshape(NTOK, HEADS, P)
    conv_p = res["conv_p"].transpose(2, 1, 0).reshape(1, 1, HIST, 8 * P)
    conv_s = res["conv_s"][:, :, :, TS:].transpose(2, 3, 1, 0).reshape(1, NB, HIST, 8 * P)
    out = (y[:SEQ].reshape(1, SEQ, D), y[SEQ:].reshape(NB, TS, D),
           k[:SEQ].reshape(1, 1, SEQ, HEADS, P), v[:SEQ].reshape(1, 1, SEQ, HEADS, P), conv_p,
           k[SEQ:].reshape(1, NB, TS, HEADS, P), v[SEQ:].reshape(1, NB, TS, HEADS, P), conv_s)
    return tuple(np.ascontiguousarray(o) for o in out)
```

```python
from contextlib import ExitStack

import numpy as np

import concourse.bass as bass
from concourse import mybir

F32 = mybir.dt.float32
F32R = mybir.dt.float32r
I32 = mybir.dt.int32
ALU = mybir.AluOpType
ACT = mybir.ActivationFunctionType
AX = mybir.AxisListType

P = 128
D = 2048
SEQ = 256
NB = 8
TS = 8
NTOK = SEQ + NB * TS
KD = D // P
DFF = 5632
FPC = 4
CHUNKS = DFF // P // FPC
HEADS = 8
QD = 64
PAGE = 128
PAST = 2048
PAGES = PAST // PAGE
NPOOL = 160
TAPS = 31
HIST = TAPS - 1
PLE_K = 2
RMS_EPS = 1e-6
LN_EPS = 1e-5
LAM_INIT = 0.2
MASKED = -1e32

SLAB = 16
RAW = 4
FFN_SLABS = 12
N_FFN = CHUNKS * FFN_SLABS
N_IN = 40
S_FFN1 = 0
S_IN = S_FFN1 + N_FFN
S_OUT = S_IN + N_IN
S_FFN2 = S_OUT + KD
S_PLE = S_FFN2 + N_FFN
N_PLE = 2 + KD
SLABS_ALL = S_PLE + N_PLE

KV_SLOTS = PAGES // 2
KCOLS = PAST + NB * TS
EV0 = 4

G_FFN1, G_MIX, G_FFN2, G_PLE, G_FINAL = (KD * i for i in range(5))
G_CN = KD * 5
B_CN = G_CN + 8
G_SUB = B_CN + 8
N_VEC = G_SUB + 1


def hymba_step(nc, x_t, slabs_ffn1, slabs_in, slabs_out, slabs_ffn2, slabs_ple, k_pool, v_pool, pages,
               state_ext, p_t, vecs, dw, lams, y_t, k_t, v_tok, conv_p, conv_s):
    ctx = ExitStack()
    with ctx:
        arena_bytes = nc.sbuf_bytes_remaining - 64
        start = nc.sbuf_base
        arena_bytes -= arena_bytes % 64
        ctx.enter_context(nc.sbuf_tensor("arena", [P, arena_bytes // 4], F32))
        start = (start + 31) // 32 * 32
        at = [start]

        def place(name, shape, dt=F32, offset=None):
            size = int(np.prod(shape[1:])) * 4
            size = (size + 31) // 32 * 32
            if offset is None:
                offset = at[0]
                at[0] += size
            assert offset + size <= start + arena_bytes, (name, offset + size - start, arena_bytes)
            return nc.alloc_sbuf_tensor_at(name, shape, dt, offset=offset)

        h = place("h", [P, KD, NTOK])
        x_at = at[0]
        x_hi = place("x_hi", [P, KD, NTOK], F32R)
        x_lo = place("x_lo", [P, KD, NTOK], F32R)
        raw = [place(f"raw{i}", [P, SLAB * P]) for i in range(RAW)]
        w_at = at[0]
        w_hi = [place(f"w_hi{i}", [P, SLAB, P], F32R) for i in range(2)]
        w_lo = [place(f"w_lo{i}", [P, SLAB, P], F32R) for i in range(2)]
        mid_at = at[0]
        mid_hi = place("mid_hi", [P, FPC, NTOK], F32R)
        mid_lo = place("mid_lo", [P, FPC, NTOK], F32R)
        qk_at = at[0]
        qT = place("qT", [P, HEADS, NTOK])
        kT = place("kT", [P, HEADS, NTOK])
        v_at = at[0]
        vtok = place("vtok", [P, 3, HEADS * P])
        u_p = place("u_p", [P, 8, HIST + SEQ])
        u_s = place("u_s", [P, 8, NB, HIST + TS])
        oT = place("oT", [P, HEADS, NTOK])
        sig = [place(f"sig{i}", [P, NTOK]) for i in range(2)]
        tmp = [place(f"tmp{i}", [P, NTOK]) for i in range(2)]
        gated = place("gated", [P, NTOK])
        ssq = place("ssq", [P, NTOK])
        rms = ssq
        rinv = place("rinv", [P, NTOK])
        ident = place("ident", [P, P])
        ones = place("ones", [P, P])
        vec = place("vec", [P, N_VEC])
        wdw = place("wdw", [P, 8, TAPS + 1])
        eps = place("eps", [P, 2])
        slope_s = place("slope_s", [P, 2])
        slope_p = place("slope_p", [P, HEADS])
        lam_row = place("lam_row", [1, 4, QD], offset=mid_at)
        lam_s = place("lam_s", [1, 8])
        neglam = place("neglam", [P, 1])
        g_sub8 = place("g_sub8", [P, 1])
        page_row = place("page_row", [1, NB * PAGES], I32)
        l_sum = place("l_sum", [P, 2 * NB])
        l_inv = place("l_inv", [P, 2 * NB])
        neg_max = place("neg_max", [P, 2])
        head_max = place("head_max", [P, 2, 2])
        head_sum = place("head_sum", [P, 2, 2])
        head_inv = place("head_inv", [P, 2, 2])
        head_c1 = place("head_c1", [P, 2])
        conv_y = place("conv_y", [P, 8, NTOK], offset=mid_at)
        x2_hi = place("x2_hi", [P, KD, NTOK], F32R, offset=qk_at)
        x2_lo = place("x2_lo", [P, KD, NTOK], F32R, offset=v_at)
        v_tmp = [place(f"v_tmp{i}", [P, NTOK], offset=mid_at + 4 * NTOK * i) for i in range(4)]
        S = place("S", [P, 2, KCOLS], offset=x_at)
        ET = place("ET", [P, 2, PAGES + 1, P], offset=x_at + 2 * KCOLS * 4)
        w_cur = [w_at]

        def in_w(name, shape, dt=F32):
            t = place(name, shape, dt, offset=w_cur[0])
            w_cur[0] += (int(np.prod(shape[1:])) * 4 + 31) // 32 * 32
            assert w_cur[0] <= mid_at
            return t

        kpos = in_w("kpos", [P, PAST])
        kpos_p = in_w("kpos_p", [P, 3 * P])
        kpos_n = in_w("kpos_n", [P, 120])
        n_mask = in_w("n_mask", [P, 120])
        n_keep = in_w("n_keep", [P, 120])
        trow_i = in_w("trow_i", [P, 1], I32)
        trow = in_w("trow", [P, 1])
        comb = in_w("comb", [P, 4, TS])
        comb1 = in_w("comb1", [P, 4, TS])
        Qb = in_w("Qb", [P, HEADS, 32])
        q_st = in_w("q_st", [P, SEQ])
        k_st = in_w("k_st", [P, SEQ])
        v_st = in_w("v_st", [P, 2, P])
        S_p = in_w("S_p", [P, 2, 3 * P])
        w_p = in_w("w_p", [P, 3 * P])
        wT_p = in_w("wT_p", [P, 3 * P])
        O_n = in_w("O_n", [P, 2, P])
        y_c = in_w("y_c", [P, NTOK])
        u_st = in_w("u_st", [P, NB, HIST + TS])
        wdw_st = in_w("wdw_st", [P, TAPS + 1])
        tap_s = [in_w(f"tap_s{i}", [P, NB, TS]) for i in range(2)]
        sub_sq = [place(f"sub_sq{i}", [P, NTOK], offset=w_at + 4 * NTOK * i) for i in range(HEADS)]
        proj = place("proj", [P, KD, NTOK], offset=qk_at)
        p_at = v_at + 4 * KD * NTOK
        p_raw = place("p_raw", [P, PLE_K, NTOK], offset=p_at)
        p_hi = place("p_hi", [P, PLE_K, NTOK], F32R, offset=p_at + 4 * PLE_K * NTOK)
        p_lo = place("p_lo", [P, PLE_K, NTOK], F32R, offset=p_at + 8 * PLE_K * NTOK)

        bank = [ctx.enter_context(nc.psum_tensor(f"bank{i}", [P, 512], F32)) for i in range(8)]
        NORM = bank[7]
        K_BANK, T_BANK, O_BANK = bank[0:2], bank[2:4], bank[4:6]
        G_BANK, H_BANK = bank[6], bank[7]

        def sem(name):
            return ctx.enter_context(nc.semaphore(name))

        x_in = [sem(f"x_in{c}") for c in range(4)]
        vec_in = sem("vec_in")
        small_in = sem("small_in")
        state_in = sem("state_in")
        p_in = sem("p_in")
        raw_in = [sem(f"raw_in{i}") for i in range(RAW)]
        kv_in = [sem(f"kv_in{i}") for i in range(RAW)]
        stored = sem("stored")
        y_stored = sem("y_stored")
        w_hi_done = sem("w_hi_done")
        w_lo_done = sem("w_lo_done")
        slab_done = sem("slab_done")
        evacuated = sem("evacuated")
        sig_done = sem("sig_done")
        gated_done = sem("gated_done")
        silu_done = sem("silu_done")
        mid_raw = sem("mid_raw")
        u_done = sem("u_done")
        proj_mm = sem("proj_mm")
        proj_read = sem("proj_read")
        mid_hi_done = sem("mid_hi_done")
        mid_done = sem("mid_done")
        h_done = sem("h_done")
        sq_done = sem("sq_done")
        ssq_done = sem("ssq_done")
        norm_mm = sem("norm_mm")
        rms_done = sem("rms_done")
        r_done = sem("r_done")
        xt_done = sem("xt_done")
        x_hi_done = sem("x_hi_done")
        x_done = sem("x_done")
        consts = sem("consts")
        attc = sem("attc")
        cchain = sem("cchain")
        lam_exp = sem("lam_exp")
        lam_mm = sem("lam_mm")
        v_turned = sem("v_turned")
        vtok_done = sem("vtok_done")
        v_used = sem("v_used")
        qb_ready = sem("qb_ready")
        scored = sem("scored")
        s_read = sem("s_read")
        maxed = sem("maxed")
        exped = sem("exped")
        l_done = sem("l_done")
        turned = sem("turned")
        et_done = sem("et_done")
        pv_done = sem("pv_done")
        o_read = sem("o_read")
        comb_mm = sem("comb_mm")
        o_done = sem("o_done")
        staged = sem("staged")
        h_scored = sem("h_scored")
        hs_done = sem("hs_done")
        h_maxed = sem("h_maxed")
        h_exped = sem("h_exped")
        h_chain = sem("h_chain")
        h_w = sem("h_w")
        h_turned = sem("h_turned")
        h_wT = sem("h_wT")
        h_pv = sem("h_pv")
        h_o = sem("h_o")
        tapped = sem("tapped")
        s_mult = sem("s_mult")
        s_tapped = sem("s_tapped")
        ln_mm = sem("ln_mm")
        ln_d = sem("ln_d")
        ln_sq = sem("ln_sq")
        ln_rms = sem("ln_rms")
        ln_chain = sem("ln_chain")
        ln_sig = sem("ln_sig")
        ln_done = sem("ln_done")
        sub_sqd = sem("sub_sqd")
        sub_mm = sem("sub_mm")
        sub_rms = sem("sub_rms")
        sub_r = sem("sub_r")
        p_hi_done = sem("p_hi_done")
        p_done = sem("p_done")
        y_done = sem("y_done")

        N_SMALL = 2

        def E(s):
            return s + 1 + EV0

        X_FFN1, X_IN, X_OUT, X_FFN2, X_PLE = (KD * i for i in range(5))
        X_OF = {0: X_FFN1, 1: X_IN, 2: X_FFN2, 3: X_PLE}
        GAINS = {0: G_FFN1, 1: G_MIX, 2: G_FFN2, 3: G_PLE}
        X_BUF = {0: (x_hi, x_lo), 1: (x_hi, x_lo), 2: (x2_hi, x2_lo), 3: (x_hi, x_lo)}

        block = ctx.enter_context(nc.Block())

        @block.sync
        def _(sp):
            def slab(src, idx, s, slot, wait):
                if wait == "split":
                    sp.wait_ge(w_lo_done, s - RAW + 1)
                sp.dma_start(raw[slot][:, :], src[idx, :, :]).then_inc(raw_in[slot], 16)

            sp.dma_start(vec[:, :], vecs).then_inc(vec_in, 16)
            sp.dma_start(lam_row[0:1, :, :], lams).then_inc(vec_in, 16)
            for t in range(4):
                sp.dma_start(h[:, 4 * t:4 * t + 4, :], x_t[:, 4 * t:4 * t + 4, :]).then_inc(x_in[t], 16)
                if t == 0:
                    slab(slabs_ffn1, 0, 0, 0, None)
            for j in range(1, RAW):
                slab(slabs_ffn1, j, j, j, None)
            with sp.Fori(1, N_FFN // RAW) as i:
                for j in range(RAW):
                    slab(slabs_ffn1, 4 * i + j, S_FFN1 + 4 * i + j, j, "split")
            with sp.Fori(0, N_IN // RAW) as i:
                for j in range(RAW):
                    slab(slabs_in, 4 * i + j, S_IN + 4 * i + j, j, "split")

            sp.wait_ge(small_in, 16 * N_SMALL)

            def two_pages(pool, b, g, slot):
                for e in range(2):
                    page = sp.value_load(page_row[0:1, bass.ds(PAGES * b + 2 * g + e, 1)],
                                         min_val=0, max_val=NPOOL - 1)
                    sp.dma_start(raw[slot][:, 1024 * e:1024 * e + 1024],
                                 pool[bass.ds(page, 1), :, :].rearrange("o p n -> (o p) n")
                                 ).then_inc(kv_in[slot], 16)

            def keys_used(b, g):
                sp.wait_ge(scored, 10 * b + 2 * (g // 2) + 2)

            def values_used(b, g):
                sp.wait_ge(v_used, KV_SLOTS * b + g + 1)

            def load_keys(b, before):
                for g in range(KV_SLOTS):
                    if g < RAW:
                        before(g + RAW)
                    else:
                        keys_used(b, g - RAW)
                    two_pages(k_pool, b, g, g % RAW)

            def load_values(b, before):
                for g in range(KV_SLOTS):
                    if g < RAW:
                        before(g + RAW)
                    else:
                        values_used(b, g - RAW)
                    two_pages(v_pool, b, g, g % RAW)

            load_keys(0, lambda g: sp.wait_ge(w_lo_done, S_OUT - KV_SLOTS + 1 + g))
            load_keys(1, lambda g: keys_used(0, g))
            load_values(0, lambda g: keys_used(1, g))
            with sp.Fori(2, NB) as b:
                load_keys(b, lambda g: values_used(b - 2, g))
                load_values(b - 1, lambda g: keys_used(b, g))
            load_values(NB - 1, lambda g: values_used(NB - 2, g))

            for j in range(RAW):
                values_used(NB - 1, j + RAW)
                slab(slabs_out, j, S_OUT + j, j, None)
            with sp.Fori(1, KD // RAW) as i:
                for j in range(RAW):
                    slab(slabs_out, 4 * i + j, S_OUT + 4 * i + j, j, "split")
            with sp.Fori(0, N_FFN // RAW) as i:
                for j in range(RAW):
                    slab(slabs_ffn2, 4 * i + j, S_FFN2 + 4 * i + j, j, "split")
            with sp.Fori(0, N_PLE // RAW) as i:
                for j in range(RAW):
                    slab(slabs_ple, 4 * i + j, S_PLE + 4 * i + j, j, "split")
            for j in range(N_PLE % RAW):
                s = N_PLE // RAW * RAW + j
                slab(slabs_ple, s, S_PLE + s, j, "split")
            for c in range(4):
                sp.wait_ge(y_done, 4 * c + 4)
                sp.dma_start(y_t[:, 4 * c:4 * c + 4, :], proj[:, 4 * c:4 * c + 4, :]).then_inc(y_stored, 16)
            sp.wait_ge(stored, 16 * 5)
            sp.wait_ge(y_stored, 16 * 4)

        @block.gpsimd
        def _(pool):
            for dst, src in ((page_row[:, :], pages), (wdw[:, :, :], dw)):
                pool.dma_start(dst, src).then_inc(small_in, 16)
            nc.gpsimd.memset(ones[:, :], 1.0)
            nc.gpsimd.memset(ident[:, :], 0.0)
            nc.gpsimd.memset(eps[:, 0:1], RMS_EPS)
            nc.gpsimd.memset(eps[:, 1:2], LN_EPS)
            nc.gpsimd.memset(u_p[:, :, 0:HIST], 0.0)
            for hd in range(HEADS):
                last = nc.gpsimd.memset(slope_p[:, hd:hd + 1], 2.0 ** -(hd + 1))
            last.then_inc(consts, 1)
            pool.wait_ge(consts, 1)
            nc.gpsimd.affine_select(out=ident[:, :], in_=ident[:, :], compare_op=ALU.not_equal, fill=1.0,
                                    base=0, pattern=[[-1, P]], channel_multiplier=1).then_inc(consts, 1)

            def sum_squares(norm):
                def add(n, u):
                    pool.wait_ge(sq_done, KD * norm + n + 1)
                    pool.wait_ge(ssq_done, KD * norm + n)
                    nc.gpsimd.tensor_tensor(ssq[:, :], ssq[:, :], tmp[u][:, :], ALU.add).then_inc(ssq_done, 1)
                pool.wait_ge(sq_done, KD * norm + 1)
                nc.gpsimd.tensor_copy(ssq[:, :], tmp[0][:, :]).then_inc(ssq_done, 1)
                add(1, 1)
                with pool.Fori(1, KD // 2) as kk:
                    for u in range(2):
                        add(2 * kk + u, u)

            sum_squares(0)
            pool.dma_start(u_s[:, :, :, :], state_ext).then_inc(state_in, 16)
            sum_squares(1)

            def queries(b):
                if not isinstance(b, int):
                    pool.wait_ge(scored, 10 * b)
                col = SEQ + TS * b
                nc.gpsimd.tensor_copy(Qb[0:QD, :, 0:TS], qT[0:QD, :, bass.ds(col, TS)]).then_inc(qb_ready, 1)
                pool.wait_ge(qb_ready, 2 * b + 1)
                nc.gpsimd.tensor_copy(Qb[QD:P, :, TS:2 * TS], qT[QD:P, :, bass.ds(col, TS)]).then_inc(qb_ready, 1)
                pool.wait_ge(qb_ready, 2 * b + 2)

            pool.wait_ge(slab_done, S_OUT)
            nc.gpsimd.memset(Qb[:, :, :], 0.0).then_inc(attc, 1)
            pool.wait_ge(attc, 1)
            queries(0)
            nc.gpsimd.iota(kpos[:, :], [[1, PAST]], base=-PAST, channel_multiplier=0,
                           allow_small_or_imprecise_dtypes=True).then_inc(attc, 1)
            nc.gpsimd.memset(comb[:, :, :], 0.0)
            nc.gpsimd.memset(comb1[:, :, :], 0.0)
            nc.gpsimd.iota(kpos_p[:, 0:P], [[1, P]], base=0, channel_multiplier=-1,
                           allow_small_or_imprecise_dtypes=True)
            nc.gpsimd.iota(kpos_p[:, P:3 * P], [[1, 2 * P]], base=-P, channel_multiplier=-1,
                           allow_small_or_imprecise_dtypes=True)
            nc.gpsimd.iota(kpos_n[:, :], [[1, 120]], base=-56, channel_multiplier=0,
                           allow_small_or_imprecise_dtypes=True)
            nc.gpsimd.iota(trow_i[:, :], [[0, 1]], base=0, channel_multiplier=1).then_inc(attc, 1)
            pool.wait_ge(attc, 3)
            nc.gpsimd.affine_select(out=kpos_p[:, 0:P], in_=kpos_p[:, 0:P], compare_op=ALU.is_ge,
                                    fill=MASKED, base=0, pattern=[[-1, P]], channel_multiplier=1)
            nc.gpsimd.affine_select(out=kpos_p[:, P:3 * P], in_=kpos_p[:, P:3 * P], compare_op=ALU.is_ge,
                                    fill=MASKED, base=P, pattern=[[-1, 2 * P]], channel_multiplier=1)
            nc.gpsimd.affine_select(out=kpos_n[:, :], in_=kpos_n[:, :], compare_op=ALU.is_ge,
                                    fill=1000.0, base=-56, pattern=[[1, 120]], channel_multiplier=0)
            nc.gpsimd.affine_select(out=comb[:, :, :], in_=comb[:, :, :], compare_op=ALU.not_equal,
                                    fill=1.0, base=0, pattern=[[-32, 4], [-1, TS]], channel_multiplier=1)
            nc.gpsimd.affine_select(out=comb1[:, :, :], in_=comb1[:, :, :], compare_op=ALU.not_equal,
                                    fill=1.0, base=-TS, pattern=[[-32, 4], [-1, TS]],
                                    channel_multiplier=1).then_inc(attc, 1)
            pool.wait_ge(evacuated, E(S_OUT - 1))
            pool.wait_ge(u_done, 8)
            pool.wait_ge(vtok_done, HEADS)
            pool.dma_start(k_t, kT[:, :, :]).then_inc(stored, 16)
            pool.dma_start(v_tok[0:SEQ, :].rearrange("(a p) n -> p a n", p=P), vtok[:, 0:2, :]).then_inc(stored, 16)
            pool.dma_start(v_tok[SEQ:NTOK, :], vtok[P - NB * TS:P, 2, :]).then_inc(stored, 16)
            pool.dma_start(conv_p, u_p[:, :, SEQ:SEQ + HIST]).then_inc(stored, 16)
            pool.dma_start(conv_s, u_s[:, :, :, :]).then_inc(stored, 16)

            def iteration(b):
                first = isinstance(b, int)
                if not first:
                    queries(b)
                if not first:
                    pool.wait_ge(h_pv, b)
                nc.gpsimd.tensor_copy(q_st[:, :], qT[:, bass.ds(b, 1), 0:SEQ].rearrange("p o n -> p (o n)"))
                nc.gpsimd.tensor_copy(k_st[:, :], kT[:, bass.ds(b, 1), 0:SEQ].rearrange("p o n -> p (o n)"))
                nc.gpsimd.tensor_copy(v_st[:, :, :], vtok[:, 0:2, bass.ds(P * b, P)]).then_inc(staged, 1)
                if not first:
                    pool.wait_ge(ln_d, b)
                    pool.wait_ge(s_tapped, TAPS * b)
                nc.gpsimd.tensor_copy(u_st[:, :, :], u_s[:, bass.ds(b, 1), :, :].rearrange("p o s t -> p (o s) t"))
                nc.gpsimd.tensor_copy(wdw_st[:, :], wdw[:, bass.ds(b, 1), :].rearrange("p o n -> p (o n)")
                                      ).then_inc(s_mult, 1)
                ys = y_c[:, SEQ:NTOK].rearrange("p (s t) -> p s t", t=TS)

                def spread(c):
                    return wdw_st[:, c:c + 1].unsqueeze(2).to_broadcast([P, NB, TS])
                pool.wait_ge(s_mult, (TAPS + 1) * b + 1)
                nc.gpsimd.tensor_tensor(tap_s[0][:, :, :], u_st[:, :, 0:TS], spread(0), ALU.mult).then_inc(s_mult, 1)
                pool.wait_ge(s_mult, (TAPS + 1) * b + 2)
                nc.gpsimd.tensor_tensor(ys, tap_s[0][:, :, :], spread(TAPS), ALU.add).then_inc(s_tapped, 1)
                for k in range(1, TAPS):
                    nc.gpsimd.tensor_scalar(tap_s[k % 2][:, :, :], u_st[:, :, k:k + TS], wdw_st[:, k:k + 1], None,
                                            ALU.mult).then_inc(s_mult, 1)
                    pool.wait_ge(s_mult, (TAPS + 1) * b + 2 + k)
                    pool.wait_ge(s_tapped, TAPS * b + k)
                    nc.gpsimd.tensor_tensor(ys, ys, tap_s[k % 2][:, :, :], ALU.add).then_inc(s_tapped, 1)

            iteration(0)
            with pool.Fori(1, NB) as b:
                iteration(b)
            pool.wait_ge(pv_done, NB)
            pool.wait_ge(h_pv, HEADS)
            pool.wait_ge(staged, HEADS)
            pool.wait_ge(stored, 16 * 5)
            pool.dma_start(p_raw[:, :, :], p_t).then_inc(p_in, 16)
            for norm in (2, 3, 4):
                sum_squares(norm)

        @block.scalar
        def _(act):
            def split_hi(s, slot2, slot4, before=True):
                act.wait_ge(raw_in[slot4], 16 * (s // RAW) + 16)
                if before:
                    act.wait_ge(slab_done, s - 1)
                nc.scalar.copy(w_hi[slot2][:, :, :], raw[slot4][:, :].rearrange("p (k n) -> p k n", n=P)
                               ).then_inc(w_hi_done, 1)

            def split_next(base, i4, j):
                n = j + 1
                act.wait_ge(raw_in[n % 4], 16 * (base // 4 + i4 + n // 4 + 1))
                act.wait_ge(slab_done, base + 4 * i4 + j)
                nc.scalar.copy(w_hi[n % 2][:, :, :], raw[n % 4][:, :].rearrange("p (k n) -> p k n", n=P)
                               ).then_inc(w_hi_done, 1)

            def square(norm, n, buf):
                act.wait_ge(h_done, KD * norm + n + 1)
                if norm or n >= 2:
                    act.wait_ge(ssq_done, KD * norm + n - 1)
                nc.scalar.activation(tmp[buf][:, :], h[:, bass.ds(n, 1), :].rearrange("p o n -> p (o n)"),
                                     ACT.Square).then_inc(sq_done, 1)

            def root(norm):
                act.wait_ge(norm_mm, norm + 1)
                nc.scalar.activation(rms[:, :], NORM[:, 0:NTOK], ACT.Sqrt, bias=eps[:, 0:1],
                                     scale=1.0 / D).then_inc(rms_done, 1)

            def upper(norm, n):
                nc.scalar.activation(X_BUF[norm][0][:, bass.ds(n, 1), :].rearrange("p o n -> p (o n)"),
                                     h[:, bass.ds(n, 1), :].rearrange("p o n -> p (o n)"), ACT.Copy,
                                     scale=vec[:, bass.ds(GAINS[norm] + n, 1)]).then_inc(x_hi_done, 1)

            def ffn_chunk(base, i, f_base, lag=None, norm_in=None, norm=None):
                s0 = base + FFN_SLABS * i

                def sigmoid(j):
                    if j < 8 and j % 2 == 0:
                        f = j // 2
                        act.wait_ge(gated_done, f_base + FPC * i + f + 1 + (8 if base else 0))
                        nc.scalar.activation(sig[f % 2][:, :], gated[:, :], ACT.Sigmoid).then_inc(sig_done, 1)

                for j in range(FFN_SLABS):
                    split_next(base, 3 * i, j)
                    if norm_in == 0 and j < 2:
                        for n in range(8 * j, 8 * j + 8):
                            square(0, n, n % 2)
                    if norm_in is None or j > lag + 1:
                        sigmoid(j)
                    elif j == lag + 1:
                        root(norm_in)
                        for early in range(lag + 2):
                            sigmoid(early)
                    if j >= 8 and norm is not None:
                        for q in range(4):
                            n = 4 * (j - 8) + q
                            act.wait_ge(h_done, KD * norm + n + 1)
                            upper(norm, n)
                            square(norm, n, q % 2)

            def ffn(base, f_base, norm, lag):
                ffn_chunk(base, 0, f_base, lag=lag, norm_in=norm - 1)
                with act.Fori(1, CHUNKS - 1) as i:
                    ffn_chunk(base, i, f_base)
                ffn_chunk(base, CHUNKS - 1, f_base, norm=norm)

            act.wait_ge(cchain, 2)
            nc.scalar.activation(lam_s[0:1, 2:4], lam_s[0:1, 0:2], ACT.Exp).then_inc(lam_exp, 1)
            act.wait_ge(vec_in, 32)
            for n in range(KD):
                act.wait_ge(x_in[n // 4], 16)
                upper(0, n)
                if n == 3:
                    split_hi(0, 0, 0, False)
            ffn(S_FFN1, 0, 1, 2)

            for j in range(4):
                split_next(S_IN, 0, j)
                if j == 1:
                    root(1)
            with act.Fori(1, 4) as i:
                for j in range(4):
                    split_next(S_IN, i, j)
            with act.Fori(0, 2) as i:
                for j in range(4):
                    split_next(S_IN + 16, i, j)
                for j in range(4):
                    act.wait_ge(v_turned, 4 * i + j + 1)
                    nc.scalar.copy(vtok[:, :, bass.ds(P * (4 * i + j), P)],
                                   bank[4 + j][:, 0:3 * P].rearrange("p (a n) -> p a n", n=P)).then_inc(vtok_done, 1)

            def conv_in(i, last):
                for j in range(4):
                    if not (last and j == 3):
                        split_next(S_IN + 24, i, j)
                    if j % 2:
                        act.wait_ge(gated_done, 44 + 2 * i + j // 2 + 1)
                        nc.scalar.activation(sig[j // 2][:, :], gated[:, :], ACT.Sigmoid).then_inc(sig_done, 1)
            with act.Fori(0, 3) as i:
                conv_in(i, False)
            conv_in(3, True)

            def exp_scores(b):
                for half in range(2):
                    act.wait_ge(maxed, 2 * b + half + 1)
                    nc.scalar.activation(S[:, half, :], S[:, half, :], ACT.Exp, bias=neg_max[:, half:half + 1],
                                         accum_out=l_sum[:, bass.ds(2 * b + half, 1)]).then_inc(exped, 1)

            def prompt_head(b):
                act.wait_ge(h_maxed, 2 * b + 2)
                for m in range(2):
                    nc.scalar.activation(S_p[:, m, 0:P], S_p[:, m, 0:P], ACT.Exp,
                                         bias=head_max[:, 0, m:m + 1], accum_out=head_sum[:, 0, m:m + 1])
                for m in range(2):
                    e = nc.scalar.activation(S_p[:, m, P:3 * P], S_p[:, m, P:3 * P], ACT.Exp,
                                             bias=head_max[:, 1, m:m + 1], accum_out=head_sum[:, 1, m:m + 1])
                e.then_inc(h_exped, 1)

            def prompt_copy(b):
                act.wait_ge(h_turned, b + 1)
                nc.scalar.copy(wT_p[:, :], G_BANK[:, 0:3 * P]).then_inc(h_wT, 1)

            def out_read(b):
                act.wait_ge(pv_done, b + 1)
                act.wait_ge(l_done, b + 1)
                for half in range(2):
                    nc.scalar.activation(O_n[:, half, :], O_BANK[half][:, 0:P], ACT.Copy,
                                         scale=l_inv[:, bass.ds(2 * b + half, 1)]).then_inc(o_read, 1)

            def copy_ET(b):
                for idx in range(10):
                    half, g = idx % 2, idx // 2
                    act.wait_ge(turned, 10 * b + idx + 1)
                    if g < 4:
                        e = nc.scalar.copy(ET[:, half, 4 * g:4 * g + 4, :],
                                           T_BANK[idx % 2][:, :].rearrange("p (a n) -> p a n", n=P))
                    else:
                        e = nc.scalar.copy(ET[P - NB * TS:P, half, PAGES, :], T_BANK[idx % 2][P - NB * TS:P, 0:P])
                    e.then_inc(et_done, 1)
                    if idx == 5 and not isinstance(b, int):
                        out_read(b - 1)

            def conv_norm(b):
                act.wait_ge(ln_d, b + 1)
                nc.scalar.activation(tmp[0][:, :], gated[:, :], ACT.Square).then_inc(ln_sq, 1)
                act.wait_ge(ln_mm, 2 * b + 2)
                nc.scalar.activation(rms[:, :], H_BANK[:, 0:NTOK], ACT.Sqrt, bias=eps[:, 1:2],
                                     scale=1.0 / P).then_inc(ln_rms, 1)
                act.wait_ge(ln_chain, 3 * b + 3)
                nc.scalar.activation(sig[0][:, :], tmp[1][:, :], ACT.Sigmoid).then_inc(ln_sig, 1)

            def attention(b):
                if not isinstance(b, int):
                    conv_norm(b - 1)
                prompt_head(b)
                exp_scores(b)
                prompt_copy(b)
                copy_ET(b)

            attention(0)
            with act.Fori(1, NB) as b:
                attention(b)
            conv_norm(NB - 1)
            out_read(NB - 1)

            act.wait_ge(pv_done, NB)
            with act.Fori(0, 4) as i:
                for u in range(2):
                    k = HEADS + 2 * i + u
                    act.wait_ge(ln_done, NB)
                    nc.scalar.copy(x_hi[:, bass.ds(k, 1), :].rearrange("p o n -> p (o n)"),
                                   conv_y[:, bass.ds(2 * i + u, 1), :].rearrange("p o n -> p (o n)")
                                   ).then_inc(x_hi_done, 1)
            act.wait_ge(o_done, NB)
            for hd in range(HEADS):
                nc.scalar.activation(sub_sq[hd][:, :], oT[:, hd, :], ACT.Square).then_inc(sub_sqd, 1)

            def head_upper(hd):
                act.wait_ge(xt_done, hd + 1)
                nc.scalar.copy(x_hi[:, hd, :], tmp[hd % 2][:, :]).then_inc(x_hi_done, 1)
            for hd in range(HEADS):
                act.wait_ge(sub_mm, hd + 1)
                if hd >= 2:
                    act.wait_ge(sub_r, hd - 1)
                nc.scalar.activation(sig[hd % 2][:, :], bank[hd][:, 0:NTOK], ACT.Sqrt, bias=eps[:, 0:1],
                                     scale=1.0 / P).then_inc(sub_rms, 1)
                if hd:
                    head_upper(hd - 1)
            head_upper(HEADS - 1)
            act.wait_ge(sub_mm, HEADS)
            act.wait_ge(raw_in[0], 16 * (S_OUT // 4) + 16)
            nc.scalar.copy(w_hi[0][:, :, :], raw[0][:, :].rearrange("p (k n) -> p k n", n=P)).then_inc(w_hi_done, 1)
            def out_tile(i, j):
                split_next(S_OUT, i, j)
                act.wait_ge(h_done, KD * 2 + 4 * i + j + 1)
                upper(2, 4 * i + j)
                square(2, 4 * i + j, j % 2)
            act.wait_ge(stored, 16 * 5)
            for n in range(KD):
                out_tile(n // 4, n % 4)
            act.wait_ge(p_in, 16)
            nc.scalar.copy(p_hi[:, :, :], p_raw[:, :, :]).then_inc(p_hi_done, 1)
            ffn(S_FFN2, 44, 3, 0)
            for j in range(2):
                split_next(S_PLE, 0, j)

            def gates(i, first, last):
                s0 = S_PLE + 2 + 4 * i

                def gate(j):
                    act.wait_ge(evacuated, E(s0 + j))
                    nc.scalar.activation(sig[j % 2][:, :], gated[:, :], ACT.Sigmoid).then_inc(sig_done, 1)
                    square(4, 4 * i + j, j % 2)
                for j in range(4):
                    n = j + 3
                    if not (last and j == 3):
                        act.wait_ge(raw_in[n % 4], 16 * (S_PLE // 4 + i + n // 4 + 1))
                        act.wait_ge(slab_done, s0 + j)
                        nc.scalar.copy(w_hi[n % 2][:, :, :], raw[n % 4][:, :].rearrange("p (k n) -> p k n", n=P)
                                       ).then_inc(w_hi_done, 1)
                    if first and j == 1:
                        root(3)
                        gate(0)
                    if not (first and j == 0):
                        gate(j)
            gates(0, True, False)
            with act.Fori(1, 3) as i:
                gates(i, False, False)
            gates(3, False, True)
            root(4)

        @block.vector
        def _(dve):
            vt = nc.vector

            def split_next(base, i4, j):
                n = j + 1
                dve.wait_ge(w_hi_done, base + 4 * i4 + j + 2)
                split(n)

            def split(n):
                vt.tensor_tensor(w_lo[n % 2][:, :, :], raw[n % 4][:, :].rearrange("p (k n) -> p k n", n=P),
                                 w_hi[n % 2][:, :, :].bitcast(F32), ALU.subtract).then_inc(w_lo_done, 1)

            def tile_of(t, n):
                return t[:, bass.ds(n, 1), :].rearrange("p o n -> p (o n)")

            def lower(norm, n):
                hi, lo = X_BUF[norm]
                dve.wait_ge(x_hi_done, X_OF[norm] + n + 1)
                vt.scalar_tensor_tensor(out=tile_of(lo, n), in0=tile_of(h, n),
                                        scalar=vec[:, bass.ds(GAINS[norm] + n, 1)],
                                        in1=tile_of(hi, n).bitcast(F32), op0=ALU.mult, op1=ALU.subtract
                                        ).then_inc(x_done, 1)

            def invert(norm):
                dve.wait_ge(rms_done, norm + 1)
                vt.reciprocal(rinv[:, :], rms[:, :]).then_inc(r_done, 1)
                dve.wait_ge(r_done, norm + 1)

            def ffn_chunk(base, i, f_base, lag=None, norm_in=None, norm=None):
                s0 = base + FFN_SLABS * i

                def evacuate(j):
                    f = j // 2
                    n = f_base + FPC * i + f + 1
                    dve.wait_ge(slab_done, s0 + j + 1)
                    if j % 2 == 0:
                        if not (isinstance(i, int) and i == 0 and f_base == 0 and f == 0):
                            dve.wait_ge(mid_raw, n - 1)
                        vt.tensor_tensor(gated[:, :], bank[j][:, 0:NTOK], rinv[:, :], ALU.mult
                                         ).then_inc(gated_done, 1)
                        dve.wait_ge(gated_done, n + (8 if base else 0))
                        dve.sem_inc(evacuated, 1)
                    else:
                        vt.tensor_tensor(tmp[f % 2][:, :], bank[j][:, 0:NTOK], rinv[:, :], ALU.mult
                                         ).then_inc(evacuated, 1)
                        dve.wait_ge(sig_done, n + (8 if base else 0))
                        vt.tensor_tensor(gated[:, :], gated[:, :], sig[f % 2][:, :], ALU.mult).then_inc(silu_done, 1)
                        dve.wait_ge(evacuated, E(s0 + j))
                        dve.wait_ge(silu_done, n)
                        vt.tensor_tensor(tmp[f % 2][:, :], tmp[f % 2][:, :], gated[:, :], ALU.mult
                                         ).then_inc(mid_raw, 1)
                        dve.wait_ge(mid_raw, n)
                        vt.tensor_copy(mid_hi[:, f, :], tmp[f % 2][:, :]).then_inc(mid_hi_done, 1)
                        dve.wait_ge(mid_hi_done, n)
                        vt.tensor_tensor(mid_lo[:, f, :], tmp[f % 2][:, :], mid_hi[:, f, :].bitcast(F32),
                                         ALU.subtract).then_inc(mid_done, 1)

                for j in range(FFN_SLABS):
                    split_next(base, 3 * i, j)
                    if j < 8:
                        if norm_in is None or j > lag + 1:
                            evacuate(j)
                        elif j == lag + 1:
                            invert(norm_in)
                            for early in range(lag + 2):
                                evacuate(early)
                    else:
                        dve.wait_ge(slab_done, s0 + j + 1)
                        for q in range(4):
                            n = 4 * (j - 8) + q
                            e = vt.scalar_tensor_tensor(out=h[:, n, :], in0=bank[n % 8][:, 0:NTOK], scalar=0.5,
                                                        in1=h[:, n, :], op0=ALU.mult, op1=ALU.add)
                            if norm is not None:
                                e.then_inc(h_done, 1)
                        if norm is None:
                            e.then_inc(evacuated, 1)
                        else:
                            dve.wait_ge(h_done, KD * norm + 4 * (j - 8) + 4)
                            dve.sem_inc(evacuated, 1)
                            for q in range(4):
                                lower(norm, 4 * (j - 8) + q)

            def ffn(base, f_base, norm, lag):
                ffn_chunk(base, 0, f_base, lag=lag, norm_in=norm - 1)
                with dve.Fori(1, CHUNKS - 1) as i:
                    ffn_chunk(base, i, f_base)
                ffn_chunk(base, CHUNKS - 1, f_base, norm=norm)

            for j in range(4):
                for half in range(2):
                    vt.memset(slope_s[32 * j:32 * j + 32, half:half + 1], 2.0 ** -(4 * half + j + 1))
            dve.sem_inc(h_done, KD)
            dve.sem_inc(evacuated, EV0)
            dve.wait_ge(vec_in, 32)
            vt.tensor_tensor(lam_row[0:1, 0:2, :], lam_row[0:1, 0:2, :], lam_row[0:1, 2:4, :], ALU.mult
                             ).then_inc(cchain, 1)
            dve.wait_ge(cchain, 1)
            vt.tensor_reduce(lam_s[0:1, 0:2], lam_row[0:1, 0:2, :], AX.X, ALU.add).then_inc(cchain, 1)
            vt.tensor_scalar(g_sub8[:, :], vec[:, G_SUB:G_SUB + 1], 1.0 - LAM_INIT, None, ALU.mult).then_inc(cchain, 1)
            dve.wait_ge(lam_exp, 1)
            vt.tensor_tensor(lam_s[0:1, 4:5], lam_s[0:1, 3:4], lam_s[0:1, 2:3], ALU.subtract).then_inc(cchain, 1)
            dve.wait_ge(cchain, 4)
            vt.tensor_scalar(lam_s[0:1, 5:6], lam_s[0:1, 4:5], -LAM_INIT, None, ALU.add).then_inc(cchain, 1)
            for n in range(4):
                lower(0, n)
            dve.wait_ge(w_hi_done, 1)
            split(0)
            for n in range(4, KD):
                lower(0, n)
            ffn(S_FFN1, 0, 1, 2)

            def query_tile(i, j):
                dve.wait_ge(slab_done, S_IN + 4 * i + j + 1)
                vt.scalar_tensor_tensor(out=tile_of(qT, 4 * i + j), in0=bank[j][:, 0:NTOK], scalar=QD ** -0.5,
                                        in1=rinv[:, :], op0=ALU.mult, op1=ALU.mult).then_inc(evacuated, 1)
            for i in range(2):
                for j in range(4):
                    split_next(S_IN, i, j)
                    if i == 0 and j == 1:
                        invert(1)
                        query_tile(0, 0)
                    if not (i == 0 and j == 0):
                        query_tile(i, j)
            with dve.Fori(0, 2) as i:
                for j in range(4):
                    split_next(S_IN + 8, i, j)
                    dve.wait_ge(slab_done, S_IN + 8 + 4 * i + j + 1)
                    vt.tensor_tensor(tile_of(kT, 4 * i + j), bank[j][:, 0:NTOK], rinv[:, :], ALU.mult
                                     ).then_inc(evacuated, 1)
            with dve.Fori(0, 2) as i:
                for j in range(4):
                    split_next(S_IN + 16, i, j)
                    dve.wait_ge(slab_done, S_IN + 16 + 4 * i + j + 1)
                    vt.tensor_tensor(v_tmp[j][:, :], bank[j][:, 0:NTOK], rinv[:, :], ALU.mult
                                     ).then_inc(evacuated, 1)

            def conv_in(i, last):
                s0 = S_IN + 24 + 4 * i
                for j in range(4):
                    if not (last and j == 3):
                        split_next(S_IN + 24, i, j)
                    if j % 2:
                        c = 2 * i + j // 2
                        dve.wait_ge(slab_done, s0 + j + 1)
                        if not (isinstance(i, int) and i == 0 and j == 1):
                            dve.wait_ge(u_done, c)
                        vt.tensor_tensor(gated[:, :], bank[j][:, 0:NTOK], rinv[:, :], ALU.mult
                                         ).then_inc(gated_done, 1)
                        vt.tensor_tensor(tmp[0][:, :], bank[j - 1][:, 0:NTOK], rinv[:, :], ALU.mult
                                         ).then_inc(evacuated, 2)
                        dve.wait_ge(evacuated, E(s0 + j))
                        dve.wait_ge(sig_done, 44 + c + 1)
                        vt.tensor_tensor(u_p[:, bass.ds(c, 1), HIST:HIST + SEQ].rearrange("p o n -> p (o n)"),
                                         tmp[0][:, 0:SEQ], sig[j // 2][:, 0:SEQ], ALU.mult)
                        vt.tensor_tensor(u_s[:, bass.ds(c, 1), :, HIST:HIST + TS].rearrange("p o s t -> p (o s) t"),
                                         tmp[0][:, SEQ:NTOK].rearrange("p (s t) -> p s t", t=TS),
                                         sig[j // 2][:, SEQ:NTOK].rearrange("p (s t) -> p s t", t=TS), ALU.mult
                                         ).then_inc(u_done, 1)
            dve.wait_ge(state_in, 16)
            dve.wait_ge(small_in, 16 * N_SMALL)
            conv_in(0, False)
            with dve.Fori(1, 3) as i:
                conv_in(i, False)
            conv_in(3, True)

            def tables():
                dve.wait_ge(attc, 4)
                dve.wait_ge(lam_mm, 1)
                vt.tensor_copy(neglam[:, :], bank[7][:, 0:1]).then_inc(cchain, 1)
                vt.tensor_scalar(trow_i[:, :], trow_i[:, :], 7, None, ALU.bitwise_and).then_inc(cchain, 1)
                dve.wait_ge(cchain, 7)
                vt.tensor_copy(trow[:, :], trow_i[:, :]).then_inc(cchain, 1)
                vt.scalar_tensor_tensor(out=comb[:, :, :], in0=comb1[:, :, :], scalar=neglam[:, :], in1=comb[:, :, :],
                                        op0=ALU.mult, op1=ALU.add)
                dve.wait_ge(cchain, 8)
                vt.tensor_scalar(n_mask[:, :], kpos_n[:, :], trow[:, :], None, ALU.is_le).then_inc(cchain, 1)
                dve.wait_ge(cchain, 9)
                vt.tensor_scalar(n_keep[:, :], n_mask[:, :], -MASKED, MASKED, ALU.mult, ALU.add).then_inc(cchain, 1)
                vt.tensor_tensor(n_mask[:, :], n_mask[:, :], kpos_n[:, :], ALU.mult).then_inc(cchain, 1)
                dve.wait_ge(cchain, 11)
                vt.tensor_tensor(kpos_n[:, :], n_mask[:, :], n_keep[:, :], ALU.add).then_inc(cchain, 1)
                dve.wait_ge(cchain, 12)

            def read_scores(b, grp):
                for half in range(2):
                    idx = 2 * grp + half
                    dve.wait_ge(scored, 10 * b + idx + 1)
                    if idx == 0 and not isinstance(b, int):
                        dve.wait_ge(turned, 10 * b)
                    if grp < 4:
                        out, pos = S[:, half, 512 * grp:512 * grp + 512], kpos[:, 512 * grp:512 * grp + 512]
                        src = K_BANK[half][:, :]
                    else:
                        out, pos = S[:, half, PAST:KCOLS], kpos_n[:, bass.ds(56 - TS * b, NB * TS)]
                        src = K_BANK[half][:, 0:NB * TS]
                    vt.scalar_tensor_tensor(out=out, in0=pos, scalar=slope_s[:, half:half + 1], in1=src,
                                            op0=ALU.mult, op1=ALU.add).then_inc(s_read, 1)

            def maxima(b):
                dve.wait_ge(s_read, 10 * b + 10)
                for half in range(2):
                    vt.tensor_reduce(neg_max[:, half:half + 1], S[:, half, :], AX.X, ALU.max, negate=True
                                     ).then_inc(maxed, 1)

            def prompt_head(b):
                dve.wait_ge(h_scored, b + 1)
                slope = slope_p[:, bass.ds(b, 1)]
                for m, src in enumerate((G_BANK, H_BANK)):
                    vt.scalar_tensor_tensor(out=S_p[:, m, :], in0=kpos_p[:, :], scalar=slope, in1=src[:, 0:3 * P],
                                            op0=ALU.mult, op1=ALU.add).then_inc(hs_done, 1)
                dve.wait_ge(hs_done, 2 * b + 2)
                vt.tensor_reduce(head_max[:, 0, :], S_p[:, :, 0:P], AX.X, ALU.max, negate=True).then_inc(h_maxed, 1)
                vt.tensor_reduce(head_max[:, 1, :], S_p[:, :, P:3 * P], AX.X, ALU.max, negate=True).then_inc(h_maxed, 1)

            def prompt_weights(b):
                dve.wait_ge(h_exped, b + 1)
                vt.reciprocal(head_inv[:, :, :], head_sum[:, :, :]).then_inc(h_chain, 1)
                dve.wait_ge(h_chain, 3 * b + 1)
                vt.tensor_scalar(head_c1[:, :], head_inv[:, :, 1], neglam[:, :], None, ALU.mult).then_inc(h_chain, 1)
                dve.wait_ge(h_chain, 3 * b + 2)
                for i, cols in enumerate((slice(0, P), slice(P, 3 * P))):
                    e = vt.tensor_scalar(w_p[:, cols], S_p[:, 1, cols], head_c1[:, i:i + 1], None, ALU.mult)
                e.then_inc(h_chain, 1)
                dve.wait_ge(h_chain, 3 * b + 3)
                for i, cols in enumerate((slice(0, P), slice(P, 3 * P))):
                    e = vt.scalar_tensor_tensor(out=w_p[:, cols], in0=S_p[:, 0, cols], scalar=head_inv[:, i, 0:1],
                                                in1=w_p[:, cols], op0=ALU.mult, op1=ALU.add)
                e.then_inc(h_w, 1)

            def prompt_out(b):
                dve.wait_ge(h_pv, b + 1)
                vt.tensor_copy(oT[:, bass.ds(b, 1), 0:SEQ].rearrange("p o n -> p (o n)"), H_BANK[:, 0:SEQ]
                               ).then_inc(h_o, 1)

            def taps(b):
                y = y_c[:, 0:SEQ]
                if not isinstance(b, int):
                    dve.wait_ge(ln_done, b)

                def w(k):
                    return wdw[:, bass.ds(b, 1), k:k + 1].rearrange("p o n -> p (o n)")

                def u(k):
                    return u_p[:, bass.ds(b, 1), k:k + SEQ].rearrange("p o n -> p (o n)")
                vt.tensor_scalar(y, u(0), w(0), w(TAPS), ALU.mult, ALU.add).then_inc(tapped, 1)
                for k in range(1, TAPS):
                    dve.wait_ge(tapped, TAPS * b + k)
                    vt.scalar_tensor_tensor(out=y, in0=u(k), scalar=w(k), in1=y, op0=ALU.mult, op1=ALU.add
                                            ).then_inc(tapped, 1)

            def inverse_sums(b):
                dve.wait_ge(exped, 2 * b + 2)
                vt.reciprocal(l_inv[:, bass.ds(2 * b, 2)], l_sum[:, bass.ds(2 * b, 2)]).then_inc(l_done, 1)

            def out_store(b):
                dve.wait_ge(comb_mm, b + 1)
                vt.tensor_copy(oT[:, :, bass.ds(SEQ + TS * b, TS)],
                               O_BANK[0][:, 256:320].rearrange("p (h q) -> p h q", q=TS)).then_inc(o_done, 1)

            def conv_center(b):
                dve.wait_ge(ln_mm, 2 * b + 1)
                vt.scalar_tensor_tensor(out=gated[:, :], in0=G_BANK[:, 0:NTOK], scalar=-1.0 / P, in1=y_c[:, :],
                                        op0=ALU.mult, op1=ALU.add).then_inc(ln_d, 1)

            def conv_scale(b):
                g = vec[:, bass.ds(G_CN + b, 1)]
                beta = vec[:, bass.ds(B_CN + b, 1)]
                dve.wait_ge(ln_rms, b + 1)
                vt.reciprocal(rinv[:, :], rms[:, :]).then_inc(ln_chain, 1)
                dve.wait_ge(ln_chain, 3 * b + 1)
                vt.scalar_tensor_tensor(out=gated[:, :], in0=gated[:, :], scalar=g, in1=rinv[:, :],
                                        op0=ALU.mult, op1=ALU.mult).then_inc(ln_chain, 1)
                dve.wait_ge(ln_chain, 3 * b + 2)
                vt.tensor_scalar(tmp[1][:, :], gated[:, :], beta, None, ALU.add).then_inc(ln_chain, 1)

            def conv_swish(b):
                dve.wait_ge(ln_sig, b + 1)
                vt.tensor_tensor(tile_of(conv_y, b), tmp[1][:, :], sig[0][:, :], ALU.mult).then_inc(ln_done, 1)

            def attention(b):
                first = isinstance(b, int)
                if first:
                    dve.wait_ge(attc, 2)
                read_scores(b, 0)
                if not first:
                    conv_center(b - 1)
                read_scores(b, 1)
                if first:
                    tables()
                else:
                    conv_scale(b - 1)
                read_scores(b, 2)
                if not first:
                    conv_swish(b - 1)
                prompt_head(b)
                read_scores(b, 3)
                read_scores(b, 4)
                maxima(b)
                prompt_weights(b)
                inverse_sums(b)
                taps(b)
                prompt_out(b)
                if not first:
                    out_store(b - 1)

            dve.wait_ge(u_done, 8)
            attention(0)
            with dve.Fori(1, NB) as b:
                attention(b)
            conv_center(NB - 1)
            conv_scale(NB - 1)
            conv_swish(NB - 1)
            out_store(NB - 1)

            with dve.Fori(0, 4) as i:
                for u in range(2):
                    dve.wait_ge(x_hi_done, X_OUT + 2 * i + u + 1)
                    vt.tensor_tensor(tile_of(x_lo, HEADS + 2 * i + u), tile_of(conv_y, 2 * i + u),
                                     tile_of(x_hi, HEADS + 2 * i + u).bitcast(F32), ALU.subtract).then_inc(x_done, 1)

            def head_lower(hd):
                dve.wait_ge(x_hi_done, X_OUT + HEADS + hd + 1)
                vt.tensor_tensor(x_lo[:, hd, :], tmp[hd % 2][:, :], x_hi[:, hd, :].bitcast(F32), ALU.subtract
                                 ).then_inc(x_done, 1)
            dve.wait_ge(o_done, NB)
            dve.wait_ge(h_o, HEADS)
            for hd in range(HEADS):
                dve.wait_ge(sub_rms, hd + 1)
                r = (rinv, gated)[hd % 2]
                vt.reciprocal(r[:, :], sig[hd % 2][:, :]).then_inc(sub_r, 1)
                dve.wait_ge(sub_r, hd + 1)
                vt.scalar_tensor_tensor(out=tmp[hd % 2][:, :], in0=oT[:, hd, :], scalar=g_sub8[:, :], in1=r[:, :],
                                        op0=ALU.mult, op1=ALU.mult).then_inc(xt_done, 1)
                if hd:
                    head_lower(hd - 1)
            head_lower(HEADS - 1)
            dve.wait_ge(w_hi_done, S_OUT + 1)
            split(0)
            def out_tile(i, j):
                n = 4 * i + j
                split_next(S_OUT, i, j)
                dve.wait_ge(slab_done, S_OUT + n + 1)
                vt.scalar_tensor_tensor(out=tile_of(h, n), in0=bank[j][:, 0:NTOK], scalar=1.0, in1=tile_of(h, n),
                                        op0=ALU.mult, op1=ALU.add).then_inc(h_done, 1)
                dve.wait_ge(h_done, KD * 2 + n + 1)
                dve.sem_inc(evacuated, 1)
                lower(2, n)
            dve.wait_ge(stored, 16 * 5)
            with dve.Fori(0, 4) as i:
                for j in range(4):
                    out_tile(i, j)
            dve.wait_ge(p_hi_done, 1)
            vt.tensor_tensor(p_lo[:, :, :], p_raw[:, :, :], p_hi[:, :, :].bitcast(F32), ALU.subtract).then_inc(p_done, 1)
            ffn(S_FFN2, 44, 3, 0)
            for t in range(2):
                split_next(S_PLE, 0, t)
                for q in range(8):
                    if q < 7:
                        dve.wait_ge(proj_mm, 7 * t + q + 1)
                    else:
                        dve.wait_ge(slab_done, S_PLE + t + 1)
                    vt.tensor_copy(proj[:, 8 * t + q, :], bank[q][:, 0:NTOK]).then_inc(proj_read, 1)
                dve.wait_ge(proj_read, 8 * t + 8)
                dve.sem_inc(evacuated, 1)

            def gates(i, first, last):
                s0 = S_PLE + 2 + 4 * i

                def gate(j):
                    n = 4 * i + j
                    dve.wait_ge(slab_done, s0 + j + 1)
                    vt.tensor_tensor(gated[:, :], bank[j][:, 0:NTOK], rinv[:, :], ALU.mult).then_inc(evacuated, 1)
                    dve.wait_ge(sig_done, 44 + 8 + 44 + n + 1)
                    vt.tensor_tensor(sig[j % 2][:, :], tile_of(proj, n), sig[j % 2][:, :], ALU.mult
                                     ).then_inc(silu_done, 1)
                    dve.wait_ge(silu_done, 88 + n + 1)
                    vt.tensor_tensor(tile_of(h, n), tile_of(h, n), sig[j % 2][:, :], ALU.add).then_inc(h_done, 1)
                for j in range(4):
                    if not (last and j == 3):
                        dve.wait_ge(w_hi_done, s0 + j + 2)
                        split(j + 3)
                    if first and j == 1:
                        invert(3)
                        gate(0)
                    if not (first and j == 0):
                        gate(j)
            gates(0, True, False)
            with dve.Fori(1, 3) as i:
                gates(i, False, False)
            gates(3, False, True)
            dve.wait_ge(rms_done, 5)
            vt.reciprocal(rinv[:, :], rms[:, :]).then_inc(r_done, 1)
            dve.wait_ge(r_done, 5)
            for k in range(KD):
                vt.scalar_tensor_tensor(out=proj[:, k, :], in0=h[:, k, :], scalar=vec[:, G_FINAL + k:G_FINAL + k + 1],
                                        in1=rinv[:, :], op0=ALU.mult, op1=ALU.mult).then_inc(y_done, 1)

        @block.tensor
        def _(pe):
            mm = nc.tensor.matmul

            def three(out, w2, t, xh, xl, start, stop):
                mm(out, w_hi[w2][:, t, :], xh, start=start, stop=False)
                mm(out, w_hi[w2][:, t, :], xl, start=False, stop=False)
                return mm(out, w_lo[w2][:, t, :], xh, start=False, stop=stop)

            def dense(s, j, b, order=range(KD), x_base=None, x=(x_hi, x_lo)):
                pe.wait_ge(w_lo_done, s + 1)
                for n, k in enumerate(order):
                    if x_base is not None:
                        pe.wait_ge(x_done, x_base + n + 1)
                    e = three(bank[b][:, 0:NTOK], j % 2, k, x[0][:, k, :], x[1][:, k, :],
                              n == 0, n == len(order) - 1)
                e.then_inc(slab_done, 1)

            def sum_features(norm):
                pe.wait_ge(ssq_done, KD * norm + KD)
                mm(NORM[:, 0:NTOK], ones[:, :], ssq[:, :], start=True, stop=True).then_inc(norm_mm, 1)

            def ffn_chunk(base, i, f_base, norm, lag):
                s0 = base + FFN_SLABS * i
                first = isinstance(i, int)
                for j in range(8):
                    if not first:
                        pe.wait_ge(evacuated, E(s0 - 2) if j < 4 else E(s0 - 1))
                    elif base == S_FFN1:
                        pass
                    elif j < 4:
                        pe.wait_ge(evacuated, E(s0 - 4 + j))
                    if first and j == 7:
                        pe.wait_ge(rms_done, norm + 1)
                    dense(s0 + j, j, j, x_base=X_OF[norm] if first and j == 0 else None, x=X_BUF[norm])
                    if first and j == lag:
                        sum_features(norm)
                for d in range(4):
                    pe.wait_ge(w_lo_done, s0 + 8 + d + 1)
                    pe.wait_ge(evacuated, E(s0 + (3, 7, 8, 9)[d]))
                    for f in range(FPC):
                        if d == 0:
                            pe.wait_ge(mid_done, f_base + FPC * i + f + 1)
                        for q in range(4):
                            e = three(bank[(4 * d + q) % 8][:, 0:NTOK], d % 2, 4 * f + q,
                                      mid_hi[:, f, :], mid_lo[:, f, :], f == 0, f == FPC - 1)
                    e.then_inc(slab_done, 1)

            def ffn(base, f_base, norm, lag):
                ffn_chunk(base, 0, f_base, norm, lag)
                with pe.Fori(1, CHUNKS) as i:
                    ffn_chunk(base, i, f_base, norm, lag)

            pe.wait_ge(consts, 1)
            ffn(S_FFN1, 0, 0, 2)

            for j in range(4):
                pe.wait_ge(evacuated, E(S_IN - 2))
                dense(S_IN + j, j, j, x_base=X_IN if j == 0 else None)
                if j == 0:
                    pe.wait_ge(evacuated, E(S_IN - 1))
                    sum_features(1)
            with pe.Fori(1, 4) as i:
                for j in range(4):
                    pe.wait_ge(evacuated, E(S_IN + 4 * i + j - 4))
                    dense(S_IN + 4 * i + j, j, j)
            pe.wait_ge(consts, 2)
            with pe.Fori(0, 2) as i:
                for j in range(4):
                    pe.wait_ge(evacuated, E(S_IN + 16 + 4 * i + j - 4))
                    dense(S_IN + 16 + 4 * i + j, j, j)
                for j in range(4):
                    pe.wait_ge(evacuated, E(S_IN + 16 + 4 * i + j))
                    pe.wait_ge(vtok_done, 4 * i)
                    for a, t0 in enumerate((0, P, NTOK - P)):
                        e = nc.tensor.transpose(bank[4 + j][:, P * a:P * a + P], v_tmp[j][:, t0:t0 + P], ident[:, :])
                    e.then_inc(v_turned, 1)
            with pe.Fori(0, 4) as i:
                for j in range(4):
                    pe.wait_ge(evacuated, E(S_IN + 24 + 4 * i + (j - 4 if j % 2 else j - 3)))
                    dense(S_IN + 24 + 4 * i + j, j, j)
            pe.wait_ge(vtok_done, HEADS)
            pe.wait_ge(cchain, 5)
            mm(bank[7][:, 0:1], ones[0:1, :], lam_s[0:1, 5:6], start=True, stop=True).then_inc(lam_mm, 1)

            def keys(slot):
                return raw[slot][:, :].rearrange("p (g h k) -> p g h k", g=2, h=HEADS)

            def score(b, grp):
                for half in range(2):
                    idx = 2 * grp + half
                    if not (isinstance(b, int) and idx < 2):
                        pe.wait_ge(s_read, 10 * b + idx - 1)
                    for e2 in range(2):
                        slot = (2 * grp + e2) % RAW
                        if half == 0:
                            pe.wait_ge(kv_in[slot], 32 * kv_round(b, 2 * grp + e2))
                        for j in range(4):
                            e = mm(K_BANK[half][32 * j:32 * j + 32, 256 * e2:256 * e2 + 256],
                                   Qb[:, 4 * half + j, :], keys(slot)[:, :, 4 * half + j, :], start=True, stop=True)
                    e.then_inc(scored, 1)

            def kv_round(b, g):
                return g // 4 + 1 if isinstance(b, int) else 4 * b - 2 + g // 4 + 1

            def score_new(b):
                for half in range(2):
                    pe.wait_ge(s_read, 10 * b + 8 + half - 1)
                    for j in range(4):
                        e = mm(K_BANK[half][32 * j:32 * j + 32, 0:NB * TS], Qb[:, 4 * half + j, :],
                               kT[:, 4 * half + j, SEQ:NTOK], start=True, stop=True)
                    e.then_inc(scored, 1)

            def prompt_scores(b):
                pe.wait_ge(staged, b + 1)
                if isinstance(b, int):
                    pe.wait_ge(cchain, 12)
                else:
                    pe.wait_ge(ln_d, b)
                    pe.wait_ge(ln_rms, b)
                for m, out in enumerate((G_BANK, H_BANK)):
                    rows = slice(QD * m, QD * m + QD)
                    for cols, keys_n, qs in ((0, P, 0), (P, 2 * P, P)):
                        e = mm(out[:, cols:cols + keys_n], q_st[rows, qs:qs + P],
                               k_st[rows, 0:keys_n], start=True, stop=True)
                e.then_inc(h_scored, 1)

            def prompt_turn(b):
                pe.wait_ge(h_w, b + 1)
                for c in range(3):
                    e = nc.tensor.transpose(G_BANK[:, P * c:P * c + P], w_p[:, P * c:P * c + P], ident[:, :])
                e.then_inc(h_turned, 1)

            def prompt_pv(b):
                pe.wait_ge(h_wT, b + 1)
                mm(H_BANK[:, 0:P], v_st[:, 0, :], wT_p[:, 0:P], start=True, stop=True)
                mm(H_BANK[:, P:2 * P], v_st[:, 0, :], wT_p[:, P:2 * P], start=True, stop=False)
                mm(H_BANK[:, P:2 * P], v_st[:, 1, :], wT_p[:, 2 * P:3 * P], start=False, stop=True).then_inc(h_pv, 1)

            def turn(b, group):
                if group == 0:
                    pe.wait_ge(exped, 2 * b + 2)
                for idx in (2 * group, 2 * group + 1):
                    half, g = idx % 2, idx // 2
                    if not (isinstance(b, int) and idx < 2):
                        pe.wait_ge(et_done, 10 * b + idx - 1)
                    if g < 4:
                        for c in range(4):
                            e = nc.tensor.transpose(T_BANK[idx % 2][:, P * c:P * c + P],
                                                    S[:, half, 512 * g + P * c:512 * g + P * c + P], ident[:, :])
                    else:
                        e = nc.tensor.transpose(T_BANK[idx % 2][:, 0:P], S[:, half, KCOLS - P:KCOLS], ident[:, :])
                    e.then_inc(turned, 1)

            def weigh(b, pair):
                if pair == 0:
                    pe.wait_ge(et_done, 10 * b + 10)
                for g in (2 * pair, 2 * pair + 1):
                    slot = g % RAW
                    pe.wait_ge(kv_in[slot], 32 * (4 * b + 4 + g // 4 + 1) if not (isinstance(b, int) and b == NB - 1)
                               else 32 * (2 * KV_SLOTS * NB // RAW - 2 + g // 4 + 1))
                    for half in range(2):
                        for e2 in range(2):
                            for j in range(4):
                                e = mm(O_BANK[half][32 * j:32 * j + 32, 0:P],
                                       ET[:, half, 2 * g + e2, 32 * j:32 * j + 32],
                                       keys(slot)[:, e2, 4 * half + j, :], start=(g == 0 and e2 == 0), stop=False)
                    e.then_inc(v_used, 1)

            def weigh_new(b):
                for half in range(2):
                    for j in range(4):
                        e = mm(O_BANK[half][32 * j:32 * j + 32, 0:P],
                               ET[P - NB * TS:P, half, PAGES, 32 * j:32 * j + 32],
                               vtok[P - NB * TS:P, 2, P * (4 * half + j):P * (4 * half + j) + P], start=False, stop=True)
                e.then_inc(pv_done, 1)

            def combine(b):
                pe.wait_ge(o_read, 2 * b + 2)
                for half in range(2):
                    e = mm(O_BANK[0][:, 256 + 32 * half:288 + 32 * half], O_n[:, half, :],
                           comb[:, :, :].rearrange("p j q -> p (j q)"), start=True, stop=True)
                e.then_inc(comb_mm, 1)

            def conv_mean(b):
                pe.wait_ge(tapped, TAPS * b + TAPS)
                pe.wait_ge(s_tapped, TAPS * b + TAPS)
                pe.wait_ge(h_wT, b + 1)
                mm(G_BANK[:, 0:NTOK], ones[:, :], y_c[:, :], start=True, stop=True).then_inc(ln_mm, 1)

            def conv_var(b):
                pe.wait_ge(ln_sq, b + 1)
                pe.wait_ge(h_o, b + 1)
                mm(H_BANK[:, 0:NTOK], ones[:, :], tmp[0][:, :], start=True, stop=True).then_inc(ln_mm, 1)

            def attention(b):
                pe.wait_ge(qb_ready, 2 * b + 2)
                first = isinstance(b, int)
                if first:
                    pe.wait_ge(evacuated, E(S_OUT - 1))
                score(b, 0)
                if not first:
                    conv_mean(b - 1)
                score(b, 1)
                if not first:
                    conv_var(b - 1)
                score(b, 2)
                prompt_scores(b)
                score(b, 3)
                score_new(b)
                if not first:
                    weigh(b - 1, 0)
                    weigh(b - 1, 1)
                prompt_turn(b)
                turn(b, 0)
                turn(b, 1)
                if not first:
                    weigh(b - 1, 2)
                prompt_pv(b)
                turn(b, 2)
                if not first:
                    weigh(b - 1, 3)
                    weigh_new(b - 1)
                turn(b, 3)
                turn(b, 4)
                if not first:
                    combine(b - 1)

            attention(0)
            with pe.Fori(1, NB) as b:
                attention(b)
            conv_mean(NB - 1)
            conv_var(NB - 1)
            for pair in range(4):
                weigh(NB - 1, pair)
            weigh_new(NB - 1)
            combine(NB - 1)

            for hd in range(HEADS):
                pe.wait_ge(sub_sqd, hd + 1)
                if hd == 0:
                    pe.wait_ge(o_done, NB)
                    pe.wait_ge(ln_done, NB)
                mm(bank[hd][:, 0:NTOK], ones[:, :], sub_sq[hd][:, :], start=True, stop=True).then_inc(sub_mm, 1)

            pe.wait_ge(sub_rms, HEADS)
            order = list(range(HEADS, KD)) + list(range(HEADS))
            with pe.Fori(0, 4) as i:
                for j in range(4):
                    pe.wait_ge(evacuated, E(S_OUT + 4 * i + j - 4))
                    dense(S_OUT + 4 * i + j, j, j, order=order, x_base=X_OUT if j == 0 else None)
            ffn(S_FFN2, 44, 2, 0)
            pe.wait_ge(p_done, 1)
            for t in range(2):
                pe.wait_ge(w_lo_done, S_PLE + t + 1)
                for q in range(8):
                    if t:
                        pe.wait_ge(proj_read, q + 1)
                    elif q % 4 == 0:
                        pe.wait_ge(evacuated, E(S_PLE - 2 + q // 4))
                    for k in range(PLE_K):
                        e = three(bank[q][:, 0:NTOK], t % 2, PLE_K * q + k, p_hi[:, k, :], p_lo[:, k, :],
                                  k == 0, k == PLE_K - 1)
                    if q < 7:
                        e.then_inc(proj_mm, 1)
                e.then_inc(slab_done, 1)
            for j in range(4):
                pe.wait_ge(proj_read, 8 + j + 1)
                dense(S_PLE + 2 + j, j, j, x_base=X_PLE if j == 0 else None)
                if j == 0:
                    pe.wait_ge(proj_read, 16)
                    sum_features(3)
            with pe.Fori(1, 4) as i:
                for j in range(4):
                    s = S_PLE + 2 + 4 * i + j
                    pe.wait_ge(evacuated, E(s - 4))
                    dense(s, j, j)
            sum_features(4)


def blocks(w, rows, cols):
    return w.reshape(rows, P, cols, P).transpose(0, 2, 1, 3)


def as_slab(b):
    return np.ascontiguousarray(np.moveaxis(b, -3, -2)).reshape(*b.shape[:-3], P, SLAB * P)


def ffn_slabs(w_gate, w_up, w_down):
    nf = DFF // P
    out = np.empty((CHUNKS, FFN_SLABS, P, SLAB * P), np.float32)
    for which, w in enumerate((w_gate, w_up)):
        b = as_slab(blocks(w, KD, nf).transpose(1, 0, 2, 3))
        out[:, which:8:2] = b.reshape(CHUNKS, FPC, P, SLAB * P)
    d = blocks(w_down, nf, KD).reshape(CHUNKS, FPC, 4, 4, P, P)
    out[:, 8:] = as_slab(d.transpose(0, 2, 1, 3, 4, 5).reshape(CHUNKS, 4, SLAB, P, P))
    return out.reshape(N_FFN, P, SLAB * P)


def per_tile(v):
    return v.reshape(-1, P).T


def kernel(**inp):
    from concourse import bacc
    from concourse.bass_utils import run_bass_kernel_spmd

    a = {k: np.asarray(v) for k, v in inp.items()}
    ns = NB * TS

    def feature_major(prompt, sample, tiles):
        t = np.concatenate([prompt.reshape(SEQ, -1), sample.reshape(ns, -1)], 0)
        return np.ascontiguousarray(t.T.reshape(tiles, P, NTOK).transpose(1, 0, 2))

    w_in = as_slab(blocks(a["w_in"][0], KD, N_IN).transpose(1, 0, 2, 3))
    conv_order = [24 + 8 * (j % 2) + j // 2 for j in range(16)]
    w_in = np.ascontiguousarray(w_in[list(range(24)) + conv_order])
    w_out = as_slab(blocks(a["w_out"][0], KD, KD).transpose(1, 0, 2, 3))
    gate = as_slab(blocks(a["w_ple_gate"][0], KD, KD).transpose(1, 0, 2, 3))
    proj = as_slab(blocks(a["w_ple_proj"][0], PLE_K, KD).reshape(PLE_K, 2, 8, P, P).transpose(1, 2, 0, 3, 4)
                   .reshape(2, SLAB, P, P))
    k_pool = np.ascontiguousarray(a["cache_k"][0].transpose(0, 3, 2, 1)).reshape(NPOOL, P, HEADS * PAGE)
    v_pool = np.ascontiguousarray(a["cache_v"][0]).reshape(NPOOL, PAGE, HEADS * P)
    state = np.zeros((P, 8, NB, HIST + TS), np.float32)
    state[:, :, :, :HIST] = a["state_conv"][0].reshape(NB, HIST, 8, P).transpose(3, 2, 0, 1)
    vecs = np.concatenate([per_tile(a[n].reshape(-1)) for n in
                           ("g_ffn1", "g_mix", "g_ffn2", "g_ple", "g_final", "g_conv_norm", "b_conv_norm",
                            "g_subln")], 1)
    dw = np.concatenate([a["w_dw"][0].reshape(TAPS, 8, P).transpose(2, 1, 0),
                         a["b_dw"][0].reshape(8, P).T[:, :, None]], 2)
    lams = np.concatenate([a[n].reshape(1, 1, QD) for n in ("lambda_q1", "lambda_q2", "lambda_k1", "lambda_k2")], 1)
    arrays = {
        "x_t": feature_major(a["x_prompt"], a["x_sample"], KD),
        "slabs_ffn1": ffn_slabs(a["w_ffn1_gate"][0], a["w_ffn1_up"][0], a["w_ffn1_down"][0]),
        "slabs_in": w_in, "slabs_out": w_out,
        "slabs_ffn2": ffn_slabs(a["w_ffn2_gate"][0], a["w_ffn2_up"][0], a["w_ffn2_down"][0]),
        "slabs_ple": np.concatenate([proj, gate], 0),
        "k_pool": k_pool, "v_pool": v_pool,
        "pages": a["page_table"].reshape(1, -1),
        "state_ext": state,
        "p_t": feature_major(a["p_prompt"], a["p_sample"], PLE_K),
        "vecs": vecs, "dw": dw, "lams": lams,
    }
    arrays = {k: np.ascontiguousarray(v) for k, v in arrays.items()}
    outs = {"y_t": (P, KD, NTOK), "k_t": (P, HEADS, NTOK), "v_tok": (NTOK, HEADS * P),
            "conv_p": (P, 8, HIST), "conv_s": (P, 8, NB, HIST + TS)}

    nc = bacc.Bacc("TRN2", target_bir_lowering=False, num_devices=1)
    args = {k: nc.dram_tensor(k, v.shape, mybir.dt.from_np(v.dtype), kind="ExternalInput").ap()
            for k, v in arrays.items()}
    args |= {k: nc.dram_tensor(k, s, F32, kind="ExternalOutput").ap() for k, s in outs.items()}
    hymba_step(nc, **args)
    res = run_bass_kernel_spmd(nc, [arrays], core_ids=[0]).results[0]

    y = res["y_t"].transpose(2, 1, 0).reshape(NTOK, D)
    k = res["k_t"].transpose(2, 1, 0).reshape(NTOK, HEADS, P)
    v = res["v_tok"].reshape(NTOK, HEADS, P)
    conv_p = res["conv_p"].transpose(2, 1, 0).reshape(1, 1, HIST, 8 * P)
    conv_s = res["conv_s"][:, :, :, TS:].transpose(2, 3, 1, 0).reshape(1, NB, HIST, 8 * P)
    out = (y[:SEQ].reshape(1, SEQ, D), y[SEQ:].reshape(NB, TS, D),
           k[:SEQ].reshape(1, 1, SEQ, HEADS, P), v[:SEQ].reshape(1, 1, SEQ, HEADS, P), conv_p,
           k[SEQ:].reshape(1, NB, TS, HEADS, P), v[SEQ:].reshape(1, NB, TS, HEADS, P), conv_s)
    return tuple(np.ascontiguousarray(o) for o in out)
```

```python
from contextlib import ExitStack

import numpy as np

import concourse.bass as bass
from concourse import mybir

F32 = mybir.dt.float32
F32R = mybir.dt.float32r
I32 = mybir.dt.int32
ALU = mybir.AluOpType
ACT = mybir.ActivationFunctionType
AX = mybir.AxisListType

P = 128
D = 2048
SEQ = 256
NB = 8
TS = 8
NTOK = SEQ + NB * TS
KD = D // P
DFF = 5632
FPC = 4
CHUNKS = DFF // P // FPC
HEADS = 8
QD = 64
PAGE = 128
PAST = 2048
PAGES = PAST // PAGE
NPOOL = 160
TAPS = 31
HIST = TAPS - 1
TAP_STEPS = TAPS + 1
PLE_K = 2
RMS_EPS = 1e-6
LN_EPS = 1e-5
LAM_INIT = 0.2
MASKED = -1e32

SLAB = 16
RAW = 4
FFN_SLABS = 12
N_FFN = CHUNKS * FFN_SLABS
N_IN = 40
S_FFN1 = 0
S_IN = S_FFN1 + N_FFN
S_OUT = S_IN + N_IN
S_FFN2 = S_OUT + KD
S_PLE = S_FFN2 + N_FFN
N_PLE = 2 + KD
SLABS_ALL = S_PLE + N_PLE

POOL_TILES = 4
KV_SLOTS = PAGES // 2
KCOLS = PAST + NB * TS
EV0 = 4

G_FFN1, G_MIX, G_FFN2, G_PLE, G_FINAL = (KD * i for i in range(5))
G_CN = KD * 5
B_CN = G_CN + 8
G_SUB = B_CN + 8
N_VEC = G_SUB + 1


def hymba_step(nc, x_t, slabs_ffn1, slabs_in, slabs_out, slabs_ffn2, slabs_ple, k_pool, v_pool, pages,
               state_ext, p_t, vecs, dw, lams, y_t, k_t, v_tok, conv_p, conv_s):
    ctx = ExitStack()
    with ctx:
        arena_bytes = nc.sbuf_bytes_remaining - 64
        start = nc.sbuf_base
        arena_bytes -= arena_bytes % 64
        ctx.enter_context(nc.sbuf_tensor("arena", [P, arena_bytes // 4], F32))
        start = (start + 31) // 32 * 32
        at = [start]

        def place(name, shape, dt=F32, offset=None):
            size = int(np.prod(shape[1:])) * 4
            size = (size + 31) // 32 * 32
            if offset is None:
                offset = at[0]
                at[0] += size
            assert offset + size <= start + arena_bytes, (name, offset + size - start, arena_bytes)
            return nc.alloc_sbuf_tensor_at(name, shape, dt, offset=offset)

        h = place("h", [P, KD, NTOK])
        x_at = at[0]
        x_hi = place("x_hi", [P, KD, NTOK], F32R)
        x_lo = place("x_lo", [P, KD, NTOK], F32R)
        raw = [place(f"raw{i}", [P, SLAB * P]) for i in range(RAW)]
        w_at = at[0]
        w_hi = [place(f"w_hi{i}", [P, SLAB, P], F32R) for i in range(2)]
        w_lo = [place(f"w_lo{i}", [P, SLAB, P], F32R) for i in range(2)]
        mid_at = at[0]
        mid_hi = place("mid_hi", [P, FPC, NTOK], F32R)
        mid_lo = place("mid_lo", [P, FPC, NTOK], F32R)
        qk_at = at[0]
        qT = place("qT", [P, HEADS, NTOK])
        kT = place("kT", [P, HEADS, NTOK])
        v_at = at[0]
        vtok = place("vtok", [P, 3, HEADS * P])
        u_p = place("u_p", [P, 8, HIST + SEQ])
        u_s = place("u_s", [P, 8, NB, HIST + TS])
        oT = place("oT", [P, HEADS, NTOK])
        sig = [place(f"sig{i}", [P, NTOK]) for i in range(2)]
        tmp = [place(f"tmp{i}", [P, NTOK]) for i in range(2)]
        gated = place("gated", [P, NTOK])
        ssq = place("ssq", [P, NTOK])
        rms = ssq
        rinv = place("rinv", [P, NTOK])
        ident = place("ident", [P, P])
        ones = place("ones", [P, P])
        vec = place("vec", [P, N_VEC])
        wdw = place("wdw", [P, 8, TAPS + 1])
        eps = place("eps", [P, 2])
        slope_s = place("slope_s", [P, 2])
        slope_p = place("slope_p", [P, HEADS])
        lam_row = place("lam_row", [1, 4, QD], offset=mid_at)
        lam_s = place("lam_s", [1, 8])
        neglam = place("neglam", [P, 1])
        g_sub8 = place("g_sub8", [P, 1])
        page_row = place("page_row", [1, NB * PAGES], I32)
        l_sum = place("l_sum", [P, 2 * NB])
        l_inv = place("l_inv", [P, 2 * NB])
        neg_max = place("neg_max", [P, 2])
        head_max = place("head_max", [P, 2, 2])
        head_sum = place("head_sum", [P, 2, 2])
        head_inv = place("head_inv", [P, 2, 2])
        head_c1 = place("head_c1", [P, 2])
        conv_y = place("conv_y", [P, 8, NTOK], offset=mid_at)
        x2_hi = place("x2_hi", [P, KD, NTOK], F32R, offset=qk_at)
        x2_lo = place("x2_lo", [P, KD, NTOK], F32R, offset=v_at)
        v_tmp = [place(f"v_tmp{i}", [P, NTOK], offset=mid_at + 4 * NTOK * i) for i in range(4)]
        S = place("S", [P, 2, KCOLS], offset=x_at)
        ET = place("ET", [P, 2, PAGES + 1, P], offset=x_at + 2 * KCOLS * 4)
        def in_w(name, shape, dt=F32):
            t = place(name, shape, dt, offset=w_cur[0])
            w_cur[0] += (int(np.prod(shape[1:])) * 4 + 31) // 32 * 32
            assert w_cur[0] <= w_end
            return t

        w_part = 4 * SLAB * P
        w_cur, w_end = [w_at], w_at + w_part
        kpos = in_w("kpos", [P, PAST])
        w_cur, w_end = [w_at + 2 * w_part], w_at + 3 * w_part
        q_st = in_w("q_st", [P, SEQ])
        k_st = in_w("k_st", [P, SEQ])
        v_st = in_w("v_st", [P, 2, P])
        w_p = in_w("w_p", [P, 3 * P])
        wT_p = in_w("wT_p", [P, 3 * P])
        Qb = in_w("Qb", [P, HEADS, 32])
        n_mask = in_w("n_mask", [P, 120])
        w_cur, w_end = [w_at + w_part], w_at + 2 * w_part
        kpos_p = in_w("kpos_p", [P, 3 * P])
        kpos_n = in_w("kpos_n", [P, 120])
        n_keep = in_w("n_keep", [P, 120])
        trow_i = in_w("trow_i", [P, 1], I32)
        trow = in_w("trow", [P, 1])
        comb = in_w("comb", [P, 4, TS])
        comb1 = in_w("comb1", [P, 4, TS])
        S_p = in_w("S_p", [P, 2, 3 * P])
        O_n = in_w("O_n", [P, 2, P])
        w_cur, w_end = [w_at + 3 * w_part], w_at + 4 * w_part
        y_c = in_w("y_c", [P, NTOK])
        y_odd = in_w("y_odd", [P, SEQ])
        u_st = in_w("u_st", [P, NB, HIST + TS])
        wdw_st = in_w("wdw_st", [P, TAPS + 1])
        tap_s = [in_w(f"tap_s{i}", [P, NB, TS]) for i in range(2)]
        s_norm = [in_w(f"s_norm{i}", [P, HEADS, n]) for i, n in enumerate((NTOK - SEQ - TS, TS))]
        proj = place("proj", [P, KD, NTOK], offset=qk_at)
        h_g = place("h_g", [P, POOL_TILES, NTOK], offset=v_at)
        p_at = v_at + 4 * KD * NTOK
        p_raw = place("p_raw", [P, PLE_K, NTOK], offset=p_at)
        p_hi = place("p_hi", [P, PLE_K, NTOK], F32R, offset=p_at + 4 * PLE_K * NTOK)
        p_lo = place("p_lo", [P, PLE_K, NTOK], F32R, offset=p_at + 8 * PLE_K * NTOK)

        bank = [ctx.enter_context(nc.psum_tensor(f"bank{i}", [P, 512], F32)) for i in range(8)]
        NORM = bank[7]
        K_BANK, T_BANK, O_BANK = bank[0:2], bank[2:4], bank[4:6]
        G_BANK, H_BANK = bank[6], bank[7]

        def sem(name):
            return ctx.enter_context(nc.semaphore(name))

        x_in = [sem(f"x_in{c}") for c in range(4)]
        vec_in = sem("vec_in")
        small_in = sem("small_in")
        state_in = sem("state_in")
        p_in = sem("p_in")
        raw_in = [sem(f"raw_in{i}") for i in range(RAW)]
        kv_in = [sem(f"kv_in{i}") for i in range(RAW)]
        stored = sem("stored")
        conv_stored = sem("conv_stored")
        y_stored = sem("y_stored")
        w_hi_done = sem("w_hi_done")
        w_lo_done = sem("w_lo_done")
        half_hi = sem("half_hi")
        half_lo = sem("half_lo")
        slab_done = sem("slab_done")
        evacuated = sem("evacuated")
        sig_done = sem("sig_done")
        gated_done = sem("gated_done")
        silu_done = sem("silu_done")
        mid_raw = sem("mid_raw")
        u_done = sem("u_done")
        proj_mm = sem("proj_mm")
        proj_read = sem("proj_read")
        mid_hi_done = sem("mid_hi_done")
        mid_done = sem("mid_done")
        h_done = sem("h_done")
        sq_done = sem("sq_done")
        ssq_done = sem("ssq_done")
        norm_mm = sem("norm_mm")
        rms_done = sem("rms_done")
        r_done = sem("r_done")
        x_hi_done = sem("x_hi_done")
        x_done = sem("x_done")
        consts = sem("consts")
        attc = sem("attc")
        cchain = sem("cchain")
        lam_exp = sem("lam_exp")
        lam_mm = sem("lam_mm")
        v_turned = sem("v_turned")
        vtok_done = sem("vtok_done")
        v_used = sem("v_used")
        qb_ready = sem("qb_ready")
        scored = sem("scored")
        s_read = sem("s_read")
        maxed = sem("maxed")
        exped = sem("exped")
        l_done = sem("l_done")
        turned = sem("turned")
        et_done = sem("et_done")
        pv_done = sem("pv_done")
        o_read = sem("o_read")
        comb_mm = sem("comb_mm")
        o_done = sem("o_done")
        staged = sem("staged")
        h_scored = sem("h_scored")
        hs_done = sem("hs_done")
        h_maxed = sem("h_maxed")
        h_exped = sem("h_exped")
        h_chain = sem("h_chain")
        h_w = sem("h_w")
        h_turned = sem("h_turned")
        h_wT = sem("h_wT")
        h_pv = sem("h_pv")
        h_o = sem("h_o")
        tapped = sem("tapped")
        s_mult = sem("s_mult")
        s_tapped = sem("s_tapped")
        ln_mm = sem("ln_mm")
        ln_d = sem("ln_d")
        ln_sq = sem("ln_sq")
        ln_rms = sem("ln_rms")
        ln_chain = sem("ln_chain")
        ln_sig = sem("ln_sig")
        ln_done = sem("ln_done")
        sub_sqd = sem("sub_sqd")
        sub_mm = sem("sub_mm")
        sub_rms = sem("sub_rms")
        sub_r = sem("sub_r")
        sub_done = sem("sub_done")
        s_sqd = sem("s_sqd")
        s_mm = sem("s_mm")
        s_rms = sem("s_rms")
        s_r = sem("s_r")
        s_done = sem("s_done")
        p_hi_done = sem("p_hi_done")
        p_done = sem("p_done")
        y_done = sem("y_done")
        y_pool = sem("y_pool")
        hg_done = sem("hg_done")

        N_SMALL = 2

        def E(s):
            return s + 1 + EV0

        X_FFN1, X_IN, X_OUT, X_FFN2, X_PLE = (KD * i for i in range(5))
        X_OF = {0: X_FFN1, 1: X_IN, 2: X_FFN2, 3: X_PLE}
        GAINS = {0: G_FFN1, 1: G_MIX, 2: G_FFN2, 3: G_PLE}
        X_BUF = {0: (x_hi, x_lo), 1: (x_hi, x_lo), 2: (x2_hi, x2_lo), 3: (x_hi, x_lo)}

        OUT_ORDER = [11, 12, 13, 14, 15, 8, 9, 10] + list(range(HEADS))
        S_PARTS = ((SEQ, NTOK - TS), (NTOK - TS, NTOK))

        block = ctx.enter_context(nc.Block())

        @block.sync
        def _(sp):
            def slab(src, idx, s, slot, wait):
                if wait == "split":
                    sp.wait_ge(w_lo_done, s - RAW + 1)
                sp.dma_start(raw[slot][:, :], src[idx, :, :]).then_inc(raw_in[slot], 16)

            sp.dma_start(vec[:, :], vecs).then_inc(vec_in, 16)
            sp.dma_start(lam_row[0:1, :, :], lams).then_inc(vec_in, 16)
            for t in range(4):
                sp.dma_start(h[:, 4 * t:4 * t + 4, :], x_t[:, 4 * t:4 * t + 4, :]).then_inc(x_in[t], 16)
                if t == 0:
                    slab(slabs_ffn1, 0, 0, 0, None)
            for j in range(1, RAW):
                slab(slabs_ffn1, j, j, j, None)
            with sp.Fori(1, N_FFN // RAW) as i:
                for j in range(RAW):
                    slab(slabs_ffn1, 4 * i + j, S_FFN1 + 4 * i + j, j, "split")
            with sp.Fori(0, N_IN // RAW) as i:
                for j in range(RAW):
                    slab(slabs_in, 4 * i + j, S_IN + 4 * i + j, j, "split")

            sp.wait_ge(small_in, 16 * N_SMALL)

            def two_pages(pool, b, g, slot):
                for e in range(2):
                    page = sp.value_load(page_row[0:1, bass.ds(PAGES * b + 2 * g + e, 1)],
                                         min_val=0, max_val=NPOOL - 1)
                    sp.dma_start(raw[slot][:, 1024 * e:1024 * e + 1024],
                                 pool[bass.ds(page, 1), :, :].rearrange("o p n -> (o p) n")
                                 ).then_inc(kv_in[slot], 16)

            def keys_used(b, g):
                sp.wait_ge(scored, 10 * b + 2 * (g // 2) + 2)

            def values_used(b, g):
                sp.wait_ge(v_used, KV_SLOTS * b + g + 1)

            def load_keys(b, before):
                for g in range(KV_SLOTS):
                    if g < RAW:
                        before(g + RAW)
                    else:
                        keys_used(b, g - RAW)
                    two_pages(k_pool, b, g, g % RAW)

            def load_values(b, before):
                for g in range(KV_SLOTS):
                    if g < RAW:
                        before(g + RAW)
                    else:
                        values_used(b, g - RAW)
                    two_pages(v_pool, b, g, g % RAW)

            load_keys(0, lambda g: sp.wait_ge(w_lo_done, S_OUT - KV_SLOTS + 1 + g))
            load_keys(1, lambda g: keys_used(0, g))
            load_values(0, lambda g: keys_used(1, g))
            with sp.Fori(2, NB) as b:
                load_keys(b, lambda g: values_used(b - 2, g))
                load_values(b - 1, lambda g: keys_used(b, g))
            load_values(NB - 1, lambda g: values_used(NB - 2, g))

            for j in range(RAW):
                values_used(NB - 1, j + RAW)
                slab(slabs_out, j, S_OUT + j, j, None)
            with sp.Fori(1, KD // RAW) as i:
                for j in range(RAW):
                    slab(slabs_out, 4 * i + j, S_OUT + 4 * i + j, j, "split")
            with sp.Fori(0, N_FFN // RAW) as i:
                for j in range(RAW):
                    slab(slabs_ffn2, 4 * i + j, S_FFN2 + 4 * i + j, j, "split")
            with sp.Fori(0, N_PLE // RAW) as i:
                for j in range(RAW):
                    slab(slabs_ple, 4 * i + j, S_PLE + 4 * i + j, j, "split")
            for j in range(N_PLE % RAW):
                s = N_PLE // RAW * RAW + j
                slab(slabs_ple, s, S_PLE + s, j, "split")
            for c in (1, 0, 2, 3):
                if c == 0:
                    sp.wait_ge(y_pool, POOL_TILES)
                else:
                    sp.wait_ge(y_done, 4 * c + 4 - POOL_TILES)
                sp.dma_start(y_t[:, 4 * c:4 * c + 4, :], proj[:, 4 * c:4 * c + 4, :]).then_inc(y_stored, 16)
            sp.wait_ge(stored, 16 * 3)
            sp.wait_ge(conv_stored, 16 * 2)
            sp.wait_ge(y_stored, 16 * 4)

        @block.gpsimd
        def _(pool):
            for dst, src in ((page_row[:, :], pages), (wdw[:, :, :], dw)):
                pool.dma_start(dst, src).then_inc(small_in, 16)
            nc.gpsimd.memset(ones[:, :], 1.0)
            nc.gpsimd.memset(ident[:, :], 0.0)
            nc.gpsimd.memset(eps[:, 0:1], RMS_EPS)
            nc.gpsimd.memset(eps[:, 1:2], LN_EPS)
            nc.gpsimd.memset(u_p[:, :, 0:HIST], 0.0)
            for hd in range(HEADS):
                last = nc.gpsimd.memset(slope_p[:, hd:hd + 1], 2.0 ** -(hd + 1))
            last.then_inc(consts, 1)
            pool.wait_ge(consts, 1)
            nc.gpsimd.affine_select(out=ident[:, :], in_=ident[:, :], compare_op=ALU.not_equal, fill=1.0,
                                    base=0, pattern=[[-1, P]], channel_multiplier=1).then_inc(consts, 1)

            def sum_squares(norm, last=True):
                def add(n, u):
                    pool.wait_ge(sq_done, KD * norm + n + 1)
                    pool.wait_ge(ssq_done, KD * norm + n)
                    nc.gpsimd.tensor_tensor(ssq[:, :], ssq[:, :], tmp[u][:, :], ALU.add).then_inc(ssq_done, 1)
                pool.wait_ge(sq_done, KD * norm + 1)
                nc.gpsimd.tensor_copy(ssq[:, :], tmp[0][:, :]).then_inc(ssq_done, 1)
                add(1, 1)
                with pool.Fori(1, KD // 2 - 1) as kk:
                    for u in range(2):
                        add(2 * kk + u, u)
                add(KD - 2, 0)
                if last:
                    add(KD - 1, 1)

            sum_squares(0)
            pool.dma_start(u_s[:, :, :, :], state_ext).then_inc(state_in, 16)
            sum_squares(1)

            def queries(b):
                if not isinstance(b, int):
                    pool.wait_ge(scored, 10 * b)
                col = SEQ + TS * b
                nc.gpsimd.tensor_copy(Qb[0:QD, :, 0:TS], qT[0:QD, :, bass.ds(col, TS)]).then_inc(qb_ready, 1)
                pool.wait_ge(qb_ready, 2 * b + 1)
                nc.gpsimd.tensor_copy(Qb[QD:P, :, TS:2 * TS], qT[QD:P, :, bass.ds(col, TS)]).then_inc(qb_ready, 1)
                pool.wait_ge(qb_ready, 2 * b + 2)

            def stage(b):
                if not isinstance(b, int):
                    pool.wait_ge(h_pv, b)
                nc.gpsimd.tensor_copy(q_st[:, :], qT[:, bass.ds(b, 1), 0:SEQ].rearrange("p o n -> p (o n)"))
                nc.gpsimd.tensor_copy(k_st[:, :], kT[:, bass.ds(b, 1), 0:SEQ].rearrange("p o n -> p (o n)"))
                nc.gpsimd.tensor_copy(v_st[:, :, :], vtok[:, 0:2, bass.ds(P * b, P)]).then_inc(staged, 1)

            pool.wait_ge(evacuated, E(S_IN + 15))
            pool.dma_start(k_t, kT[:, :, :]).then_inc(stored, 16)
            pool.wait_ge(vtok_done, HEADS)
            pool.dma_start(v_tok[0:SEQ, :].rearrange("(a p) n -> p a n", p=P), vtok[:, 0:2, :]).then_inc(stored, 16)
            pool.dma_start(v_tok[SEQ:NTOK, :], vtok[P - NB * TS:P, 2, :]).then_inc(stored, 16)

            pool.wait_ge(slab_done, S_OUT - 1)
            nc.gpsimd.memset(Qb[:, :, :], 0.0).then_inc(attc, 1)
            pool.wait_ge(attc, 1)
            queries(0)
            nc.gpsimd.iota(kpos[:, :], [[1, PAST]], base=-PAST, channel_multiplier=0,
                           allow_small_or_imprecise_dtypes=True).then_inc(attc, 1)
            stage(0)
            pool.wait_ge(slab_done, S_OUT)
            nc.gpsimd.memset(comb[:, :, :], 0.0)
            nc.gpsimd.memset(comb1[:, :, :], 0.0)
            nc.gpsimd.iota(kpos_p[:, 0:P], [[1, P]], base=0, channel_multiplier=-1,
                           allow_small_or_imprecise_dtypes=True)
            nc.gpsimd.iota(kpos_p[:, P:3 * P], [[1, 2 * P]], base=-P, channel_multiplier=-1,
                           allow_small_or_imprecise_dtypes=True)
            nc.gpsimd.iota(kpos_n[:, :], [[1, 120]], base=-56, channel_multiplier=0,
                           allow_small_or_imprecise_dtypes=True)
            nc.gpsimd.iota(trow_i[:, :], [[0, 1]], base=0, channel_multiplier=1).then_inc(attc, 1)
            pool.wait_ge(attc, 3)
            nc.gpsimd.affine_select(out=kpos_p[:, 0:P], in_=kpos_p[:, 0:P], compare_op=ALU.is_ge,
                                    fill=MASKED, base=0, pattern=[[-1, P]], channel_multiplier=1)
            nc.gpsimd.affine_select(out=kpos_p[:, P:3 * P], in_=kpos_p[:, P:3 * P], compare_op=ALU.is_ge,
                                    fill=MASKED, base=P, pattern=[[-1, 2 * P]], channel_multiplier=1)
            nc.gpsimd.affine_select(out=kpos_n[:, :], in_=kpos_n[:, :], compare_op=ALU.is_ge,
                                    fill=1000.0, base=-56, pattern=[[1, 120]], channel_multiplier=0)
            nc.gpsimd.affine_select(out=comb[:, :, :], in_=comb[:, :, :], compare_op=ALU.not_equal,
                                    fill=1.0, base=0, pattern=[[-32, 4], [-1, TS]], channel_multiplier=1)
            nc.gpsimd.affine_select(out=comb1[:, :, :], in_=comb1[:, :, :], compare_op=ALU.not_equal,
                                    fill=1.0, base=-TS, pattern=[[-32, 4], [-1, TS]],
                                    channel_multiplier=1).then_inc(attc, 1)
            def iteration(b):
                first = isinstance(b, int)
                if not first:
                    queries(b)
                    stage(b)
                if not first:
                    pool.wait_ge(ln_d, b)
                    pool.wait_ge(s_tapped, TAPS * b)
                nc.gpsimd.tensor_copy(u_st[:, :, :], u_s[:, bass.ds(b, 1), :, :].rearrange("p o s t -> p (o s) t"))
                nc.gpsimd.tensor_copy(wdw_st[:, :], wdw[:, bass.ds(b, 1), :].rearrange("p o n -> p (o n)")
                                      ).then_inc(s_mult, 1)
                ys = y_c[:, SEQ:NTOK].rearrange("p (s t) -> p s t", t=TS)

                def spread(c):
                    return wdw_st[:, c:c + 1].unsqueeze(2).to_broadcast([P, NB, TS])
                pool.wait_ge(s_mult, (TAPS + 1) * b + 1)
                nc.gpsimd.tensor_tensor(tap_s[0][:, :, :], u_st[:, :, 0:TS], spread(0), ALU.mult).then_inc(s_mult, 1)
                pool.wait_ge(s_mult, (TAPS + 1) * b + 2)
                nc.gpsimd.tensor_tensor(ys, tap_s[0][:, :, :], spread(TAPS), ALU.add).then_inc(s_tapped, 1)
                for k in range(1, TAPS):
                    nc.gpsimd.tensor_scalar(tap_s[k % 2][:, :, :], u_st[:, :, k:k + TS], wdw_st[:, k:k + 1], None,
                                            ALU.mult).then_inc(s_mult, 1)
                    pool.wait_ge(s_mult, (TAPS + 1) * b + 2 + k)
                    pool.wait_ge(s_tapped, TAPS * b + k)
                    nc.gpsimd.tensor_tensor(ys, ys, tap_s[k % 2][:, :, :], ALU.add).then_inc(s_tapped, 1)

            iteration(0)
            with pool.Fori(1, NB) as b:
                iteration(b)
            pool.wait_ge(u_done, 8)
            pool.wait_ge(v_used, KV_SLOTS * NB - 3)
            pool.dma_start(conv_p, u_p[:, :, SEQ:SEQ + HIST]).then_inc(conv_stored, 16)
            pool.dma_start(conv_s, u_s[:, :, :, :]).then_inc(conv_stored, 16)
            pool.wait_ge(conv_stored, 16 * 2)
            pool.dma_start(p_raw[:, :, :], p_t).then_inc(p_in, 16)
            for norm in (2, 3):
                sum_squares(norm)
            sum_squares(4, last=False)
            pool.wait_ge(hg_done, POOL_TILES)
            pool.wait_ge(r_done, 5)
            for k in range(POOL_TILES):
                nc.gpsimd.tensor_tensor(proj[:, k, :], h_g[:, k, :], rinv[:, :], ALU.mult).then_inc(y_pool, 1)

        @block.scalar
        def _(act):
            def split_halves(s, first):
                act.wait_ge(raw_in[0], 16 * (s // RAW) + 16)
                src = raw[0][:, :].rearrange("p (k n) -> p k n", n=P)
                nc.scalar.copy(w_hi[0][:, first:first + 8, :], src[:, first:first + 8, :]).then_inc(half_hi, 1)
                nc.scalar.copy(w_hi[0][:, 8 - first:16 - first, :], src[:, 8 - first:16 - first, :]
                               ).then_inc(w_hi_done, 1)

            def split_next(base, i4, j):
                n = j + 1
                act.wait_ge(raw_in[n % 4], 16 * (base // 4 + i4 + n // 4 + 1))
                act.wait_ge(slab_done, base + 4 * i4 + j)
                nc.scalar.copy(w_hi[n % 2][:, :, :], raw[n % 4][:, :].rearrange("p (k n) -> p k n", n=P)
                               ).then_inc(w_hi_done, 1)

            def square(norm, n, buf):
                act.wait_ge(h_done, KD * norm + n + 1)
                if norm or n >= 2:
                    act.wait_ge(ssq_done, KD * norm + n - 1)
                nc.scalar.activation(tmp[buf][:, :], h[:, bass.ds(n, 1), :].rearrange("p o n -> p (o n)"),
                                     ACT.Square).then_inc(sq_done, 1)

            def root(norm):
                act.wait_ge(norm_mm, norm + 1)
                nc.scalar.activation(rms[:, :], NORM[:, 0:NTOK], ACT.Sqrt, bias=eps[:, 0:1],
                                     scale=1.0 / D).then_inc(rms_done, 1)

            def upper(norm, n):
                nc.scalar.activation(X_BUF[norm][0][:, bass.ds(n, 1), :].rearrange("p o n -> p (o n)"),
                                     h[:, bass.ds(n, 1), :].rearrange("p o n -> p (o n)"), ACT.Copy,
                                     scale=vec[:, bass.ds(GAINS[norm] + n, 1)]).then_inc(x_hi_done, 1)

            def squares(norm, d):
                for q in range(4):
                    square(norm, 4 * d + q, q % 2)

            def ffn_chunk(base, i, f_base, lag=None, norm_in=None, norm=None):
                s0 = base + FFN_SLABS * i

                def sigmoid(j):
                    if j < 8 and j % 2 == 0:
                        f = j // 2
                        act.wait_ge(gated_done, f_base + FPC * i + f + 1 + (8 if base else 0))
                        nc.scalar.activation(sig[f % 2][:, :], gated[:, :], ACT.Sigmoid).then_inc(sig_done, 1)

                for j in range(FFN_SLABS):
                    split_next(base, 3 * i, j)
                    if j >= 9 and norm is not None:
                        squares(norm, j - 9)
                    if norm_in == 0 and j < 2:
                        for n in range(8 * j, 8 * j + 8):
                            square(0, n, n % 2)
                    if norm_in is None or j > lag + 1:
                        sigmoid(j)
                    elif j == lag + 1:
                        root(norm_in)
                        for early in range(lag + 2):
                            sigmoid(early)
                    if j >= 8 and norm is not None:
                        for q in range(4):
                            n = 4 * (j - 8) + q
                            act.wait_ge(h_done, KD * norm + n + 1)
                            upper(norm, n)

            def ffn(base, f_base, norm, lag):
                ffn_chunk(base, 0, f_base, lag=lag, norm_in=norm - 1)
                with act.Fori(1, CHUNKS - 1) as i:
                    ffn_chunk(base, i, f_base)
                ffn_chunk(base, CHUNKS - 1, f_base, norm=norm)

            act.wait_ge(cchain, 2)
            nc.scalar.activation(lam_s[0:1, 2:4], lam_s[0:1, 0:2], ACT.Exp).then_inc(lam_exp, 1)
            act.wait_ge(vec_in, 32)
            for n in range(KD):
                act.wait_ge(x_in[n // 4], 16)
                upper(0, n)
                if n == 3:
                    split_halves(0, 0)
            ffn(S_FFN1, 0, 1, 2)

            for j in range(4):
                split_next(S_IN, 0, j)
                if j == 0:
                    squares(1, 3)
                if j == 2:
                    root(1)
            with act.Fori(1, 4) as i:
                for j in range(4):
                    split_next(S_IN, i, j)
            with act.Fori(0, 2) as i:
                for j in range(4):
                    split_next(S_IN + 16, i, j)
                for j in range(4):
                    act.wait_ge(v_turned, 4 * i + j + 1)
                    nc.scalar.copy(vtok[:, :, bass.ds(P * (4 * i + j), P)],
                                   bank[4 + j][:, 0:3 * P].rearrange("p (a n) -> p a n", n=P)).then_inc(vtok_done, 1)

            def conv_in(i, last):
                for j in range(4):
                    if not (last and j == 3):
                        split_next(S_IN + 24, i, j)
                    if j % 2:
                        act.wait_ge(gated_done, 44 + 2 * i + j // 2 + 1)
                        nc.scalar.activation(sig[j // 2][:, :], gated[:, :], ACT.Sigmoid).then_inc(sig_done, 1)
            with act.Fori(0, 3) as i:
                conv_in(i, False)
            conv_in(3, True)

            def exp_scores(b):
                for half in range(2):
                    act.wait_ge(maxed, 2 * b + half + 1)
                    nc.scalar.activation(S[:, half, :], S[:, half, :], ACT.Exp, bias=neg_max[:, half:half + 1],
                                         accum_out=l_sum[:, bass.ds(2 * b + half, 1)]).then_inc(exped, 1)

            def prompt_head(b):
                act.wait_ge(h_maxed, 2 * b + 2)
                for m in range(2):
                    nc.scalar.activation(S_p[:, m, 0:P], S_p[:, m, 0:P], ACT.Exp,
                                         bias=head_max[:, 0, m:m + 1], accum_out=head_sum[:, 0, m:m + 1])
                for m in range(2):
                    e = nc.scalar.activation(S_p[:, m, P:3 * P], S_p[:, m, P:3 * P], ACT.Exp,
                                             bias=head_max[:, 1, m:m + 1], accum_out=head_sum[:, 1, m:m + 1])
                e.then_inc(h_exped, 1)

            def prompt_copy(b):
                act.wait_ge(h_turned, b + 1)
                nc.scalar.copy(wT_p[:, :], G_BANK[:, 0:3 * P]).then_inc(h_wT, 1)

            def out_read(b):
                act.wait_ge(pv_done, b + 1)
                act.wait_ge(l_done, b + 1)
                for half in range(2):
                    nc.scalar.activation(O_n[:, half, :], O_BANK[half][:, 0:P], ACT.Copy,
                                         scale=l_inv[:, bass.ds(2 * b + half, 1)]).then_inc(o_read, 1)

            def copy_ET(b):
                for idx in range(10):
                    half, g = idx % 2, idx // 2
                    act.wait_ge(turned, 10 * b + idx + 1)
                    if g < 4:
                        e = nc.scalar.copy(ET[:, half, 4 * g:4 * g + 4, :],
                                           T_BANK[idx % 2][:, :].rearrange("p (a n) -> p a n", n=P))
                    else:
                        e = nc.scalar.copy(ET[P - NB * TS:P, half, PAGES, :], T_BANK[idx % 2][P - NB * TS:P, 0:P])
                    e.then_inc(et_done, 1)
                    if idx == 5:
                        prompt_out(b)
                        if not isinstance(b, int):
                            out_read(b - 1)

            def prompt_out(b):
                if not isinstance(b, int):
                    act.wait_ge(sub_done, b)
                act.wait_ge(h_pv, b + 1)
                nc.scalar.activation(sig[1][:, 0:SEQ], H_BANK[:, 0:SEQ], ACT.Square).then_inc(sub_sqd, 1)
                nc.scalar.copy(oT[:, bass.ds(b, 1), 0:SEQ].rearrange("p o n -> p (o n)"), H_BANK[:, 0:SEQ]
                               ).then_inc(h_o, 1)

            def conv_norm(b):
                act.wait_ge(ln_d, b + 1)
                nc.scalar.activation(tmp[0][:, :], gated[:, :], ACT.Square).then_inc(ln_sq, 1)
                act.wait_ge(sub_mm, b + 1)
                nc.scalar.activation(sig[1][:, 0:SEQ], T_BANK[0][:, 0:SEQ], ACT.Sqrt, bias=eps[:, 0:1],
                                     scale=1.0 / P).then_inc(sub_rms, 1)
                act.wait_ge(ln_mm, 2 * b + 2)
                nc.scalar.activation(rms[:, :], H_BANK[:, 0:NTOK], ACT.Sqrt, bias=eps[:, 1:2],
                                     scale=1.0 / P).then_inc(ln_rms, 1)
                act.wait_ge(ln_chain, 3 * b + 3)
                nc.scalar.activation(sig[0][:, :], tmp[1][:, :], ACT.Sigmoid).then_inc(ln_sig, 1)

            def attention(b):
                if not isinstance(b, int):
                    conv_norm(b - 1)
                prompt_head(b)
                exp_scores(b)
                prompt_copy(b)
                copy_ET(b)

            attention(0)
            with act.Fori(1, NB) as b:
                attention(b)
            conv_norm(NB - 1)

            def sample_square(part):
                c0, c1 = S_PARTS[part]
                nc.scalar.activation(s_norm[part][:, :, :], oT[:, :, c0:c1], ACT.Square).then_inc(s_sqd, 1)

            def sample_root(part, out):
                act.wait_ge(s_mm, part + 1)
                n = HEADS * (S_PARTS[part][1] - S_PARTS[part][0])
                nc.scalar.activation(s_norm[part][:, :, :].rearrange("p h n -> p (h n)"), out[:, 0:n], ACT.Sqrt,
                                     bias=eps[:, 0:1], scale=1.0 / P).then_inc(s_rms, 1)

            act.wait_ge(o_done, NB - 1)
            sample_square(0)
            sample_root(0, G_BANK)
            act.wait_ge(v_used, KV_SLOTS * (NB - 1) + 4)
            act.wait_ge(ln_done, NB)
            for k in OUT_ORDER[:HEADS]:
                nc.scalar.copy(x_hi[:, k, :], conv_y[:, k - HEADS, :]).then_inc(x_hi_done, 1)
            out_read(NB - 1)
            act.wait_ge(o_done, NB)
            sample_square(1)
            split_halves(S_OUT, 8)
            sample_root(1, H_BANK)
            act.wait_ge(s_done, 2)
            for hd in range(HEADS):
                nc.scalar.copy(x_hi[:, hd, :], oT[:, hd, :]).then_inc(x_hi_done, 1)
            def out_tile(i, j):
                split_next(S_OUT, i, j)
                act.wait_ge(h_done, KD * 2 + 4 * i + j + 1)
                upper(2, 4 * i + j)
                square(2, 4 * i + j, j % 2)
            act.wait_ge(stored, 16 * 3)
            for n in range(KD):
                out_tile(n // 4, n % 4)
            act.wait_ge(p_in, 16)
            nc.scalar.copy(p_hi[:, :, :], p_raw[:, :, :]).then_inc(p_hi_done, 1)
            ffn(S_FFN2, 44, 3, 0)
            for j in range(2):
                split_next(S_PLE, 0, j)
                if j == 0:
                    squares(3, 3)

            def gates(i, first, last):
                s0 = S_PLE + 2 + 4 * i

                def gate(j):
                    act.wait_ge(evacuated, E(s0 + j))
                    nc.scalar.activation(sig[j % 2][:, :], gated[:, :], ACT.Sigmoid).then_inc(sig_done, 1)
                for j in range(4):
                    n = j + 3
                    if not (last and j == 3):
                        act.wait_ge(raw_in[n % 4], 16 * (S_PLE // 4 + i + n // 4 + 1))
                        act.wait_ge(slab_done, s0 + j)
                        nc.scalar.copy(w_hi[n % 2][:, :, :], raw[n % 4][:, :].rearrange("p (k n) -> p k n", n=P)
                                       ).then_inc(w_hi_done, 1)
                    if first and j == 1:
                        root(3)
                        gate(0)
                    elif not (first and j == 0):
                        square(4, 4 * i + j - 1, (j - 1) % 2)
                    if first and j == 1:
                        square(4, 0, 0)
                    if not (first and j == 0):
                        gate(j)
            gates(0, True, False)
            with act.Fori(1, 3) as i:
                gates(i, False, False)
            for k in range(POOL_TILES):
                nc.scalar.activation(h_g[:, k, :], h[:, k, :], ACT.Copy, scale=vec[:, G_FINAL + k:G_FINAL + k + 1]
                                     ).then_inc(hg_done, 1)
            gates(3, False, True)
            nc.scalar.activation(lam_s[0:1, 6:7], eps[0:1, 0:1], ACT.Sqrt)
            square(4, KD - 1, 1)
            root(4)

        @block.vector
        def _(dve):
            vt = nc.vector

            def split_next(base, i4, j):
                n = j + 1
                dve.wait_ge(w_hi_done, base + 4 * i4 + j + 2)
                split(n)

            def split(n):
                vt.tensor_tensor(w_lo[n % 2][:, :, :], raw[n % 4][:, :].rearrange("p (k n) -> p k n", n=P),
                                 w_hi[n % 2][:, :, :].bitcast(F32), ALU.subtract).then_inc(w_lo_done, 1)

            def split_halves(s, first):
                src = raw[0][:, :].rearrange("p (k n) -> p k n", n=P)
                for done, hi_sem, hi_n, k in ((half_lo, half_hi, 2 if s else 1, first),
                                              (w_lo_done, w_hi_done, s + 1, 8 - first)):
                    dve.wait_ge(hi_sem, hi_n)
                    vt.tensor_tensor(w_lo[0][:, k:k + 8, :], src[:, k:k + 8, :],
                                     w_hi[0][:, k:k + 8, :].bitcast(F32), ALU.subtract).then_inc(done, 1)

            def tile_of(t, n):
                return t[:, bass.ds(n, 1), :].rearrange("p o n -> p (o n)")

            def lower(norm, n):
                hi, lo = X_BUF[norm]
                dve.wait_ge(x_hi_done, X_OF[norm] + n + 1)
                vt.scalar_tensor_tensor(out=tile_of(lo, n), in0=tile_of(h, n),
                                        scalar=vec[:, bass.ds(GAINS[norm] + n, 1)],
                                        in1=tile_of(hi, n).bitcast(F32), op0=ALU.mult, op1=ALU.subtract
                                        ).then_inc(x_done, 1)

            def invert(norm):
                dve.wait_ge(rms_done, norm + 1)
                vt.reciprocal(rinv[:, :], rms[:, :]).then_inc(r_done, 1)
                dve.wait_ge(r_done, norm + 1)

            def ffn_chunk(base, i, f_base, lag=None, norm_in=None, norm=None):
                s0 = base + FFN_SLABS * i

                def evacuate(j):
                    f = j // 2
                    n = f_base + FPC * i + f + 1
                    dve.wait_ge(slab_done, s0 + j + 1)
                    if j % 2 == 0:
                        if not (isinstance(i, int) and i == 0 and f_base == 0 and f == 0):
                            dve.wait_ge(mid_raw, n - 1)
                        vt.tensor_tensor(gated[:, :], bank[j][:, 0:NTOK], rinv[:, :], ALU.mult
                                         ).then_inc(gated_done, 1)
                        dve.wait_ge(gated_done, n + (8 if base else 0))
                        dve.sem_inc(evacuated, 1)
                    else:
                        vt.tensor_tensor(tmp[f % 2][:, :], bank[j][:, 0:NTOK], rinv[:, :], ALU.mult
                                         ).then_inc(evacuated, 1)
                        dve.wait_ge(sig_done, n + (8 if base else 0))
                        vt.tensor_tensor(gated[:, :], gated[:, :], sig[f % 2][:, :], ALU.mult).then_inc(silu_done, 1)
                        dve.wait_ge(evacuated, E(s0 + j))
                        dve.wait_ge(silu_done, n)
                        vt.tensor_tensor(tmp[f % 2][:, :], tmp[f % 2][:, :], gated[:, :], ALU.mult
                                         ).then_inc(mid_raw, 1)
                        dve.wait_ge(mid_raw, n)
                        vt.tensor_copy(mid_hi[:, f, :], tmp[f % 2][:, :]).then_inc(mid_hi_done, 1)
                        dve.wait_ge(mid_hi_done, n)
                        vt.tensor_tensor(mid_lo[:, f, :], tmp[f % 2][:, :], mid_hi[:, f, :].bitcast(F32),
                                         ALU.subtract).then_inc(mid_done, 1)

                for j in range(FFN_SLABS):
                    split_next(base, 3 * i, j)
                    if j < 8:
                        if norm_in is None or j > lag + 1:
                            evacuate(j)
                        elif j == lag + 1:
                            invert(norm_in)
                            for early in range(lag + 2):
                                evacuate(early)
                    else:
                        dve.wait_ge(slab_done, s0 + j + 1)
                        for q in range(4):
                            n = 4 * (j - 8) + q
                            e = vt.scalar_tensor_tensor(out=h[:, n, :], in0=bank[n % 8][:, 0:NTOK], scalar=0.5,
                                                        in1=h[:, n, :], op0=ALU.mult, op1=ALU.add)
                            if norm is not None:
                                e.then_inc(h_done, 1)
                        if norm is None:
                            e.then_inc(evacuated, 1)
                        else:
                            dve.wait_ge(h_done, KD * norm + 4 * (j - 8) + 4)
                            dve.sem_inc(evacuated, 1)
                            for q in range(4):
                                lower(norm, 4 * (j - 8) + q)

            def ffn(base, f_base, norm, lag):
                ffn_chunk(base, 0, f_base, lag=lag, norm_in=norm - 1)
                with dve.Fori(1, CHUNKS - 1) as i:
                    ffn_chunk(base, i, f_base)
                ffn_chunk(base, CHUNKS - 1, f_base, norm=norm)

            for j in range(4):
                for half in range(2):
                    vt.memset(slope_s[32 * j:32 * j + 32, half:half + 1], 2.0 ** -(4 * half + j + 1))
            dve.sem_inc(h_done, KD)
            dve.sem_inc(evacuated, EV0)
            dve.wait_ge(vec_in, 32)
            vt.tensor_tensor(lam_row[0:1, 0:2, :], lam_row[0:1, 0:2, :], lam_row[0:1, 2:4, :], ALU.mult
                             ).then_inc(cchain, 1)
            dve.wait_ge(cchain, 1)
            vt.tensor_reduce(lam_s[0:1, 0:2], lam_row[0:1, 0:2, :], AX.X, ALU.add).then_inc(cchain, 1)
            vt.tensor_scalar(g_sub8[:, :], vec[:, G_SUB:G_SUB + 1], 1.0 - LAM_INIT, None, ALU.mult).then_inc(cchain, 1)
            dve.wait_ge(lam_exp, 1)
            vt.tensor_tensor(lam_s[0:1, 4:5], lam_s[0:1, 3:4], lam_s[0:1, 2:3], ALU.subtract).then_inc(cchain, 1)
            dve.wait_ge(cchain, 4)
            vt.tensor_scalar(lam_s[0:1, 5:6], lam_s[0:1, 4:5], -LAM_INIT, None, ALU.add).then_inc(cchain, 1)
            for n in range(4):
                lower(0, n)
            split_halves(0, 0)
            for n in range(4, KD):
                lower(0, n)
            ffn(S_FFN1, 0, 1, 2)

            def query_tile(i, j):
                dve.wait_ge(slab_done, S_IN + 4 * i + j + 1)
                vt.scalar_tensor_tensor(out=tile_of(qT, 4 * i + j), in0=bank[j][:, 0:NTOK], scalar=QD ** -0.5,
                                        in1=rinv[:, :], op0=ALU.mult, op1=ALU.mult).then_inc(evacuated, 1)
            for i in range(2):
                for j in range(4):
                    split_next(S_IN, i, j)
                    if i == 0 and j == 2:
                        invert(1)
                        query_tile(0, 0)
                        query_tile(0, 1)
                    if i or j >= 2:
                        query_tile(i, j)
            with dve.Fori(0, 2) as i:
                for j in range(4):
                    split_next(S_IN + 8, i, j)
                    dve.wait_ge(slab_done, S_IN + 8 + 4 * i + j + 1)
                    vt.tensor_tensor(tile_of(kT, 4 * i + j), bank[j][:, 0:NTOK], rinv[:, :], ALU.mult
                                     ).then_inc(evacuated, 1)
            with dve.Fori(0, 2) as i:
                for j in range(4):
                    split_next(S_IN + 16, i, j)
                    dve.wait_ge(slab_done, S_IN + 16 + 4 * i + j + 1)
                    vt.tensor_tensor(v_tmp[j][:, :], bank[j][:, 0:NTOK], rinv[:, :], ALU.mult
                                     ).then_inc(evacuated, 1)

            def conv_in(i, last):
                s0 = S_IN + 24 + 4 * i
                for j in range(4):
                    if not (last and j == 3):
                        split_next(S_IN + 24, i, j)
                    if j % 2:
                        c = 2 * i + j // 2
                        dve.wait_ge(slab_done, s0 + j + 1)
                        if not (isinstance(i, int) and i == 0 and j == 1):
                            dve.wait_ge(u_done, c)
                        vt.tensor_tensor(gated[:, :], bank[j][:, 0:NTOK], rinv[:, :], ALU.mult
                                         ).then_inc(gated_done, 1)
                        vt.tensor_tensor(tmp[0][:, :], bank[j - 1][:, 0:NTOK], rinv[:, :], ALU.mult
                                         ).then_inc(evacuated, 2)
                        dve.wait_ge(evacuated, E(s0 + j))
                        dve.wait_ge(sig_done, 44 + c + 1)
                        vt.tensor_tensor(u_p[:, bass.ds(c, 1), HIST:HIST + SEQ].rearrange("p o n -> p (o n)"),
                                         tmp[0][:, 0:SEQ], sig[j // 2][:, 0:SEQ], ALU.mult)
                        vt.tensor_tensor(u_s[:, bass.ds(c, 1), :, HIST:HIST + TS].rearrange("p o s t -> p (o s) t"),
                                         tmp[0][:, SEQ:NTOK].rearrange("p (s t) -> p s t", t=TS),
                                         sig[j // 2][:, SEQ:NTOK].rearrange("p (s t) -> p s t", t=TS), ALU.mult
                                         ).then_inc(u_done, 1)
            dve.wait_ge(state_in, 16)
            dve.wait_ge(small_in, 16 * N_SMALL)
            conv_in(0, False)
            with dve.Fori(1, 3) as i:
                conv_in(i, False)
            conv_in(3, True)

            def tables():
                dve.wait_ge(attc, 4)
                dve.wait_ge(lam_mm, 1)
                vt.tensor_copy(neglam[:, :], bank[7][:, 0:1]).then_inc(cchain, 1)
                vt.tensor_scalar(trow_i[:, :], trow_i[:, :], 7, None, ALU.bitwise_and).then_inc(cchain, 1)
                dve.wait_ge(cchain, 7)
                vt.tensor_copy(trow[:, :], trow_i[:, :]).then_inc(cchain, 1)
                vt.scalar_tensor_tensor(out=comb[:, :, :], in0=comb1[:, :, :], scalar=neglam[:, :], in1=comb[:, :, :],
                                        op0=ALU.mult, op1=ALU.add)
                dve.wait_ge(cchain, 8)
                vt.tensor_scalar(n_mask[:, :], kpos_n[:, :], trow[:, :], None, ALU.is_le).then_inc(cchain, 1)
                dve.wait_ge(cchain, 9)
                vt.tensor_scalar(n_keep[:, :], n_mask[:, :], -MASKED, MASKED, ALU.mult, ALU.add).then_inc(cchain, 1)
                vt.tensor_tensor(n_mask[:, :], n_mask[:, :], kpos_n[:, :], ALU.mult).then_inc(cchain, 1)
                dve.wait_ge(cchain, 11)
                vt.tensor_tensor(kpos_n[:, :], n_mask[:, :], n_keep[:, :], ALU.add).then_inc(cchain, 1)
                dve.wait_ge(cchain, 12)

            def read_scores(b, grp):
                for half in range(2):
                    idx = 2 * grp + half
                    dve.wait_ge(scored, 10 * b + idx + 1)
                    if idx == 0 and not isinstance(b, int):
                        dve.wait_ge(turned, 10 * b)
                    if grp < 4:
                        out, pos = S[:, half, 512 * grp:512 * grp + 512], kpos[:, 512 * grp:512 * grp + 512]
                        src = K_BANK[half][:, :]
                    else:
                        out, pos = S[:, half, PAST:KCOLS], kpos_n[:, bass.ds(56 - TS * b, NB * TS)]
                        src = K_BANK[half][:, 0:NB * TS]
                    vt.scalar_tensor_tensor(out=out, in0=pos, scalar=slope_s[:, half:half + 1], in1=src,
                                            op0=ALU.mult, op1=ALU.add).then_inc(s_read, 1)

            def maxima(b):
                dve.wait_ge(s_read, 10 * b + 10)
                for half in range(2):
                    vt.tensor_reduce(neg_max[:, half:half + 1], S[:, half, :], AX.X, ALU.max, negate=True
                                     ).then_inc(maxed, 1)

            def prompt_head(b):
                dve.wait_ge(h_scored, b + 1)
                slope = slope_p[:, bass.ds(b, 1)]
                for m, src in enumerate((G_BANK, H_BANK)):
                    vt.scalar_tensor_tensor(out=S_p[:, m, :], in0=kpos_p[:, :], scalar=slope, in1=src[:, 0:3 * P],
                                            op0=ALU.mult, op1=ALU.add).then_inc(hs_done, 1)
                dve.wait_ge(hs_done, 2 * b + 2)
                vt.tensor_reduce(head_max[:, 0, :], S_p[:, :, 0:P], AX.X, ALU.max, negate=True).then_inc(h_maxed, 1)
                vt.tensor_reduce(head_max[:, 1, :], S_p[:, :, P:3 * P], AX.X, ALU.max, negate=True).then_inc(h_maxed, 1)

            def prompt_weights(b):
                dve.wait_ge(h_exped, b + 1)
                vt.reciprocal(head_inv[:, :, :], head_sum[:, :, :]).then_inc(h_chain, 1)
                dve.wait_ge(h_chain, 3 * b + 1)
                vt.tensor_scalar(head_c1[:, :], head_inv[:, :, 1], neglam[:, :], None, ALU.mult).then_inc(h_chain, 1)
                dve.wait_ge(h_chain, 3 * b + 2)
                for i, cols in enumerate((slice(0, P), slice(P, 3 * P))):
                    e = vt.tensor_scalar(w_p[:, cols], S_p[:, 1, cols], head_c1[:, i:i + 1], None, ALU.mult)
                e.then_inc(h_chain, 1)
                dve.wait_ge(h_chain, 3 * b + 3)
                for i, cols in enumerate((slice(0, P), slice(P, 3 * P))):
                    e = vt.scalar_tensor_tensor(out=w_p[:, cols], in0=S_p[:, 0, cols], scalar=head_inv[:, i, 0:1],
                                                in1=w_p[:, cols], op0=ALU.mult, op1=ALU.add)
                e.then_inc(h_w, 1)

            def taps(b):
                y = (y_c[:, 0:SEQ], y_odd[:, :])
                if not isinstance(b, int):
                    dve.wait_ge(ln_done, b)

                def w(k):
                    return wdw[:, bass.ds(b, 1), k:k + 1].rearrange("p o n -> p (o n)")

                def u(k):
                    return u_p[:, bass.ds(b, 1), k:k + SEQ].rearrange("p o n -> p (o n)")
                vt.tensor_scalar(y[0], u(0), w(0), w(TAPS), ALU.mult, ALU.add).then_inc(tapped, 1)
                vt.tensor_scalar(y[1], u(1), w(1), None, ALU.mult).then_inc(tapped, 1)
                for k in range(2, TAPS):
                    dve.wait_ge(tapped, TAP_STEPS * b + k - 1)
                    vt.scalar_tensor_tensor(out=y[k % 2], in0=u(k), scalar=w(k), in1=y[k % 2], op0=ALU.mult,
                                            op1=ALU.add).then_inc(tapped, 1)
                dve.wait_ge(tapped, TAP_STEPS * b + TAPS)
                vt.tensor_tensor(y[0], y[0], y[1], ALU.add).then_inc(tapped, 1)

            def inverse_sums(b):
                dve.wait_ge(exped, 2 * b + 2)
                vt.reciprocal(l_inv[:, bass.ds(2 * b, 2)], l_sum[:, bass.ds(2 * b, 2)]).then_inc(l_done, 1)

            def out_store(b):
                dve.wait_ge(comb_mm, b + 1)
                vt.tensor_copy(oT[:, :, bass.ds(SEQ + TS * b, TS)],
                               O_BANK[0][:, 256:320].rearrange("p (h q) -> p h q", q=TS)).then_inc(o_done, 1)

            def conv_center(b):
                dve.wait_ge(ln_mm, 2 * b + 1)
                vt.scalar_tensor_tensor(out=gated[:, :], in0=G_BANK[:, 0:NTOK], scalar=-1.0 / P, in1=y_c[:, :],
                                        op0=ALU.mult, op1=ALU.add).then_inc(ln_d, 1)

            def conv_scale(b):
                g = vec[:, bass.ds(G_CN + b, 1)]
                beta = vec[:, bass.ds(B_CN + b, 1)]
                dve.wait_ge(ln_rms, b + 1)
                vt.reciprocal(rinv[:, :], rms[:, :]).then_inc(ln_chain, 1)
                dve.wait_ge(ln_chain, 3 * b + 1)
                vt.scalar_tensor_tensor(out=gated[:, :], in0=gated[:, :], scalar=g, in1=rinv[:, :],
                                        op0=ALU.mult, op1=ALU.mult).then_inc(ln_chain, 1)
                dve.wait_ge(ln_chain, 3 * b + 2)
                vt.tensor_scalar(tmp[1][:, :], gated[:, :], beta, None, ALU.add).then_inc(ln_chain, 1)

            def conv_swish(b):
                dve.wait_ge(ln_sig, b + 1)
                vt.tensor_tensor(tile_of(conv_y, b), tmp[1][:, :], sig[0][:, :], ALU.mult).then_inc(ln_done, 1)

            def head_scale(b):
                dve.wait_ge(sub_rms, b + 1)
                vt.reciprocal(sig[1][:, 0:SEQ], sig[1][:, 0:SEQ]).then_inc(sub_r, 1)
                o = oT[:, bass.ds(b, 1), 0:SEQ].rearrange("p o n -> p (o n)")
                dve.wait_ge(sub_r, b + 1)
                vt.scalar_tensor_tensor(out=o, in0=o, scalar=g_sub8[:, :], in1=sig[1][:, 0:SEQ],
                                        op0=ALU.mult, op1=ALU.mult).then_inc(sub_done, 1)

            def attention(b):
                first = isinstance(b, int)
                if first:
                    dve.wait_ge(attc, 2)
                read_scores(b, 0)
                if not first:
                    conv_center(b - 1)
                read_scores(b, 1)
                if first:
                    tables()
                else:
                    conv_scale(b - 1)
                read_scores(b, 2)
                if not first:
                    conv_swish(b - 1)
                prompt_head(b)
                read_scores(b, 3)
                read_scores(b, 4)
                maxima(b)
                prompt_weights(b)
                inverse_sums(b)
                if not first:
                    head_scale(b - 1)
                taps(b)
                if not first:
                    out_store(b - 1)

            dve.wait_ge(u_done, 8)
            attention(0)
            with dve.Fori(1, NB) as b:
                attention(b)
            conv_center(NB - 1)
            conv_scale(NB - 1)
            conv_swish(NB - 1)
            head_scale(NB - 1)

            def sample_scale(part):
                c0, c1 = S_PARTS[part]
                dve.wait_ge(s_rms, part + 1)
                vt.reciprocal(s_norm[part][:, :, :], s_norm[part][:, :, :]).then_inc(s_r, 1)
                dve.wait_ge(s_r, part + 1)
                vt.scalar_tensor_tensor(out=oT[:, :, c0:c1], in0=oT[:, :, c0:c1], scalar=g_sub8[:, :],
                                        in1=s_norm[part][:, :, :], op0=ALU.mult, op1=ALU.mult).then_inc(s_done, 1)

            sample_scale(0)
            for n, k in enumerate(OUT_ORDER[:HEADS]):
                if k == 8:
                    out_store(NB - 1)
                dve.wait_ge(x_hi_done, X_OUT + n + 1)
                vt.tensor_tensor(x_lo[:, k, :], conv_y[:, k - HEADS, :], x_hi[:, k, :].bitcast(F32), ALU.subtract
                                 ).then_inc(x_done, 1)
            split_halves(S_OUT, 8)
            sample_scale(1)
            for hd in range(HEADS):
                dve.wait_ge(x_hi_done, X_OUT + HEADS + hd + 1)
                vt.tensor_tensor(x_lo[:, hd, :], oT[:, hd, :], x_hi[:, hd, :].bitcast(F32), ALU.subtract
                                 ).then_inc(x_done, 1)
            def out_tile(i, j):
                n = 4 * i + j
                split_next(S_OUT, i, j)
                dve.wait_ge(slab_done, S_OUT + n + 1)
                vt.scalar_tensor_tensor(out=tile_of(h, n), in0=bank[j][:, 0:NTOK], scalar=1.0, in1=tile_of(h, n),
                                        op0=ALU.mult, op1=ALU.add).then_inc(h_done, 1)
                dve.wait_ge(h_done, KD * 2 + n + 1)
                dve.sem_inc(evacuated, 1)
                lower(2, n)
            dve.wait_ge(stored, 16 * 3)
            with dve.Fori(0, 2) as i:
                for j in range(4):
                    out_tile(i, j)
            dve.wait_ge(conv_stored, 16 * 2)
            with dve.Fori(2, 4) as i:
                for j in range(4):
                    out_tile(i, j)
            dve.wait_ge(p_hi_done, 1)
            vt.tensor_tensor(p_lo[:, :, :], p_raw[:, :, :], p_hi[:, :, :].bitcast(F32), ALU.subtract
                             ).then_inc(p_done, 1)
            ffn(S_FFN2, 44, 3, 0)
            for t in range(2):
                split_next(S_PLE, 0, t)
                for q in range(8):
                    if q < 7:
                        dve.wait_ge(proj_mm, 7 * t + q + 1)
                    else:
                        dve.wait_ge(slab_done, S_PLE + t + 1)
                    vt.tensor_copy(proj[:, 8 * t + q, :], bank[q][:, 0:NTOK]).then_inc(proj_read, 1)
                dve.wait_ge(proj_read, 8 * t + 8)
                dve.sem_inc(evacuated, 1)

            def gates(i, first, last):
                s0 = S_PLE + 2 + 4 * i

                def gate(j):
                    n = 4 * i + j
                    dve.wait_ge(slab_done, s0 + j + 1)
                    vt.tensor_tensor(gated[:, :], bank[j][:, 0:NTOK], rinv[:, :], ALU.mult).then_inc(evacuated, 1)
                    dve.wait_ge(sig_done, 44 + 8 + 44 + n + 1)
                    vt.tensor_tensor(sig[j % 2][:, :], tile_of(proj, n), sig[j % 2][:, :], ALU.mult
                                     ).then_inc(silu_done, 1)
                    dve.wait_ge(silu_done, 88 + n + 1)
                    vt.tensor_tensor(tile_of(h, n), tile_of(h, n), sig[j % 2][:, :], ALU.add).then_inc(h_done, 1)
                for j in range(4):
                    if not (last and j == 3):
                        dve.wait_ge(w_hi_done, s0 + j + 2)
                        split(j + 3)
                    if first and j == 1:
                        invert(3)
                        gate(0)
                    if not (first and j == 0):
                        gate(j)
            gates(0, True, False)
            with dve.Fori(1, 3) as i:
                gates(i, False, False)
            gates(3, False, True)
            dve.wait_ge(rms_done, 5)
            vt.reciprocal(rinv[:, :], rms[:, :]).then_inc(r_done, 1)
            dve.wait_ge(r_done, 5)
            for k in range(POOL_TILES, KD):
                vt.scalar_tensor_tensor(out=proj[:, k, :], in0=h[:, k, :], scalar=vec[:, G_FINAL + k:G_FINAL + k + 1],
                                        in1=rinv[:, :], op0=ALU.mult, op1=ALU.mult).then_inc(y_done, 1)

        @block.tensor
        def _(pe):
            mm = nc.tensor.matmul

            def three(out, w2, t, xh, xl, start, stop):
                mm(out, w_hi[w2][:, t, :], xh, start=start, stop=False)
                mm(out, w_hi[w2][:, t, :], xl, start=False, stop=False)
                return mm(out, w_lo[w2][:, t, :], xh, start=False, stop=stop)

            def dense(s, j, b, order=range(KD), x_base=None, x=(x_hi, x_lo), half=None):
                pe.wait_ge(half_lo, half) if half else pe.wait_ge(w_lo_done, s + 1)
                for n, k in enumerate(order):
                    if half and n == 8:
                        pe.wait_ge(w_lo_done, s + 1)
                    if x_base is not None:
                        pe.wait_ge(x_done, x_base + n + 1)
                    e = three(bank[b][:, 0:NTOK], j % 2, k, x[0][:, k, :], x[1][:, k, :],
                              n == 0, n == len(order) - 1)
                e.then_inc(slab_done, 1)

            def sum_features(norm):
                pe.wait_ge(ssq_done, KD * norm + KD)
                mm(NORM[:, 0:NTOK], ones[:, :], ssq[:, :], start=True, stop=True).then_inc(norm_mm, 1)

            def ffn_chunk(base, i, f_base, norm, lag):
                s0 = base + FFN_SLABS * i
                first = isinstance(i, int)
                for j in range(8):
                    if not first:
                        pe.wait_ge(evacuated, E(s0 - 2) if j < 4 else E(s0 - 1))
                    elif base != S_FFN1 and j < 4:
                        pe.wait_ge(evacuated, E(s0 - 4 + j))
                    if first and j == 7:
                        pe.wait_ge(rms_done, norm + 1)
                    dense(s0 + j, j, j, x_base=X_OF[norm] if first and j == 0 else None, x=X_BUF[norm],
                          half=1 if first and s0 + j == 0 else None)
                    if first and j == lag:
                        sum_features(norm)
                for d in range(4):
                    pe.wait_ge(w_lo_done, s0 + 8 + d + 1)
                    pe.wait_ge(evacuated, E(s0 + (3, 7, 8, 9)[d]))
                    for f in range(FPC):
                        if d == 0:
                            pe.wait_ge(mid_done, f_base + FPC * i + f + 1)
                        for q in range(4):
                            e = three(bank[(4 * d + q) % 8][:, 0:NTOK], d % 2, 4 * f + q,
                                      mid_hi[:, f, :], mid_lo[:, f, :], f == 0, f == FPC - 1)
                    e.then_inc(slab_done, 1)

            def ffn(base, f_base, norm, lag):
                ffn_chunk(base, 0, f_base, norm, lag)
                with pe.Fori(1, CHUNKS) as i:
                    ffn_chunk(base, i, f_base, norm, lag)

            pe.wait_ge(consts, 1)
            ffn(S_FFN1, 0, 0, 2)

            for j in range(4):
                pe.wait_ge(evacuated, E(S_IN - 2))
                dense(S_IN + j, j, j, x_base=X_IN if j == 0 else None)
                if j == 1:
                    pe.wait_ge(evacuated, E(S_IN - 1))
                    sum_features(1)
            with pe.Fori(1, 4) as i:
                for j in range(4):
                    pe.wait_ge(evacuated, E(S_IN + 4 * i + j - 4))
                    dense(S_IN + 4 * i + j, j, j)
            pe.wait_ge(consts, 2)
            for i in range(2):
                for j in range(4):
                    pe.wait_ge(evacuated, E(S_IN + 16 + 4 * i + j - 4))
                    dense(S_IN + 16 + 4 * i + j, j, j)
                for j in range(4):
                    pe.wait_ge(evacuated, E(S_IN + 16 + 4 * i + j))
                    if i:
                        pe.wait_ge(vtok_done, 4)
                    for a, t0 in enumerate((0, P, NTOK - P)):
                        e = nc.tensor.transpose(bank[4 + j][:, P * a:P * a + P], v_tmp[j][:, t0:t0 + P], ident[:, :])
                    e.then_inc(v_turned, 1)
            with pe.Fori(0, 4) as i:
                for j in range(4):
                    pe.wait_ge(evacuated, E(S_IN + 24 + 4 * i + (j - 4 if j % 2 else j - 3)))
                    dense(S_IN + 24 + 4 * i + j, j, j)
            pe.wait_ge(vtok_done, HEADS)
            pe.wait_ge(cchain, 5)
            mm(bank[7][:, 0:1], ones[0:1, :], lam_s[0:1, 5:6], start=True, stop=True).then_inc(lam_mm, 1)

            def keys(slot):
                return raw[slot][:, :].rearrange("p (g h k) -> p g h k", g=2, h=HEADS)

            def score(b, grp):
                for half in range(2):
                    idx = 2 * grp + half
                    if not (isinstance(b, int) and idx < 2):
                        pe.wait_ge(s_read, 10 * b + idx - 1)
                    for e2 in range(2):
                        slot = (2 * grp + e2) % RAW
                        if half == 0:
                            pe.wait_ge(kv_in[slot], 32 * kv_round(b, 2 * grp + e2))
                        for j in range(4):
                            e = mm(K_BANK[half][32 * j:32 * j + 32, 256 * e2:256 * e2 + 256],
                                   Qb[:, 4 * half + j, :], keys(slot)[:, :, 4 * half + j, :], start=True, stop=True)
                    e.then_inc(scored, 1)

            def kv_round(b, g):
                return g // 4 + 1 if isinstance(b, int) else 4 * b - 2 + g // 4 + 1

            def score_new(b):
                for half in range(2):
                    pe.wait_ge(s_read, 10 * b + 8 + half - 1)
                    for j in range(4):
                        e = mm(K_BANK[half][32 * j:32 * j + 32, 0:NB * TS], Qb[:, 4 * half + j, :],
                               kT[:, 4 * half + j, SEQ:NTOK], start=True, stop=True)
                    e.then_inc(scored, 1)

            def prompt_scores(b):
                pe.wait_ge(staged, b + 1)
                if isinstance(b, int):
                    pe.wait_ge(cchain, 12)
                else:
                    pe.wait_ge(ln_d, b)
                    pe.wait_ge(ln_rms, b)
                for m, out in enumerate((G_BANK, H_BANK)):
                    rows = slice(QD * m, QD * m + QD)
                    for cols, keys_n, qs in ((0, P, 0), (P, 2 * P, P)):
                        e = mm(out[:, cols:cols + keys_n], q_st[rows, qs:qs + P],
                               k_st[rows, 0:keys_n], start=True, stop=True)
                e.then_inc(h_scored, 1)

            def prompt_turn(b):
                pe.wait_ge(h_w, b + 1)
                for c in range(3):
                    e = nc.tensor.transpose(G_BANK[:, P * c:P * c + P], w_p[:, P * c:P * c + P], ident[:, :])
                e.then_inc(h_turned, 1)

            def prompt_pv(b):
                pe.wait_ge(h_wT, b + 1)
                mm(H_BANK[:, 0:P], v_st[:, 0, :], wT_p[:, 0:P], start=True, stop=True)
                mm(H_BANK[:, P:2 * P], v_st[:, 0, :], wT_p[:, P:2 * P], start=True, stop=False)
                mm(H_BANK[:, P:2 * P], v_st[:, 1, :], wT_p[:, 2 * P:3 * P], start=False, stop=True).then_inc(h_pv, 1)

            def turn(b, group):
                if group == 0:
                    pe.wait_ge(exped, 2 * b + 2)
                    if not isinstance(b, int):
                        pe.wait_ge(sub_rms, b)
                for idx in (2 * group, 2 * group + 1):
                    half, g = idx % 2, idx // 2
                    if not (isinstance(b, int) and idx < 2):
                        pe.wait_ge(et_done, 10 * b + idx - 1)
                    if g < 4:
                        for c in range(4):
                            e = nc.tensor.transpose(T_BANK[idx % 2][:, P * c:P * c + P],
                                                    S[:, half, 512 * g + P * c:512 * g + P * c + P], ident[:, :])
                    else:
                        e = nc.tensor.transpose(T_BANK[idx % 2][:, 0:P], S[:, half, KCOLS - P:KCOLS], ident[:, :])
                    e.then_inc(turned, 1)

            def weigh(b, pair):
                if pair == 0:
                    pe.wait_ge(et_done, 10 * b + 10)
                for g in (2 * pair, 2 * pair + 1):
                    slot = g % RAW
                    pe.wait_ge(kv_in[slot], 32 * (4 * b + 4 + g // 4 + 1) if not (isinstance(b, int) and b == NB - 1)
                               else 32 * (2 * KV_SLOTS * NB // RAW - 2 + g // 4 + 1))
                    for half in range(2):
                        for e2 in range(2):
                            for j in range(4):
                                e = mm(O_BANK[half][32 * j:32 * j + 32, 0:P],
                                       ET[:, half, 2 * g + e2, 32 * j:32 * j + 32],
                                       keys(slot)[:, e2, 4 * half + j, :], start=(g == 0 and e2 == 0), stop=False)
                    e.then_inc(v_used, 1)

            def weigh_new(b):
                for half in range(2):
                    for j in range(4):
                        e = mm(O_BANK[half][32 * j:32 * j + 32, 0:P],
                               ET[P - NB * TS:P, half, PAGES, 32 * j:32 * j + 32],
                               vtok[P - NB * TS:P, 2, P * (4 * half + j):P * (4 * half + j) + P],
                               start=False, stop=True)
                e.then_inc(pv_done, 1)

            def combine(b):
                pe.wait_ge(o_read, 2 * b + 2)
                for half in range(2):
                    e = mm(O_BANK[0][:, 256 + 32 * half:288 + 32 * half], O_n[:, half, :],
                           comb[:, :, :].rearrange("p j q -> p (j q)"), start=True, stop=True)
                e.then_inc(comb_mm, 1)

            def conv_mean(b):
                pe.wait_ge(tapped, TAP_STEPS * b + TAP_STEPS)
                pe.wait_ge(s_tapped, TAPS * b + TAPS)
                pe.wait_ge(h_wT, b + 1)
                mm(G_BANK[:, 0:NTOK], ones[:, :], y_c[:, :], start=True, stop=True).then_inc(ln_mm, 1)

            def conv_var(b):
                pe.wait_ge(ln_sq, b + 1)
                pe.wait_ge(h_o, b + 1)
                mm(H_BANK[:, 0:NTOK], ones[:, :], tmp[0][:, :], start=True, stop=True).then_inc(ln_mm, 1)

            def head_sum(b):
                pe.wait_ge(et_done, 10 * b + 10)
                pe.wait_ge(sub_sqd, b + 1)
                mm(T_BANK[0][:, 0:SEQ], ones[:, :], sig[1][:, 0:SEQ], start=True, stop=True).then_inc(sub_mm, 1)

            def sample_sum(part, out):
                pe.wait_ge(s_sqd, part + 1)
                sq = s_norm[part][:, :, :].rearrange("p h n -> p (h n)")
                mm(out[:, 0:HEADS * (S_PARTS[part][1] - S_PARTS[part][0])], ones[:, :], sq, start=True, stop=True
                   ).then_inc(s_mm, 1)

            def attention(b):
                pe.wait_ge(qb_ready, 2 * b + 2)
                first = isinstance(b, int)
                if first:
                    pe.wait_ge(evacuated, E(S_OUT - 1))
                score(b, 0)
                if not first:
                    head_sum(b - 1)
                    conv_mean(b - 1)
                score(b, 1)
                if not first:
                    conv_var(b - 1)
                score(b, 2)
                prompt_scores(b)
                score(b, 3)
                score_new(b)
                if not first:
                    weigh(b - 1, 0)
                    weigh(b - 1, 1)
                prompt_turn(b)
                turn(b, 0)
                turn(b, 1)
                if not first:
                    weigh(b - 1, 2)
                prompt_pv(b)
                turn(b, 2)
                if not first:
                    weigh(b - 1, 3)
                    weigh_new(b - 1)
                turn(b, 3)
                turn(b, 4)
                if not first:
                    combine(b - 1)

            attention(0)
            with pe.Fori(1, NB) as b:
                attention(b)
            head_sum(NB - 1)
            conv_mean(NB - 1)
            conv_var(NB - 1)
            weigh(NB - 1, 0)
            pe.wait_ge(ln_d, NB)
            sample_sum(0, G_BANK)
            for pair in range(1, 4):
                weigh(NB - 1, pair)
            weigh_new(NB - 1)
            combine(NB - 1)
            pe.wait_ge(ln_rms, NB)
            sample_sum(1, H_BANK)

            for j in range(4):
                dense(S_OUT + j, j, j, order=OUT_ORDER, x_base=X_OUT if j == 0 else None,
                      half=2 if j == 0 else None)
            with pe.Fori(1, 4) as i:
                for j in range(4):
                    pe.wait_ge(evacuated, E(S_OUT + 4 * i + j - 4))
                    dense(S_OUT + 4 * i + j, j, j, order=OUT_ORDER)
            ffn(S_FFN2, 44, 2, 0)
            pe.wait_ge(p_done, 1)
            for t in range(2):
                pe.wait_ge(w_lo_done, S_PLE + t + 1)
                for q in range(8):
                    if t:
                        pe.wait_ge(proj_read, q + 1)
                    elif q % 4 == 0:
                        pe.wait_ge(evacuated, E(S_PLE - 2 + q // 4))
                    for k in range(PLE_K):
                        e = three(bank[q][:, 0:NTOK], t % 2, PLE_K * q + k, p_hi[:, k, :], p_lo[:, k, :],
                                  k == 0, k == PLE_K - 1)
                    if q < 7:
                        e.then_inc(proj_mm, 1)
                e.then_inc(slab_done, 1)
            for j in range(4):
                pe.wait_ge(proj_read, 8 + j + 1)
                dense(S_PLE + 2 + j, j, j, x_base=X_PLE if j == 0 else None)
                if j == 0:
                    pe.wait_ge(proj_read, 16)
                    sum_features(3)
            with pe.Fori(1, 4) as i:
                for j in range(4):
                    s = S_PLE + 2 + 4 * i + j
                    pe.wait_ge(evacuated, E(s - 4))
                    dense(s, j, j)
            pe.wait_ge(ssq_done, KD * 4 + KD - 1)
            mm(NORM[:, 0:NTOK], ones[:, :], ssq[:, :], start=True, stop=False)
            pe.wait_ge(sq_done, KD * 4 + KD)
            mm(NORM[:, 0:NTOK], ones[:, :], tmp[1][:, :], start=False, stop=True).then_inc(norm_mm, 1)


def blocks(w, rows, cols):
    return w.reshape(rows, P, cols, P).transpose(0, 2, 1, 3)


def as_slab(b):
    return np.ascontiguousarray(np.moveaxis(b, -3, -2)).reshape(*b.shape[:-3], P, SLAB * P)


def ffn_slabs(w_gate, w_up, w_down):
    nf = DFF // P
    out = np.empty((CHUNKS, FFN_SLABS, P, SLAB * P), np.float32)
    for which, w in enumerate((w_gate, w_up)):
        b = as_slab(blocks(w, KD, nf).transpose(1, 0, 2, 3))
        out[:, which:8:2] = b.reshape(CHUNKS, FPC, P, SLAB * P)
    d = blocks(w_down, nf, KD).reshape(CHUNKS, FPC, 4, 4, P, P)
    out[:, 8:] = as_slab(d.transpose(0, 2, 1, 3, 4, 5).reshape(CHUNKS, 4, SLAB, P, P))
    return out.reshape(N_FFN, P, SLAB * P)


def per_tile(v):
    return v.reshape(-1, P).T


def kernel(**inp):
    from concourse import bacc
    from concourse.bass_utils import run_bass_kernel_spmd

    a = {k: np.asarray(v) for k, v in inp.items()}
    ns = NB * TS

    def feature_major(prompt, sample, tiles):
        t = np.concatenate([prompt.reshape(SEQ, -1), sample.reshape(ns, -1)], 0)
        return np.ascontiguousarray(t.T.reshape(tiles, P, NTOK).transpose(1, 0, 2))

    w_in = as_slab(blocks(a["w_in"][0], KD, N_IN).transpose(1, 0, 2, 3))
    conv_order = [24 + 8 * (j % 2) + j // 2 for j in range(16)]
    w_in = np.ascontiguousarray(w_in[list(range(24)) + conv_order])
    w_out = as_slab(blocks(a["w_out"][0], KD, KD).transpose(1, 0, 2, 3))
    gate = as_slab(blocks(a["w_ple_gate"][0], KD, KD).transpose(1, 0, 2, 3))
    proj = as_slab(blocks(a["w_ple_proj"][0], PLE_K, KD).reshape(PLE_K, 2, 8, P, P).transpose(1, 2, 0, 3, 4)
                   .reshape(2, SLAB, P, P))
    k_pool = np.ascontiguousarray(a["cache_k"][0].transpose(0, 3, 2, 1)).reshape(NPOOL, P, HEADS * PAGE)
    v_pool = np.ascontiguousarray(a["cache_v"][0]).reshape(NPOOL, PAGE, HEADS * P)
    state = np.zeros((P, 8, NB, HIST + TS), np.float32)
    state[:, :, :, :HIST] = a["state_conv"][0].reshape(NB, HIST, 8, P).transpose(3, 2, 0, 1)
    vecs = np.concatenate([per_tile(a[n].reshape(-1)) for n in
                           ("g_ffn1", "g_mix", "g_ffn2", "g_ple", "g_final", "g_conv_norm", "b_conv_norm",
                            "g_subln")], 1)
    dw = np.concatenate([a["w_dw"][0].reshape(TAPS, 8, P).transpose(2, 1, 0),
                         a["b_dw"][0].reshape(8, P).T[:, :, None]], 2)
    lams = np.concatenate([a[n].reshape(1, 1, QD) for n in ("lambda_q1", "lambda_q2", "lambda_k1", "lambda_k2")], 1)
    arrays = {
        "x_t": feature_major(a["x_prompt"], a["x_sample"], KD),
        "slabs_ffn1": ffn_slabs(a["w_ffn1_gate"][0], a["w_ffn1_up"][0], a["w_ffn1_down"][0]),
        "slabs_in": w_in, "slabs_out": w_out,
        "slabs_ffn2": ffn_slabs(a["w_ffn2_gate"][0], a["w_ffn2_up"][0], a["w_ffn2_down"][0]),
        "slabs_ple": np.concatenate([proj, gate], 0),
        "k_pool": k_pool, "v_pool": v_pool,
        "pages": a["page_table"].reshape(1, -1),
        "state_ext": state,
        "p_t": feature_major(a["p_prompt"], a["p_sample"], PLE_K),
        "vecs": vecs, "dw": dw, "lams": lams,
    }
    arrays = {k: np.ascontiguousarray(v) for k, v in arrays.items()}
    outs = {"y_t": (P, KD, NTOK), "k_t": (P, HEADS, NTOK), "v_tok": (NTOK, HEADS * P),
            "conv_p": (P, 8, HIST), "conv_s": (P, 8, NB, HIST + TS)}

    nc = bacc.Bacc("TRN2", target_bir_lowering=False, num_devices=1)
    args = {k: nc.dram_tensor(k, v.shape, mybir.dt.from_np(v.dtype), kind="ExternalInput").ap()
            for k, v in arrays.items()}
    args |= {k: nc.dram_tensor(k, s, F32, kind="ExternalOutput").ap() for k, s in outs.items()}
    hymba_step(nc, **args)
    res = run_bass_kernel_spmd(nc, [arrays], core_ids=[0]).results[0]

    y = res["y_t"].transpose(2, 1, 0).reshape(NTOK, D)
    k = res["k_t"].transpose(2, 1, 0).reshape(NTOK, HEADS, P)
    v = res["v_tok"].reshape(NTOK, HEADS, P)
    conv_p = res["conv_p"].transpose(2, 1, 0).reshape(1, 1, HIST, 8 * P)
    conv_s = res["conv_s"][:, :, :, TS:].transpose(2, 3, 1, 0).reshape(1, NB, HIST, 8 * P)
    out = (y[:SEQ].reshape(1, SEQ, D), y[SEQ:].reshape(NB, TS, D),
           k[:SEQ].reshape(1, 1, SEQ, HEADS, P), v[:SEQ].reshape(1, 1, SEQ, HEADS, P), conv_p,
           k[SEQ:].reshape(1, NB, TS, HEADS, P), v[SEQ:].reshape(1, NB, TS, HEADS, P), conv_s)
    return tuple(np.ascontiguousarray(o) for o in out)
```
